# Optimizing a Trainium2 kernel written in Bass

```python
import math
import jax
import jax.numpy as jnp
from jax import lax
import numpy as np
import jax, jax.numpy as jnp

D_MODEL = 1024
BATCH = 1
SEQ = 1024
DEPTH = 2

GRID_W = 64
CTX_LEN = 256
HEAD_DIM = 64
BRANCH_W = D_MODEL // 2
MIX_W = 2 * BRANCH_W
NA_HEADS = BRANCH_W // HEAD_DIM
NA_WIN_ROWS = 8
NA_WIN_COLS = 16
GQA_HEADS = BRANCH_W // HEAD_DIM
GQA_KV_HEADS = 2
GQA_GROUP = GQA_HEADS // GQA_KV_HEADS
GQA_KV_W = GQA_KV_HEADS * HEAD_DIM
ROPE_THETA = 10000.0
ROPE_FREQS = HEAD_DIM // 4
Q_BLOCK = 128
RWKV_HEADS = BRANCH_W // HEAD_DIM
DECAY_LORA = 32
ICLR_LORA = 32
HY_WIDTH = BRANCH_W
HY_ORDER = 2
HY_POS_BANDS = 16
HY_POS_DIM = 1 + 2 * HY_POS_BANDS
HY_FILTER_HIDDEN = 64
HY_DECAY_TARGET = 1e-2
HY_FAST_DECAY_PCT = 0.3
HY_SLOW_DECAY_PCT = 1.5
NORM_EPS = 1e-6
RWKV_GN_EPS = 64e-5
N_ATTN_LAYERS = (DEPTH + 1) // 2
N_REC_LAYERS = DEPTH // 2
ATTN_SPLITS = (BRANCH_W, BRANCH_W, BRANCH_W, BRANCH_W, BRANCH_W, GQA_KV_W, GQA_KV_W, BRANCH_W)
ATTN_IN = 6 * BRANCH_W + 2 * GQA_KV_W
RWKV_SPLITS = (BRANCH_W, BRANCH_W, BRANCH_W, DECAY_LORA, DECAY_LORA, ICLR_LORA, ICLR_LORA)
RWKV_SHIFT_W = 3 * BRANCH_W + 2 * DECAY_LORA + 2 * ICLR_LORA
HY_IN_W = (HY_ORDER + 1) * HY_WIDTH
REC_SPLITS = (RWKV_SHIFT_W, BRANCH_W, HY_IN_W, HY_WIDTH)
REC_IN = RWKV_SHIFT_W + BRANCH_W + HY_IN_W + HY_WIDTH


def split_cols(u, sizes):
    parts, start = [], 0
    for s in sizes:
        parts.append(u[..., start:start + s])
        start += s
    return parts

def to_heads(t, n_heads):
    return t.reshape(t.shape[:-1] + (n_heads, HEAD_DIM))

def rms_norm(x, gain):
    xf = x.astype(jnp.float32)
    y = xf * lax.rsqrt(jnp.mean(xf * xf, axis=-1, keepdims=True) + NORM_EPS)
    return (y * gain.astype(jnp.float32)).astype(x.dtype)

def adaln(cond, ada_w, ada_b):
    m = jax.nn.silu(cond) @ ada_w + ada_b
    return jnp.split(m, 3, axis=-1)

def modulate(x, gain, shift, scale):
    return rms_norm(x, gain) * (1 + scale) + shift

def centred_pad(u):
    return jnp.pad(u, ((0, 0), (1, 1), (0, 0)))

def centred_conv3(u, taps):
    up = centred_pad(u)
    return up[:, :-2] * taps[0] + up[:, 1:-1] * taps[1] + up[:, 2:] * taps[2]

def centred_token_shift(u, mu):
    up = centred_pad(u)
    return u + (0.5 * (up[:, :-2] + up[:, 2:]) - u) * mu

def axial_rope_tables(n):
    t = jnp.arange(n, dtype=jnp.int32)
    pos = jnp.stack([t // GRID_W, t % GRID_W], axis=-1).astype(jnp.float32)
    inv_freq = ROPE_THETA ** (-jnp.arange(ROPE_FREQS, dtype=jnp.float32) / ROPE_FREQS)
    ang = pos[:, :, None] * inv_freq
    return jnp.cos(ang), jnp.sin(ang)

def apply_axial_rope(x, cos, sin):
    xs = x.astype(jnp.float32).reshape(x.shape[:-1] + (2, 2, ROPE_FREQS))
    x1, x2 = xs[..., 0, :], xs[..., 1, :]
    c, s = cos[None, :, None], sin[None, :, None]
    y = jnp.stack([x1 * c - x2 * s, x2 * c + x1 * s], axis=-2)
    return y.reshape(x.shape).astype(x.dtype)

def softmax_f32(s):
    return jax.nn.softmax(s.astype(jnp.float32), axis=-1)

def dense_gqa(q, k, v):
    s = jnp.einsum('bqhgd,bkhd->bhgqk', q, k) * (q.shape[-1] ** -0.5)
    p = softmax_f32(s).astype(v.dtype)
    return jnp.einsum('bhgqk,bkhd->bqhgd', p, v)

def blockwise_gqa(q, k, v, k_ctx, v_ctx):
    b, n, hk, g, dh = q.shape
    scale = dh ** -0.5

    def block(q_blk):
        s = jnp.concatenate([jnp.einsum('bqhgd,bkhd->bhgqk', q_blk, k),
                             jnp.einsum('bqhgd,bkhd->bhgqk', q_blk, k_ctx)], axis=-1) * scale
        p = softmax_f32(s).astype(v.dtype)
        return (jnp.einsum('bhgqk,bkhd->bqhgd', p[..., :n], v)
                + jnp.einsum('bhgqk,bkhd->bqhgd', p[..., n:], v_ctx))

    q_blocks = jnp.moveaxis(q.reshape(b, n // Q_BLOCK, Q_BLOCK, hk, g, dh), 1, 0)
    out = lax.map(block, q_blocks)
    return jnp.moveaxis(out, 0, 1).reshape(b, n, hk, g, dh)

def neighbourhood_layout(n, rows):
    kh, kw = min(NA_WIN_ROWS, rows), NA_WIN_COLS
    t = jnp.arange(n, dtype=jnp.int32)
    q_row, q_col = t // GRID_W, t % GRID_W
    row0 = jnp.clip(q_row - kh // 2, 0, rows - kh)
    col0 = jnp.clip(q_col - kw // 2, 0, GRID_W - kw)
    k_row = row0[:, None, None] + jnp.arange(kh, dtype=jnp.int32)[None, :, None]
    k_col = col0[:, None, None] + jnp.arange(kw, dtype=jnp.int32)[None, None, :]
    shape = (n, kh, kw)
    idx = jnp.broadcast_to(k_row * GRID_W + k_col, shape).reshape(n, kh * kw)
    rel_r = jnp.broadcast_to(k_row - q_row[:, None, None] + NA_WIN_ROWS - 1, shape).reshape(n, kh * kw)
    rel_c = jnp.broadcast_to(k_col - q_col[:, None, None] + NA_WIN_COLS - 1, shape).reshape(n, kh * kw)
    return idx, rel_r, rel_c

def neighbourhood_attention(q, k, v, k_ctx, v_ctx, rpb, rows):
    b, n, h, dh = q.shape
    idx, rel_r, rel_c = neighbourhood_layout(n, rows)
    n_win = idx.shape[-1]
    nblk = n // Q_BLOCK
    scale = dh ** -0.5

    def block(args):
        q_blk, idx_blk, rr_blk, rc_blk = args
        k_win = jnp.take(k, idx_blk, axis=1)
        v_win = jnp.take(v, idx_blk, axis=1)
        s_win = jnp.einsum('bqhd,bqkhd->bhqk', q_blk, k_win) * scale + rpb[:, rr_blk, rc_blk][None]
        s_ctx = jnp.einsum('bqhd,bkhd->bhqk', q_blk, k_ctx) * scale
        p = softmax_f32(jnp.concatenate([s_win, s_ctx], axis=-1)).astype(v.dtype)
        return (jnp.einsum('bhqk,bqkhd->bqhd', p[..., :n_win], v_win)
                + jnp.einsum('bhqk,bkhd->bqhd', p[..., n_win:], v_ctx))

    xs = (jnp.moveaxis(q.reshape(b, nblk, Q_BLOCK, h, dh), 1, 0),
          idx.reshape(nblk, Q_BLOCK, n_win),
          rel_r.reshape(nblk, Q_BLOCK, n_win),
          rel_c.reshape(nblk, Q_BLOCK, n_win))
    out = lax.map(block, xs)
    return jnp.moveaxis(out, 0, 1).reshape(b, n, h, dh)

def rwkv_features(u, w0, w_up, a0, a_up, k_k, k_a):
    r, k, v, dw_f, dw_b, da_f, da_b = split_cols(u, RWKV_SPLITS)
    kk = to_heads(k * k_k, RWKV_HEADS).astype(jnp.float32)
    kk = kk * lax.rsqrt(jnp.sum(kk * kk, axis=-1, keepdims=True) + 1e-12)
    dirs = []
    for d, (dw, da) in enumerate(((dw_f, da_f), (dw_b, da_b))):
        w_log = -jax.nn.softplus(-(w0[d] + jnp.tanh(dw) @ w_up[d])) - 0.5
        decay = jnp.exp(-jnp.exp(w_log.astype(jnp.float32)))
        a = jax.nn.sigmoid(a0[d] + da @ a_up[d])
        k_d = k * (1 + (a - 1) * k_a)
        dirs.append((to_heads(decay, RWKV_HEADS), to_heads(k_d, RWKV_HEADS), kk * to_heads(a, RWKV_HEADS)))
    return to_heads(r, RWKV_HEADS), to_heads(v, RWKV_HEADS), kk, dirs

def wkv_scan(s0, r, decay, k, v, kk, b, reverse, emit):
    xs = tuple(jnp.moveaxis(t, 1, 0) for t in (r, decay, k, v, kk, b))

    def step(s, inp):
        r_t, w_t, k_t, v_t, kk_t, b_t = inp
        sa = jnp.einsum('bhij,bhj->bhi', s, kk_t)
        s = s * w_t[:, :, None, :] - sa[..., None] * b_t[:, :, None, :] + v_t[..., None] * k_t[:, :, None, :]
        y = jnp.einsum('bhij,bhj->bhi', s, r_t) if emit else None
        return s, y

    s_final, ys = lax.scan(step, s0, xs, reverse=reverse)
    return s_final, (jnp.moveaxis(ys, 0, 1) if emit else None)

def rwkv_readout(y, r, k_bonus, v, r_k, gn_w, gn_b):
    yf = y.astype(jnp.float32)
    mean = jnp.mean(yf, axis=-1, keepdims=True)
    var = jnp.mean(jnp.square(yf - mean), axis=-1, keepdims=True)
    yn = ((yf - mean) * lax.rsqrt(var + RWKV_GN_EPS)).reshape(y.shape[:2] + (BRANCH_W,))
    yn = (yn * gn_w + gn_b).astype(v.dtype)
    bonus = jnp.sum(r * k_bonus * r_k, axis=-1, keepdims=True) * v
    return yn + bonus.reshape(yn.shape)

def rwkv_branch(u_lat, u_ctx, mu, w0, w_up, a0, a_up, k_k, k_a, r_k, gn_w, gn_b, ctx_out):
    r, v, kk, dirs = rwkv_features(centred_token_shift(u_lat, mu), w0, w_up, a0, a_up, k_k, k_a)
    rc, vc, kkc, dirs_c = rwkv_features(centred_token_shift(u_ctx, mu), w0, w_up, a0, a_up, k_k, k_a)
    s0 = jnp.zeros((u_lat.shape[0], RWKV_HEADS, HEAD_DIM, HEAD_DIM), jnp.float32)
    y_lat, y_ctx = [], []
    for d in range(2):
        reverse = d == 1
        decay_c, k_c, b_c = dirs_c[d]
        s_ctx, yc = wkv_scan(s0, rc, decay_c, k_c, vc, kkc, b_c, reverse, ctx_out)
        decay_l, k_l, b_l = dirs[d]
        _, yl = wkv_scan(s_ctx, r, decay_l, k_l, v, kk, b_l, reverse, True)
        y_lat.append(yl)
        y_ctx.append(yc)
    out_lat = rwkv_readout(y_lat[0] + y_lat[1], r, 0.5 * (dirs[0][1] + dirs[1][1]), v, r_k, gn_w, gn_b)
    out_ctx = None
    if ctx_out:
        out_ctx = rwkv_readout(y_ctx[0] + y_ctx[1], rc, 0.5 * (dirs_c[0][1] + dirs_c[1][1]), vc, r_k, gn_w, gn_b)
    return out_lat, out_ctx

def hyena_filters(L, w1, b1, w2, b2, w3, b3):
    t_idx = jnp.arange(L, dtype=jnp.float32)
    t = t_idx / max(L - 1, 1)
    bands = jnp.linspace(1e-4, HY_POS_BANDS - 1, HY_POS_BANDS, dtype=jnp.float32)
    ang = 2.0 * math.pi * bands[None, :] * t_idx[:, None] / L
    feats = jnp.concatenate([t[:, None], jnp.cos(ang), -jnp.sin(ang)], axis=-1)
    hid = jnp.sin(feats @ w1 + b1)
    hid = jnp.sin(hid @ w2 + b2)
    taps = (hid @ w3 + b3).reshape(L, 2, HY_ORDER, HY_WIDTH)
    deltas = jnp.linspace(math.log(HY_DECAY_TARGET) / HY_FAST_DECAY_PCT,
                          math.log(HY_DECAY_TARGET) / HY_SLOW_DECAY_PCT, HY_WIDTH, dtype=jnp.float32)
    window = jnp.exp(-t[:, None] * jnp.abs(deltas))
    taps = taps * window[:, None, None, :]
    fwd, bwd = taps[:, 0], taps[:, 1]
    kern = jnp.concatenate([fwd[:1] + bwd[:1], fwd[1:], jnp.zeros_like(fwd[:1]), bwd[:0:-1]], axis=0)
    kern = kern.astype(jnp.float32)
    return kern * lax.rsqrt(jnp.sum(kern * kern, axis=0, keepdims=True))

def fft_long_conv(z, kern, skip):
    L = z.shape[1]
    zf = jnp.fft.rfft(z.astype(jnp.float32), n=2 * L, axis=1)
    kf = jnp.fft.rfft(kern, n=2 * L, axis=0)
    y = jnp.fft.irfft(zf * kf[None], n=2 * L, axis=1)[:, :L]
    return (y + z * skip).astype(z.dtype)

def hyena_operator(u, short_taps, kern, skip):
    v, x1, x2 = split_cols(centred_conv3(u, short_taps), (HY_WIDTH, HY_WIDTH, HY_WIDTH))
    z = v
    for o, gate in enumerate((x1, x2)):
        z = gate * fft_long_conv(z, kern[:, o], skip[o])
    return z

def attn_layer(x, ctx, c, c_ctx, norm_g, ada_w, ada_b, w_in, rpb, q_gain, k_gain, w_out, cos, sin, rows, ctx_out):
    b, n, _ = x.shape
    lc = ctx.shape[1]
    shift, scale, gate = adaln(c, ada_w, ada_b)
    shift_c, scale_c, gate_c = adaln(c_ctx, ada_w, ada_b)
    u = modulate(x, norm_g, shift[:, None], scale[:, None]) @ w_in
    uc = modulate(ctx, norm_g, shift_c, scale_c) @ w_in
    qa, ka, va, ga, qb, kb, vb, gb = split_cols(u, ATTN_SPLITS)
    qa_c, ka_c, va_c, ga_c, qb_c, kb_c, vb_c, gb_c = split_cols(uc, ATTN_SPLITS)
    ka_c, va_c = to_heads(ka_c, NA_HEADS), to_heads(va_c, NA_HEADS)
    o_a = neighbourhood_attention(to_heads(qa, NA_HEADS), to_heads(ka, NA_HEADS), to_heads(va, NA_HEADS),
                                  ka_c, va_c, rpb, rows)
    kb_c = rms_norm(to_heads(kb_c, GQA_KV_HEADS), k_gain)
    vb_c = to_heads(vb_c, GQA_KV_HEADS)
    q_lat = apply_axial_rope(rms_norm(to_heads(qb, GQA_HEADS), q_gain), cos, sin)
    q_lat = q_lat.reshape(b, n, GQA_KV_HEADS, GQA_GROUP, HEAD_DIM)
    k_lat = apply_axial_rope(rms_norm(to_heads(kb, GQA_KV_HEADS), k_gain), cos, sin)
    o_b = blockwise_gqa(q_lat, k_lat, to_heads(vb, GQA_KV_HEADS), kb_c, vb_c)
    y = jnp.concatenate([o_a.reshape(b, n, BRANCH_W) * jax.nn.silu(ga),
                         o_b.reshape(b, n, BRANCH_W) * jax.nn.silu(gb)], axis=-1) @ w_out
    x = x + gate[:, None] * y
    if ctx_out:
        oa_c = dense_gqa(to_heads(qa_c, NA_HEADS)[:, :, :, None], ka_c, va_c)
        qb_c = rms_norm(to_heads(qb_c, GQA_HEADS), q_gain).reshape(b, lc, GQA_KV_HEADS, GQA_GROUP, HEAD_DIM)
        ob_c = dense_gqa(qb_c, kb_c, vb_c)
        yc = jnp.concatenate([oa_c.reshape(b, lc, BRANCH_W) * jax.nn.silu(ga_c),
                              ob_c.reshape(b, lc, BRANCH_W) * jax.nn.silu(gb_c)], axis=-1) @ w_out
        ctx = ctx + gate_c * yc
    return x, ctx

def rec_layer(x, ctx, c, c_ctx, norm_g, ada_w, ada_b, w_in, mu, w0, w_up, a0, a_up, k_k, k_a, r_k, gn_w, gn_b,
              hy_short, hy_w1, hy_b1, hy_w2, hy_b2, hy_w3, hy_b3, hy_skip, w_out, ctx_out):
    shift, scale, gate = adaln(c, ada_w, ada_b)
    shift_c, scale_c, gate_c = adaln(c_ctx, ada_w, ada_b)
    u = modulate(x, norm_g, shift[:, None], scale[:, None]) @ w_in
    uc = modulate(ctx, norm_g, shift_c, scale_c) @ w_in
    u_rw, g_rw, u_hy, g_hy = split_cols(u, REC_SPLITS)
    uc_rw, gc_rw, uc_hy, gc_hy = split_cols(uc, REC_SPLITS)
    y_rw, yc_rw = rwkv_branch(u_rw, uc_rw, mu, w0, w_up, a0, a_up, k_k, k_a, r_k, gn_w, gn_b, ctx_out)
    y_hy = hyena_operator(u_hy, hy_short, hyena_filters(x.shape[1], hy_w1, hy_b1, hy_w2, hy_b2, hy_w3, hy_b3), hy_skip)
    y = jnp.concatenate([y_rw * jax.nn.silu(g_rw), y_hy * jax.nn.silu(g_hy)], axis=-1) @ w_out
    x = x + gate[:, None] * y
    if ctx_out:
        kern_c = hyena_filters(ctx.shape[1], hy_w1, hy_b1, hy_w2, hy_b2, hy_w3, hy_b3)
        yc_hy = hyena_operator(uc_hy, hy_short, kern_c, hy_skip)
        yc = jnp.concatenate([yc_rw * jax.nn.silu(gc_rw), yc_hy * jax.nn.silu(gc_hy)], axis=-1) @ w_out
        ctx = ctx + gate_c * yc
    return x, ctx

def first_inputs(seed: int = 0) -> dict:
    key = jax.random.key(seed)
    keys = iter(jax.random.split(key, 48))

    def normal(shape, scale=1.0):
        return scale * jax.random.normal(next(keys), shape, jnp.float32)

    na, nr, d = N_ATTN_LAYERS, N_REC_LAYERS, D_MODEL
    return {
        "x": normal((BATCH, SEQ, d)),
        "c": normal((BATCH, d)),
        "ctx": normal((BATCH, CTX_LEN, d)),
        "c_ctx": normal((d,)),
        "attn_norm": 1.0 + normal((na, d), 0.1),
        "attn_ada_w": normal((na, d, 3 * d), d ** -0.5),
        "attn_ada_b": normal((na, 3 * d), 0.1),
        "attn_w_in": normal((na, d, ATTN_IN), d ** -0.5),
        "na_rpb": normal((na, NA_HEADS, 2 * NA_WIN_ROWS - 1, 2 * NA_WIN_COLS - 1), 0.5),
        "gqa_q_gain": 1.0 + normal((na, HEAD_DIM), 0.1),
        "gqa_k_gain": 1.0 + normal((na, HEAD_DIM), 0.1),
        "attn_w_out": normal((na, MIX_W, d), MIX_W ** -0.5),
        "rec_norm": 1.0 + normal((nr, d), 0.1),
        "rec_ada_w": normal((nr, d, 3 * d), d ** -0.5),
        "rec_ada_b": normal((nr, 3 * d), 0.1),
        "rec_w_in": normal((nr, d, REC_IN), d ** -0.5),
        "rwkv_mu": jax.random.uniform(next(keys), (nr, RWKV_SHIFT_W), jnp.float32),
        "rwkv_w0": jnp.linspace(-6.0, -0.5, BRANCH_W, dtype=jnp.float32) + normal((nr, 2, BRANCH_W), 0.1),
        "rwkv_w_up": normal((nr, 2, DECAY_LORA, BRANCH_W), 0.1),
        "rwkv_a0": normal((nr, 2, BRANCH_W), 0.5),
        "rwkv_a_up": normal((nr, 2, ICLR_LORA, BRANCH_W), ICLR_LORA ** -0.5),
        "rwkv_k_k": 0.85 + normal((nr, BRANCH_W), 0.05),
        "rwkv_k_a": 1.0 + normal((nr, BRANCH_W), 0.05),
        "rwkv_r_k": normal((nr, RWKV_HEADS, HEAD_DIM), 0.1),
        "rwkv_gn_w": 1.0 + normal((nr, BRANCH_W), 0.1),
        "rwkv_gn_b": normal((nr, BRANCH_W), 0.1),
        "hy_short": normal((nr, 3, HY_IN_W), 3 ** -0.5),
        "hy_w1": normal((nr, HY_POS_DIM, HY_FILTER_HIDDEN), HY_POS_DIM ** -0.5),
        "hy_b1": normal((nr, HY_FILTER_HIDDEN), 0.1),
        "hy_w2": normal((nr, HY_FILTER_HIDDEN, HY_FILTER_HIDDEN), HY_FILTER_HIDDEN ** -0.5),
        "hy_b2": normal((nr, HY_FILTER_HIDDEN), 0.1),
        "hy_w3": normal((nr, HY_FILTER_HIDDEN, 2 * HY_ORDER * HY_WIDTH), HY_FILTER_HIDDEN ** -0.5),
        "hy_b3": normal((nr, 2 * HY_ORDER * HY_WIDTH), 0.1),
        "hy_skip": normal((nr, HY_ORDER, HY_WIDTH), 0.5),
        "rec_w_out": normal((nr, MIX_W, d), MIX_W ** -0.5),
        "final_norm": 1.0 + normal((d,), 0.1),
    }

def first_block(x, c, ctx, c_ctx, attn_norm, attn_ada_w, attn_ada_b, attn_w_in, na_rpb, gqa_q_gain, gqa_k_gain,
              attn_w_out, rec_norm, rec_ada_w, rec_ada_b, rec_w_in, rwkv_mu, rwkv_w0, rwkv_w_up, rwkv_a0, rwkv_a_up,
              rwkv_k_k, rwkv_k_a, rwkv_r_k, rwkv_gn_w, rwkv_gn_b, hy_short, hy_w1, hy_b1, hy_w2, hy_b2, hy_w3, hy_b3,
              hy_skip, rec_w_out, final_norm):
    n = x.shape[1]
    rows = n // GRID_W
    cos, sin = axial_rope_tables(n)
    for layer in range(DEPTH):
        i = layer // 2
        ctx_out = layer < DEPTH - 1
        if layer % 2 == 0:
            x, ctx = attn_layer(x, ctx, c, c_ctx, attn_norm[i], attn_ada_w[i], attn_ada_b[i], attn_w_in[i],
                                na_rpb[i], gqa_q_gain[i], gqa_k_gain[i], attn_w_out[i], cos, sin, rows, ctx_out)
        else:
            x, ctx = rec_layer(x, ctx, c, c_ctx, rec_norm[i], rec_ada_w[i], rec_ada_b[i], rec_w_in[i],
                               rwkv_mu[i], rwkv_w0[i], rwkv_w_up[i], rwkv_a0[i], rwkv_a_up[i], rwkv_k_k[i],
                               rwkv_k_a[i], rwkv_r_k[i], rwkv_gn_w[i], rwkv_gn_b[i], hy_short[i], hy_w1[i],
                               hy_b1[i], hy_w2[i], hy_b2[i], hy_w3[i], hy_b3[i], hy_skip[i], rec_w_out[i], ctx_out)
    return rms_norm(x, final_norm)


DEPTH_2 = 1

MIX_WIDTH = D_MODEL
A_WIDTH = MIX_WIDTH // 2
B_WIDTH = MIX_WIDTH - A_WIDTH
A_GROUPS = A_WIDTH // HEAD_DIM
A_GROUP_DIM = A_WIDTH // A_GROUPS
B_HEADS = B_WIDTH // HEAD_DIM
CHUNK = 128
D_FF = ((8 * D_MODEL // 3 + 255) // 256) * 256
COL_A_U = 0
COL_A_V = COL_A_U + A_WIDTH
COL_B_Q = COL_A_V + A_WIDTH
COL_B_K = COL_B_Q + B_WIDTH
COL_B_V = COL_B_K + B_WIDTH
COL_B_F = COL_B_V + B_WIDTH
IN_COLS = COL_B_F + B_HEADS
RMS_EPS = 1e-6
LN_EPS = 1e-5


def _rmsnorm(x, g):
    x32 = x.astype(jnp.float32)
    y = x32 * lax.rsqrt(jnp.mean(x32 * x32, axis=-1, keepdims=True) + RMS_EPS)
    return (y * g.astype(jnp.float32)).astype(x.dtype)

def _layernorm(x, g, b):
    x32 = x.astype(jnp.float32)
    mu = jnp.mean(x32, axis=-1, keepdims=True)
    var = jnp.mean(jnp.square(x32 - mu), axis=-1, keepdims=True)
    y = (x32 - mu) * lax.rsqrt(var + LN_EPS)
    return (y * g.astype(jnp.float32) + b.astype(jnp.float32)).astype(x.dtype)

def _spatial_gating(u, v, ln_g, ln_b, w_s, b_s):
    B, S, _ = v.shape
    nc = S // CHUNK
    v = _layernorm(v, ln_g, ln_b)
    v = v.reshape(B, nc, CHUNK, A_GROUPS, A_GROUP_DIM)
    tril = jnp.tril(jnp.ones((CHUNK, CHUNK), dtype=w_s.dtype))
    w_masked = w_s * tril[None]
    mixed = jnp.einsum('gts,bcsgd->bctgd', w_masked, v) + b_s.T[None, None, :, :, None]
    out = u.reshape(B, nc, CHUNK, A_GROUPS, A_GROUP_DIM) * mixed
    return out.reshape(B, S, A_WIDTH)

def _forgetting_attention(q, k, v, f_logit, b_f):
    B, S, _ = q.shape
    def heads(t):
        return t.reshape(B, S, B_HEADS, HEAD_DIM).transpose(0, 2, 1, 3)
    q, k, v = heads(q), heads(k), heads(v)
    log_f = jax.nn.log_sigmoid(f_logit.astype(jnp.float32) + b_f.astype(jnp.float32))
    c = jnp.cumsum(log_f, axis=1).transpose(0, 2, 1)
    scale = HEAD_DIM ** -0.5
    pos = jnp.arange(S)
    outs = []
    for i in range(S // Q_BLOCK):
        q0, q1 = i * Q_BLOCK, (i + 1) * Q_BLOCK
        q_blk = q[:, :, q0:q1]
        k_blk = k[:, :, :q1]
        v_blk = v[:, :, :q1]
        logits = jnp.einsum('bhqd,bhkd->bhqk', q_blk, k_blk).astype(jnp.float32) * scale
        logits = logits + c[:, :, q0:q1, None] - c[:, :, None, :q1]
        mask = pos[q0:q1, None] >= pos[None, :q1]
        logits = jnp.where(mask[None, None], logits, -jnp.inf)
        p = jax.nn.softmax(logits, axis=-1).astype(v.dtype)
        outs.append(jnp.einsum('bhqk,bhkd->bhqd', p, v_blk))
    o = jnp.concatenate(outs, axis=2)
    return o.transpose(0, 2, 1, 3).reshape(B, S, B_WIDTH)

def second_inputs(seed: int = 0) -> dict:
    key = jax.random.key(seed)
    ks = jax.random.split(key, 20)
    f32 = jnp.float32
    L = DEPTH_2
    def nrm(k, shape, scale):
        return jax.random.normal(k, shape, f32) * scale
    return {
        "x": jax.random.normal(ks[0], (BATCH, SEQ, D_MODEL), f32),
        "pre_mix_gain": 1.0 + nrm(ks[1], (L, D_MODEL), 0.02),
        "w_in": nrm(ks[2], (L, D_MODEL, IN_COLS), D_MODEL ** -0.5),
        "ln_v_gain": 1.0 + nrm(ks[3], (L, A_WIDTH), 0.02),
        "ln_v_bias": nrm(ks[4], (L, A_WIDTH), 0.02),
        "w_spatial": nrm(ks[5], (L, A_GROUPS, CHUNK, CHUNK), 0.5 * CHUNK ** -0.5),
        "b_spatial": 1.0 + nrm(ks[6], (L, A_GROUPS, CHUNK), 0.1),
        "b_forget": 2.0 + nrm(ks[7], (L, B_HEADS), 0.5),
        "out_norm_a_gain": 1.0 + nrm(ks[8], (L, A_WIDTH), 0.02),
        "out_norm_b_gain": 1.0 + nrm(ks[9], (L, B_WIDTH), 0.02),
        "w_out": nrm(ks[10], (L, MIX_WIDTH, D_MODEL), MIX_WIDTH ** -0.5),
        "post_mix_gain": 1.0 + nrm(ks[11], (L, D_MODEL), 0.02),
        "pre_ffn_gain": 1.0 + nrm(ks[12], (L, D_MODEL), 0.02),
        "w_ffn_in": nrm(ks[13], (L, D_MODEL, 2 * D_FF), D_MODEL ** -0.5),
        "w_ffn_out": nrm(ks[14], (L, D_FF, D_MODEL), D_FF ** -0.5),
        "post_ffn_gain": 1.0 + nrm(ks[15], (L, D_MODEL), 0.02),
    }

def second_block(x, pre_mix_gain, w_in, ln_v_gain, ln_v_bias, w_spatial, b_spatial,
              b_forget, out_norm_a_gain, out_norm_b_gain, w_out, post_mix_gain,
              pre_ffn_gain, w_ffn_in, w_ffn_out, post_ffn_gain):
    h = x
    for l in range(DEPTH_2):
        n = _rmsnorm(h, pre_mix_gain[l])
        proj = jnp.einsum('bsd,dc->bsc', n, w_in[l])
        a_u = jax.nn.gelu(proj[..., COL_A_U:COL_A_V], approximate=False)
        a_v = jax.nn.gelu(proj[..., COL_A_V:COL_B_Q], approximate=False)
        a_out = _spatial_gating(a_u, a_v, ln_v_gain[l], ln_v_bias[l],
                                w_spatial[l], b_spatial[l])
        b_out = _forgetting_attention(proj[..., COL_B_Q:COL_B_K],
                                      proj[..., COL_B_K:COL_B_V],
                                      proj[..., COL_B_V:COL_B_F],
                                      proj[..., COL_B_F:IN_COLS],
                                      b_forget[l])
        merged = jnp.concatenate([_rmsnorm(a_out, out_norm_a_gain[l]),
                                  _rmsnorm(b_out, out_norm_b_gain[l])], axis=-1)
        mix = jnp.einsum('bsc,cd->bsd', merged, w_out[l])
        h = h + _rmsnorm(mix, post_mix_gain[l])
        n2 = _rmsnorm(h, pre_ffn_gain[l])
        gu = jnp.einsum('bsd,df->bsf', n2, w_ffn_in[l])
        ff = jax.nn.silu(gu[..., :D_FF]) * gu[..., D_FF:]
        ff = jnp.einsum('bsf,fd->bsd', ff, w_ffn_out[l])
        h = h + _rmsnorm(ff, post_ffn_gain[l])
    return h


_first_inputs = second_inputs


def second_inputs(seed=0):
    import zlib

    import numpy as np

    out = dict(_first_inputs(seed))
    spreads = {}
    factors = {'ln_v_gain': 8.0,
     'ln_v_bias': 8.0,
     'out_norm_a_gain': 5.117,
     'out_norm_b_gain': 4.957,
     'post_mix_gain': 3.435,
     'pre_ffn_gain': 3.481,
     'post_ffn_gain': 4.955}
    for name, (base, spread) in spreads.items():
        noise = np.random.default_rng([zlib.crc32(name.encode()), seed]).standard_normal(out[name].shape)
        drawn = base * np.exp(spread * noise) if base else spread * noise
        out[name] = __import__('jax').numpy.asarray(drawn.astype(out[name].dtype))
    for name, factor in factors.items():
        out[name] = (out[name] * factor).astype(out[name].dtype)
    return out


_narrow_inputs = second_inputs


def second_inputs(seed=0):

    out = dict(_narrow_inputs(seed))
    wider = {'ln_v_gain': 4.2,
     'ln_v_bias': 4.13,
     'out_norm_a_gain': 3.75,
     'out_norm_b_gain': 3.74,
     'post_ffn_gain': 3.97}
    for name, times in wider.items():
        mean = out[name].mean()
        out[name] = (mean + times * (out[name] - mean)).astype(out[name].dtype)
    return out


def setup_inputs(seed=0):
    out = dict(first_inputs(seed))
    for name, value in second_inputs(seed + 1).items():
        if name != "x":
            out[name + "_2"] = value
    return out


def reference(
    x, c, ctx, c_ctx, attn_norm, attn_ada_w, attn_ada_b, attn_w_in, na_rpb, gqa_q_gain,
    gqa_k_gain, attn_w_out, rec_norm, rec_ada_w, rec_ada_b, rec_w_in, rwkv_mu, rwkv_w0,
    rwkv_w_up, rwkv_a0, rwkv_a_up, rwkv_k_k, rwkv_k_a, rwkv_r_k, rwkv_gn_w, rwkv_gn_b, hy_short,
    hy_w1, hy_b1, hy_w2, hy_b2, hy_w3, hy_b3, hy_skip, rec_w_out, final_norm, pre_mix_gain_2,
    w_in_2, ln_v_gain_2, ln_v_bias_2, w_spatial_2, b_spatial_2, b_forget_2, out_norm_a_gain_2,
    out_norm_b_gain_2, w_out_2, post_mix_gain_2, pre_ffn_gain_2, w_ffn_in_2, w_ffn_out_2,
    post_ffn_gain_2,
):
    x = first_block(
        x, c, ctx, c_ctx, attn_norm, attn_ada_w, attn_ada_b, attn_w_in, na_rpb, gqa_q_gain,
        gqa_k_gain, attn_w_out, rec_norm, rec_ada_w, rec_ada_b, rec_w_in, rwkv_mu, rwkv_w0,
        rwkv_w_up, rwkv_a0, rwkv_a_up, rwkv_k_k, rwkv_k_a, rwkv_r_k, rwkv_gn_w, rwkv_gn_b,
        hy_short, hy_w1, hy_b1, hy_w2, hy_b2, hy_w3, hy_b3, hy_skip, rec_w_out, final_norm,
    )
    return second_block(
        x, pre_mix_gain_2, w_in_2, ln_v_gain_2, ln_v_bias_2, w_spatial_2, b_spatial_2,
        b_forget_2, out_norm_a_gain_2, out_norm_b_gain_2, w_out_2, post_mix_gain_2,
        pre_ffn_gain_2, w_ffn_in_2, w_ffn_out_2, post_ffn_gain_2,
    )


_drawn_inputs = setup_inputs


def setup_inputs(seed=0):
    import zlib

    import numpy as np

    out = dict(_drawn_inputs(seed))
    spreads = {}
    factors = {'gqa_q_gain': 6.051,
     'gqa_k_gain': 5.809,
     'rwkv_w_up': 3.58,
     'rwkv_gn_w': 4.69,
     'rwkv_gn_b': 3.771}
    for name, (base, spread) in spreads.items():
        noise = np.random.default_rng([zlib.crc32(name.encode()), seed]).standard_normal(out[name].shape)
        drawn = base * np.exp(spread * noise) if base else spread * noise
        out[name] = jnp.asarray(drawn.astype(out[name].dtype))
    for name, factor in factors.items():
        out[name] = (out[name] * factor).astype(out[name].dtype)
    return out
```

```python
from contextlib import ExitStack

import numpy as np
import concourse.bass as bass
from concourse import mybir

F32 = mybir.dt.float32
ACT = mybir.ActivationFunctionType
ALU = mybir.AluOpType
AX = mybir.AxisListType

P = 128
D = 1024
KT = D // P
LAT = 1024
CTX = 256
TOK = LAT + CTX
LT = LAT // P
CT = CTX // P
HD = 64
HEADS = 8
HW = HEADS * HD
ATTN_IN = 3328
REC_IN = 4224
BLK_IN = 2568
FF = 2816
NORM_EPS = 1e-6


class Linked:

    def __init__(self, eng, sem):
        self.eng, self.sem, self.n = eng, sem, 0

    def __call__(self, ins):
        self.n += 1
        ins.then_inc(self.sem, 1)
        self.eng.wait_ge(self.sem, self.n)


class Stage:

    def __init__(self, nc, name):
        self.nc, self.name, self.stack, self.sems, self.n = nc, name, ExitStack(), [], 0

    def __enter__(self):
        return self

    def sb(self, name, shape, dt=F32, side="left"):
        return self.stack.enter_context(self.nc.sbuf_tensor(f"{self.name}_{name}", shape, dt, side=side))

    def ps(self, name, shape=(P, 512), dt=F32):
        return self.stack.enter_context(self.nc.psum_tensor(f"{self.name}_{name}", list(shape), dt))

    def sem(self, name):
        s = self.stack.enter_context(self.nc.semaphore(f"{self.name}_{name}"))
        self.sems.append(s)
        return s

    def clear(self):
        for s in self.sems:
            self.nc.sync.sem_clear(s)
        self.nc.all_engine_barrier()

    def __exit__(self, *a):
        if a[0] is None:
            self.clear()
        self.stack.close()


def cols(v):
    return v.rearrange("(k p) -> p k", p=P)


def adaln_stage(nc, ap, pre, keep):
    name = "ada" + pre
    with Stage(nc, name) as st:
        w = st.sb("w", [P, KT, 3 * D])
        cc = st.sb("cc", [P, KT, 2])
        sc = st.sb("sc", [P, KT, 2])
        wide = st.sb("wide", [P, KT, 2, P])
        bcol = st.sb("bcol", [P, 16])
        gcol = st.sb("gcol", [P, KT])
        brow = st.sb("brow", [P, D])
        pc = st.ps("pc")
        pg = [st.ps(f"pg{i}") for i in range(4)]
        w_in, small_in, silu, spread, cols_mm, gate_mm, dve_seq = (st.sem(n) for n in (
            "w_in", "small_in", "silu", "spread", "cols_mm", "gate_mm", "dve_seq"))
        wd = ap[pre + "_ada_w"][0].rearrange("(k p) n -> p k n", p=P)
        modA, modB, gate = keep
        with nc.Block() as block:
            @block.sync
            def _(sp):
                sp.dma_start(cc[:, :, 0], cols(ap["c"][0]), allow_slow_non_contiguous=True).then_inc(small_in, 16)
                sp.dma_start(cc[:, :, 1], cols(ap["c_ctx"]), allow_slow_non_contiguous=True).then_inc(small_in, 16)
                for k in range(KT):
                    sp.dma_start(w[:, k, :], wd[:, k, :]).then_inc(w_in, 16)
                sp.dma_start(bcol[:, :], cols(ap[pre + "_ada_b"][0][0:2 * D]), allow_slow_non_contiguous=True).then_inc(small_in, 16)
                sp.dma_start(gcol[:, :], cols(ap[pre + "_norm"][0]), allow_slow_non_contiguous=True).then_inc(small_in, 16)
                sp.dma_start(brow[:, :], ap[pre + "_ada_b"][0][2 * D:3 * D].partition_broadcast(P)).then_inc(small_in, 16)

            @block.scalar
            def _(act):
                act.wait_ge(small_in, 80)
                nc.scalar.activation(sc[:, :, :], cc[:, :, :], ACT.Silu).then_inc(silu, 1)

            @block.tensor
            def _(pe):
                pe.wait_ge(silu, 1)
                pe.wait_ge(w_in, 16 * KT)
                for n in range(16):
                    for k in range(KT):
                        mm = pe.matmul(pc[:, 2 * n:2 * n + 2], w[:, k, n * P:(n + 1) * P], sc[:, k, :],
                                       start=(k == 0), stop=(k == KT - 1))
                mm.then_inc(cols_mm, 1)
                pe.wait_ge(spread, 1)
                for v in range(2):
                    for h in range(2):
                        for k in range(KT):
                            mm = pe.matmul(pg[2 * v + h][:, :], wide[:, k, v, :],
                                           w[:, k, 2 * D + 512 * h:2 * D + 512 * (h + 1)],
                                           start=(k == 0), stop=(k == KT - 1))
                mm.then_inc(gate_mm, 1)

            @block.vector
            def _(dve):
                link = Linked(dve, dve_seq)
                dve.wait_ge(silu, 1)
                dve.tensor_copy(wide[:, :, :, :], sc[:, :, :].unsqueeze(3).to_broadcast([P, KT, 2, P])).then_inc(spread, 1)
                dve.wait_ge(small_in, 80)
                dve.wait_ge(cols_mm, 1)
                pcv = pc[:, 0:32].rearrange("p (n v) -> p v n", v=2)
                for v in range(2):
                    link(dve.tensor_tensor(modB[:, v, :], pcv[:, v, 0:8], bcol[:, 0:8], ALU.add))
                    link(dve.tensor_tensor(modA[:, v, :], pcv[:, v, 8:16], bcol[:, 8:16], ALU.add))
                    link(dve.tensor_scalar(modA[:, v, :], modA[:, v, :], 1.0, None, ALU.add))
                    link(dve.tensor_tensor(modA[:, v, :], modA[:, v, :], gcol[:, :], ALU.mult))
                dve.wait_ge(gate_mm, 1)
                for v in range(2):
                    for h in range(2):
                        s = slice(512 * h, 512 * h + 512)
                        link(dve.tensor_tensor(gate[:, v, s], pg[2 * v + h][:, :], brow[:, s], ALU.add))


def norm_stage(nc, name, ident, tiles, xT, x_of, y_of=None, gate=None, y_row=None, z_row=None, z_out=None,
               modA=None, modB=None):
    lo, hi = tiles
    with Stage(nc, name) as st:
        x = [st.sb(f"x{p}", [P, D]) for p in range(2)]
        y = [st.sb(f"y{p}", [P, D]) for p in range(2)] if y_of else None
        sq = st.sb("sq", [P, D])
        t = [st.sb(f"t{p}", [P, D]) for p in range(2)]
        row = st.sb("row", [P, D])
        ss = st.sb("ss", [P, 8])
        rs = st.sb("rs", [P, 8])
        pt = [st.ps(f"pt{i}") for i in range(4)]
        loaded = [st.sem(f"loaded{p}") for p in range(2)]
        row_in = st.sem("row_in")
        z_ready, ss_ready, ms_ready, rt_ready, xn_ready, trans, evac, stored, dve_seq, zz = (st.sem(n) for n in (
            "z_ready", "ss_ready", "ms_ready", "rt_ready", "xn_ready", "trans", "evac", "stored", "dve_seq", "zz"))
        rms_of = []
        for p in range(2):
            if y_row is not None:
                rms_of.append((p, "y"))
            if z_row is not None:
                rms_of.append((p, "z"))
            if xT is not None:
                rms_of.append((p, "n"))
        rowsrc = y_row if y_row is not None else z_row
        if rowsrc is not None:
            with nc.Block() as block:
                @block.sync
                def _(sp):
                    sp.dma_start(row[:, :], rowsrc.partition_broadcast(P)).then_inc(row_in, 16)
                    sp.wait_ge(row_in, 16)
        with nc.Fori(lo, hi) as i:
            with nc.Block() as block:
                nload = 32 if y_of else 16

                @block.sync
                def _(sp):
                    for p in range(2):
                        sp.dma_start(x[p][:, :], x_of(i, p)).then_inc(loaded[p], 16)
                        if y_of:
                            sp.dma_start(y[p][:, :], y_of(i, p)).then_inc(loaded[p], 16)
                    if z_out:
                        for p in range(2):
                            sp.wait_ge(zz, p + 1)
                            sp.dma_start(z_out(i, p), x[p][:, :]).then_inc(stored, 16)
                        sp.wait_ge(stored, 32)

                @block.scalar
                def _(act):
                    for n, (p, what) in enumerate(rms_of):
                        src = y[p] if what == "y" else x[p]
                        act.wait_ge(loaded[p], nload)
                        act.wait_ge(z_ready, n + 1)
                        nc.scalar.activation(sq[:, :], src[:, :], ACT.Square, accum_out=ss[:, n:n + 1]).then_inc(ss_ready, 1)
                        act.wait_ge(ms_ready, n + 1)
                        nc.scalar.activation(rs[:, n:n + 1], ss[:, n:n + 1], ACT.Sqrt).then_inc(rt_ready, 1)
                        if what == "n":
                            for b in range(2):
                                act.wait_ge(trans, 2 * p + b + 1)
                                for k in range(4 * b, 4 * b + 4, 1):
                                    nc.scalar.activation(
                                        xT[:, k, bass.ds(i * 2 * P + p * P, P)], pt[2 * p + b][:, (k % 4) * P:(k % 4 + 1) * P],
                                        ACT.Identity, scale=modA[:, k:k + 1],
                                        bias=(modB[:, k:k + 1] if modB is not None else 0.0)).then_inc(evac, 1)

                @block.tensor
                def _(pe):
                    if xT is not None:
                        for p in range(2):
                            pe.wait_ge(xn_ready, p + 1)
                            for b in range(2):
                                for k in range(4):
                                    mm = pe.transpose(pt[2 * p + b][:, k * P:(k + 1) * P],
                                                      t[p][:, (4 * b + k) * P:(4 * b + k + 1) * P], ident[:, :])
                                mm.then_inc(trans, 1)

                @block.vector
                def _(dve):
                    link = Linked(dve, dve_seq)
                    n = 0

                    def rstd(n):
                        dve.wait_ge(ss_ready, n + 1)
                        dve.tensor_scalar(ss[:, n:n + 1], ss[:, n:n + 1], 1.0 / D, NORM_EPS, ALU.mult, ALU.add).then_inc(ms_ready, 1)
                        dve.wait_ge(rt_ready, n + 1)
                        link(dve.reciprocal(rs[:, n:n + 1], rs[:, n:n + 1]))

                    for p in range(2):
                        dve.wait_ge(loaded[p], nload)
                        if gate is not None:
                            link(dve.tensor_tensor(t[p][:, :], y[p][:, :], gate[:, :], ALU.mult))
                            link(dve.tensor_tensor(x[p][:, :], x[p][:, :], t[p][:, :], ALU.add))
                        if y_row is not None:
                            dve.sem_inc(z_ready, 1)
                            rstd(n)
                            link(dve.scalar_tensor_tensor(out=t[p][:, :], in0=y[p][:, :], scalar=rs[:, n:n + 1],
                                                          in1=row[:, :], op0=ALU.mult, op1=ALU.mult))
                            link(dve.tensor_tensor(x[p][:, :], x[p][:, :], t[p][:, :], ALU.add))
                            n += 1
                        if z_row is not None:
                            dve.sem_inc(z_ready, 1)
                            rstd(n)
                            link(dve.scalar_tensor_tensor(out=x[p][:, :], in0=x[p][:, :], scalar=rs[:, n:n + 1],
                                                          in1=row[:, :], op0=ALU.mult, op1=ALU.mult))
                            n += 1
                        if z_out:
                            dve.sem_inc(zz, 1)
                        if xT is not None:
                            dve.sem_inc(z_ready, 1)
                            rstd(n)
                            dve.tensor_scalar(t[p][:, :], x[p][:, :], rs[:, n:n + 1], None, ALU.mult).then_inc(xn_ready, 1)
                            n += 1
            st.clear()


def gemm_stage(nc, name, xT, kt, mt, w_of, nb, wn, out_of):
    R = 4 if mt % 4 == 0 else 5
    per = mt // R
    with Stage(nc, name) as st:
        w = [st.sb(f"w{b}", [P, kt, wn]) for b in range(2)]
        o = [st.sb(f"o{r}", [P, wn]) for r in range(R)]
        acc = [st.ps(f"acc{r}") for r in range(R)]
        w_in = [st.sem(f"w_in{b}") for b in range(2)]
        summed = [st.sem(f"summed{r}") for r in range(R)]
        emptied = [st.sem(f"emptied{r}") for r in range(R)]
        stored = [st.sem(f"stored{r}") for r in range(R)]
        with nc.Block() as block:
            @block.sync
            def _(sp):
                for b in range(2):
                    sp.dma_start(w[b][:, :, :], w_of(0, b)).then_inc(w_in[b], 16)
                for r in range(R):
                    sp.sem_inc(stored[r], 16)

                def stores(j, b):
                    for m in range(mt):
                        r = m % R
                        sp.wait_ge(emptied[r], (j * 2 + b) * per + m // R + 2)
                        sp.dma_start(out_of(j, b, m), o[r][:, :]).then_inc(stored[r], 16)

                if nb > 1:
                    with sp.Fori(0, nb - 1) as j:
                        for b in range(2):
                            stores(j, b)
                            sp.wait_ge(summed[R - 1], (j * 2 + b) * per + per)
                            sp.dma_start(w[b][:, :, :], w_of(j + 1, b)).then_inc(w_in[b], 16)
                for b in range(2):
                    stores(nb - 1, b)
                for r in range(R):
                    sp.wait_ge(stored[r], 16 * (2 * nb * per + 1))

            @block.tensor
            def _(pe):
                for r in range(R):
                    pe.sem_inc(emptied[r], 1)
                with pe.Fori(0, nb) as j:
                    for b in range(2):
                        pe.wait_ge(w_in[b], j * 16 + 16)
                        for m in range(mt):
                            r = m % R
                            pe.wait_ge(emptied[r], (j * 2 + b) * per + m // R + 1)
                            for k in range(kt):
                                mm = pe.matmul(acc[r][:, 0:wn], xT[:, k, m * P:(m + 1) * P], w[b][:, k, :],
                                               start=(k == 0), stop=(k == kt - 1))
                            mm.then_inc(summed[r], 1)

            def copies(eng, odd):
                with eng.Fori(0, nb) as j:
                    for b in range(2):
                        for m in range(mt):
                            r = m % R
                            if m % 2 != odd:
                                continue
                            eng.wait_ge(summed[r], (j * 2 + b) * per + m // R + 1)
                            eng.wait_ge(stored[r], (j * 2 + b) * per * 16 + m // R * 16 + 16)
                            if odd:
                                nc.scalar.copy(o[r][:, :], acc[r][:, 0:wn]).then_inc(emptied[r], 1)
                            else:
                                nc.vector.tensor_copy(o[r][:, :], acc[r][:, 0:wn]).then_inc(emptied[r], 1)

            @block.scalar
            def _(act):
                copies(act, 1)

            @block.vector
            def _(dve):
                copies(dve, 0)


def attn_prep_stage(nc, ap, ident, U, QT, pairs, rope_rows, row0):
    NH = 10
    lo, hi = pairs
    with Stage(nc, f"prep{lo}") as st:
        u = [st.sb(f"u{p}", [P, 2688]) for p in range(2)]
        sq = st.sb("sq", [P, NH, HD])
        xn = [st.sb(f"xn{p}", [P, NH, HD]) for p in range(2)]
        tmp = st.sb("tmp", [P, NH, HD])
        cs = [st.sb(f"cs{p}", [P, 2, HD]) for p in range(2)]
        gain = st.sb("gain", [P, NH, HD])
        gq = st.sb("gq", [P, 2, HD])
        ss = st.sb("ss", [P, 2, NH])
        tb = st.sb("tb", [P, 13, 2 * P])
        pt = [st.ps(f"pt{i}") for i in range(8)]
        loaded = [st.sem(f"loaded{p}") for p in range(2)]
        gains_in, ss_ready, ms_ready, rt_ready, roped, trans, evac_a, evac_v, stored, dve_seq = (st.sem(n) for n in (
            "gains_in", "ss_ready", "ms_ready", "rt_ready", "roped", "trans", "evac_a", "evac_v", "stored", "dve_seq"))
        with nc.Block() as block:
            @block.sync
            def _(sp):
                sp.dma_start(gq[:, 0, :], ap["gqa_q_gain"][0].partition_broadcast(P)).then_inc(gains_in, 16)
                sp.dma_start(gq[:, 1, :], ap["gqa_k_gain"][0].partition_broadcast(P)).then_inc(gains_in, 16)

            @block.vector
            def _(dve):
                link = Linked(dve, dve_seq)
                dve.wait_ge(gains_in, 32)
                link(dve.tensor_scalar(gain[:, 0:8, :], gq[:, 0:1, :].to_broadcast([P, 8, HD]), HD ** -0.5, None, ALU.mult))
                link(dve.tensor_copy(gain[:, 8:10, :], gq[:, 1:2, :].to_broadcast([P, 2, HD])))
        st.clear()
        SRC = [c * P for c in range(8)]
        with nc.Fori(lo, hi) as i:
            with nc.Block() as block:
                @block.sync
                def _(sp):
                    for p in range(2):
                        sp.dma_start(u[p][:, 0:1024], U.rearrange("(n q p) d -> n q p d", q=2, p=P)[i, p][:, 0:1024]).then_inc(loaded[p], 16)
                        sp.dma_start(u[p][:, 2048:2688], U.rearrange("(n q p) d -> n q p d", q=2, p=P)[i, p][:, 2048:2688]).then_inc(loaded[p], 16)
                        sp.dma_start(cs[p][:, :, :], ap["rope"].rearrange("(n q p) a d -> n q p a d", q=2, p=P)[i, p]).then_inc(loaded[p], 16)
                    sp.wait_ge(evac_a, 4)
                    sp.wait_ge(evac_v, 4)
                    sp.dma_start(QT.rearrange("(b p) (n t) -> n p b t", p=P, t=2 * P)[i], tb[:, :, :]).then_inc(stored, 16)
                    sp.wait_ge(stored, 16)

                @block.scalar
                def _(act):
                    for p in range(2):
                        act.wait_ge(loaded[p], 48)
                        if p:
                            act.wait_ge(ms_ready, p)
                        nc.scalar.activation(sq[:, :, :], u[p][:, 2048:2688].rearrange("p (h d) -> p h d", d=HD), ACT.Square).then_inc(ss_ready, 1)
                        act.wait_ge(ms_ready, p + 1)
                        nc.scalar.activation(ss[:, p, :], ss[:, p, :], ACT.Sqrt).then_inc(rt_ready, 1)
                    for p in range(2):
                        for b in range(2):
                            act.wait_ge(trans, 2 * p + b + 1)
                            nc.scalar.mul(tb[:, 4 * b:4 * b + 4, p * P:(p + 1) * P],
                                          pt[4 * p + b][:, :].rearrange("p (b t) -> p b t", t=P),
                                          HD ** -0.5 if b == 0 else 1.0).then_inc(evac_a, 1)

                @block.tensor
                def _(pe):
                    for p in range(2):
                        pe.wait_ge(loaded[p], 48)
                        for b in range(2):
                            for k in range(4):
                                mm = pe.transpose(pt[4 * p + b][:, k * P:(k + 1) * P], u[p][:, (4 * b + k) * P:(4 * b + k + 1) * P], ident[:, :])
                            mm.then_inc(trans, 1)
                    for p in range(2):
                        pe.wait_ge(roped, p + 1)
                        xf = xn[p][:, :, :].rearrange("p h d -> p (h d)")
                        for k in range(5):
                            mm = pe.transpose(pt[4 * p + 2 + k // 4][:, (k % 4) * P:(k % 4 + 1) * P], xf[:, k * P:(k + 1) * P], ident[:, :])
                            if k in (3, 4):
                                mm.then_inc(trans, 1)

                @block.vector
                def _(dve):
                    link = Linked(dve, dve_seq)
                    for p in range(2):
                        dve.wait_ge(ss_ready, p + 1)
                        link(dve.tensor_reduce(ss[:, p, :], sq[:, :, :], AX.X, ALU.add))
                        dve.tensor_scalar(ss[:, p, :], ss[:, p, :], 1.0 / HD, NORM_EPS, ALU.mult, ALU.add).then_inc(ms_ready, 1)
                        dve.wait_ge(rt_ready, p + 1)
                        link(dve.reciprocal(ss[:, p, :], ss[:, p, :]))
                        link(dve.tensor_tensor(xn[p][:, :, :], u[p][:, 2048:2688].rearrange("p (h d) -> p h d", d=HD),
                                               ss[:, p, :].unsqueeze(2).to_broadcast([P, NH, HD]), ALU.mult))
                        link(dve.tensor_tensor(xn[p][:, :, :], xn[p][:, :, :], gain[:, :, :], ALU.mult))
                        for a in range(2):
                            for s in range(2):
                                to, of = 32 * a + 16 * s, 32 * a + 16 * (1 - s)
                                dve.tensor_tensor(tmp[:, :, to:to + 16], xn[p][:, :, of:of + 16],
                                                  cs[p][:, 1:2, to:to + 16].to_broadcast([P, NH, 16]), ALU.mult).then_inc(dve_seq, 1)
                                link.n += 1
                        dve.wait_ge(dve_seq, link.n)
                        link(dve.tensor_tensor(xn[p][:, :, :], xn[p][:, :, :], cs[p][:, 0:1, :].to_broadcast([P, NH, HD]), ALU.mult))
                        dve.tensor_tensor(xn[p][:, :, :], xn[p][:, :, :], tmp[:, :, :], ALU.add).then_inc(roped, 1)
                        dve.wait_ge(roped, p + 1)
                    for p in range(2):
                        dve.wait_ge(trans, 4 + 2 * p + 1)
                        dve.tensor_copy(tb[:, 8:12, p * P:(p + 1) * P], pt[4 * p + 2][:, :].rearrange("p (b t) -> p b t", t=P)).then_inc(evac_v, 1)
                        dve.wait_ge(trans, 4 + 2 * p + 2)
                        dve.tensor_copy(tb[:, 12, p * P:(p + 1) * P], pt[4 * p + 3][:, 0:P]).then_inc(evac_v, 1)
            st.clear()


def attention_stage(nc, name, ident, loops, K, nk, units, loads, NLOAD, kv_shared, o_out, window=None, causal=None):
    SMAX = max(sum(n for _, n in u["keys"]) for u in units)
    NB = (SMAX + 511) // 512
    NQ = max(u["q"] for u in units) + P
    NT = (SMAX + P - 1) // P
    with Stage(nc, name) as st:
        qT = [st.sb(f"qT{s}", [K, NQ]) for s in range(2)]
        kT = [st.sb(f"kT{s}", [K, nk]) for s in range(1 if kv_shared else 2)]
        v = [st.sb(f"v{s}", [P, nk // P, HD]) for s in range(1 if kv_shared else 2)]
        prob = [st.sb(f"prob{s}", [P, SMAX]) for s in range(2)]
        probT = [st.sb(f"probT{s}", [P, NT, P]) for s in range(2)]
        mx = st.sb("mx", [P, 2])
        den = st.sb("den", [P, 2])
        rden = st.sb("rden", [P, 2])
        o = st.sb("o", [P, len(units), 2, HD])
        scores = st.ps("scores", [P, 512 * NB])
        pt = [st.ps(f"pt{i}") for i in range(3)]
        po = [st.ps(f"po{i}") for i in range(2)]
        bufs = dict(qT=qT, kT=kT, v=v)
        if window is not None:
            table = [st.sb(f"table{s}", [P, 18 * HD]) for s in range(2)]
            bias = [st.sb(f"bias{s}", [P, 5, 640]) for s in range(2)]
            mask = st.sb("mask", [P, 5, 640])
            biased = [st.sb(f"biased{s}", [P, SMAX]) for s in range(2)]
            bufs["table"] = table
        if causal is not None:
            mask = st.sb("mask", [P, P])
        const_in = st.sem("const_in")
        loaded = [st.sem(f"loaded{s}") for s in range(2)]
        scored, maxed, probs, trans, turned, summed, normed, stored, dve_seq, bias_ready = (st.sem(n) for n in (
            "scored", "maxed", "probs", "trans", "turned", "summed", "normed", "stored", "dve_seq", "bias_ready"))
        work = [(s, x) for s in range(2) for x in range(len(units))]
        groups = []
        for s, x in work:
            tl = units[x]["tiles"]
            groups.append([list(range(g, min(g + 4, len(tl)))) for g in range(0, len(tl), 4)])
        first = [0]
        for g in groups:
            first.append(first[-1] + len(g))
        if window is not None or causal is not None:
            with nc.Block() as block:
                @block.sync
                def _(sp):
                    if window is not None:
                        sp.dma_start(mask[:, :, :], window.rearrange("c p k -> p c k")).then_inc(const_in, 16)
                    else:
                        sp.dma_start(mask[:, :], causal).then_inc(const_in, 16)
                    sp.wait_ge(const_in, 16)
        loop = ExitStack()
        idx = []
        for n in loops:
            idx.append(loop.enter_context(nc.Fori(0, n)))
        with loop:
            with nc.Block() as block:
                @block.sync
                def _(sp):
                    loads(sp, idx, bufs, loaded)
                    sp.wait_ge(normed, len(work))
                    o_out(sp, idx, o, stored)

                if window is not None:
                    @block.gpsimd
                    def _(pool):
                        for s in range(2):
                            pool.wait_ge(loaded[s], NLOAD[s])
                            for c, off in enumerate((8, 6, 4, 2, 0)):
                                pool.tensor_tensor(bias[s][:, c, :], table[s][:, off * HD:off * HD + 640], mask[:, c, :], ALU.add).then_inc(bias_ready, 1)

                @block.tensor
                def _(pe):
                    def score(w):
                        s, x = work[w]
                        u = units[x]
                        ks = 0 if kv_shared else s
                        pe.wait_ge(loaded[s], NLOAD[s])
                        if kv_shared:
                            pe.wait_ge(loaded[0], NLOAD[0])
                        if w:
                            biased_before = window is not None and units[work[w - 1][1]]["bias"] is not None
                            pe.wait_ge(maxed if biased_before else probs, w)
                        at = 0
                        for c0, n in u["keys"]:
                            while n:
                                m = min(n, 512 - at % 512)
                                mm = pe.matmul(scores[:, at:at + m], qT[s][:, u["q"]:u["q"] + P], kT[ks][:, c0:c0 + m], start=True, stop=True)
                                at, c0, n = at + m, c0 + m, n - m
                        mm.then_inc(scored, 1)

                    def mix(w):
                        s, x = work[w]
                        u = units[x]
                        ks = 0 if kv_shared else s
                        pe.wait_ge(probs, w + 1)
                        if w >= 2:
                            pe.wait_ge(normed, w - 1)
                        for g, tl in enumerate(groups[w]):
                            n = first[w] + g
                            if n >= 3:
                                pe.wait_ge(turned, n - 2)
                            for a, t in enumerate(tl):
                                mm = pe.transpose(pt[n % 3][:, a * P:(a + 1) * P], prob[w % 2][:, t * P:(t + 1) * P], ident[:, :])
                            mm.then_inc(trans, 1)
                        for g, tl in enumerate(groups[w]):
                            pe.wait_ge(turned, first[w] + g + 1)
                            for t in tl:
                                mm = pe.matmul(po[w % 2][:, 0:HD], probT[w % 2][:, t, :], v[ks][:, u["tiles"][t], :],
                                               start=(t == 0), stop=(t == len(u["tiles"]) - 1))
                        mm.then_inc(summed, 1)

                    for w in range(len(work) + 1):
                        if w < len(work):
                            score(w)
                        if w:
                            mix(w - 1)

                @block.scalar
                def _(act):
                    def softmax(w):
                        s, x = work[w]
                        n = sum(m for _, m in units[x]["keys"])
                        act.wait_ge(maxed, w + 1)
                        if w >= 2:
                            act.wait_ge(trans, first[w - 1])
                            act.wait_ge(normed, w - 1)
                        src = biased[w % 2] if window is not None and units[x]["bias"] is not None else scores
                        nc.scalar.activation(prob[w % 2][:, 0:n], src[:, 0:n], ACT.Exp, bias=mx[:, w % 2:w % 2 + 1],
                                             accum_out=den[:, w % 2:w % 2 + 1]).then_inc(probs, 1)

                    def turn(w):
                        if w >= 2:
                            act.wait_ge(summed, w - 1)
                        for g, tl in enumerate(groups[w]):
                            n = first[w] + g
                            act.wait_ge(trans, n + 1)
                            nc.scalar.copy(probT[w % 2][:, tl[0]:tl[-1] + 1, :],
                                           pt[n % 3][:, 0:len(tl) * P].rearrange("p (b t) -> p b t", t=P)).then_inc(turned, 1)

                    for w in range(len(work) + 1):
                        if w:
                            turn(w - 1)
                        if w < len(work):
                            softmax(w)

                @block.vector
                def _(dve):
                    link = Linked(dve, dve_seq)

                    def maximum(w):
                        s, x = work[w]
                        u = units[x]
                        n = sum(m for _, m in u["keys"])
                        dve.wait_ge(scored, w + 1)
                        src = scores
                        if window is not None and u["bias"] is not None:
                            if w >= 2:
                                dve.wait_ge(probs, w - 1)
                            dve.wait_ge(bias_ready, 5 * (s + 1))
                            src = biased[w % 2]
                            dve.tensor_tensor(src[:, 0:640], scores[:, 0:640], bias[s][:, u["bias"], :], ALU.add).then_inc(dve_seq, 1)
                            link.n += 1
                            link(dve.tensor_copy(src[:, 640:n], scores[:, 640:n]))
                        if causal is not None:
                            link(dve.tensor_tensor(scores[:, n - P:n], scores[:, n - P:n], mask[:, :], ALU.add))
                        if w >= 2:
                            dve.wait_ge(probs, w - 1)
                        link(dve.tensor_reduce(mx[:, w % 2:w % 2 + 1], src[:, 0:n], AX.X, ALU.max))
                        dve.tensor_scalar(mx[:, w % 2:w % 2 + 1], mx[:, w % 2:w % 2 + 1], -1.0, None, ALU.mult).then_inc(maxed, 1)

                    def normalize(w):
                        s, x = work[w]
                        dve.wait_ge(probs, w + 1)
                        link(dve.reciprocal(rden[:, w % 2:w % 2 + 1], den[:, w % 2:w % 2 + 1]))
                        dve.wait_ge(summed, w + 1)
                        dve.tensor_scalar(o[:, x, s, :], po[w % 2][:, 0:HD], rden[:, w % 2:w % 2 + 1], None, ALU.mult).then_inc(normed, 1)

                    for w in range(len(work) + 1):
                        if w < len(work):
                            maximum(w)
                        if w:
                            normalize(w - 1)
            st.clear()


PADR = 19


def window_table_stage(nc, ap, REP):
    with Stage(nc, "pad") as st:
        pad = st.sb("pad", [HEADS, PADR, P])
        zeroed, filled, stored = (st.sem(n) for n in ("zeroed", "filled", "stored"))
        with nc.Block() as block:
            @block.vector
            def _(dve):
                dve.memset(pad[:, :, :], 0.0).then_inc(zeroed, 1)

            @block.sync
            def _(sp):
                sp.wait_ge(zeroed, 1)
                sp.dma_start(pad[:, 2:17, 48:79], ap["na_rpb"][0]).then_inc(filled, 16)
                sp.wait_ge(filled, 16)
                for r in range(PADR):
                    sp.dma_start(REP[:, r], pad[:, r:r + 1, :].to_broadcast([HEADS, HD, P])).then_inc(stored, 16)
                sp.wait_ge(stored, 16 * PADR)


def na_stage(nc, ap, ident, U, QT, REP, O):
    start = [min(max(i - 2, 0), 3) for i in range(LT)]
    kind = [{8: 0, 6: 1, 4: 2, 2: 3, 0: 4}[2 * s - 2 * i + 8] for i, s in enumerate(start)]
    units = [dict(q=i * P, keys=[(s * P, 640), (LAT, CTX)], tiles=[s + a for a in range(5)] + [8, 9], bias=k)
             for i, (s, k) in enumerate(zip(start, kind))]
    units += [dict(q=LAT + i * P, keys=[(LAT, CTX)], tiles=[8, 9], bias=None) for i in range(CT)]
    qv = QT[0:HW, :].rearrange("(j s d) t -> j s d t", s=2, d=HD)
    kv = QT[HW:2 * HW, :].rearrange("(j s d) t -> j s d t", s=2, d=HD)
    vv = U[:, 1024:1536].rearrange("(m p) (j s d) -> j s p m d", p=P, s=2, d=HD)
    tables = [bass.AP(tensor=REP.tensor, offset=(1 - r) * HD * P + HD - 1,
                      ap=[[2 * PADR * HD * P, 4], [PADR * HD * P, 2], [P - 1, HD], [HD * P, 18], [1, HD]]) for r in range(2)]

    def loads(sp, idx, b, loaded):
        (j,) = idx
        for s in range(2):
            sp.dma_start(b["qT"][s][:, :], qv[j, s]).then_inc(loaded[s], 16)
            sp.dma_start(b["kT"][s][:, :], kv[j, s]).then_inc(loaded[s], 16)
            sp.dma_start(b["v"][s][:, :, :], vv[j, s]).then_inc(loaded[s], 16)
            for r in range(2):
                sp.dma_start(b["table"][s][HD * r:HD * (r + 1), :].rearrange("p (j k) -> p j k", k=HD), tables[r][j, s]).then_inc(loaded[s], 16)

    ov = O[:, 0:HW].rearrange("(x p) (j s d) -> j p x s d", p=P, s=2, d=HD)

    def out(sp, idx, o, stored):
        (j,) = idx
        sp.dma_start(ov[j], o[:, :, :, :]).then_inc(stored, 16)
        sp.wait_ge(stored, 16)

    attention_stage(nc, "na", ident, [4], HD, TOK, units, loads, [80, 80], False, out, window=ap["window_mask"])


def gqa_stage(nc, ap, ident, U, QT, O):
    units = [dict(q=i * P, keys=[(0, TOK)], tiles=list(range(10)), bias=None) for i in range(LT)]
    units += [dict(q=LAT + i * P, keys=[(LAT, CTX)], tiles=[8, 9], bias=None) for i in range(CT)]
    qv = QT[2 * HW:3 * HW, :].rearrange("(g j s d) t -> g j s d t", j=2, s=2, d=HD)
    kv = QT[3 * HW:3 * HW + 2 * HD, :].rearrange("(g d) t -> g d t", d=HD)
    vv = U[:, 2688:2816].rearrange("(m p) (g d) -> g p m d", p=P, d=HD)

    def loads(sp, idx, b, loaded):
        g, j = idx
        sp.dma_start(b["kT"][0][:, :], kv[g]).then_inc(loaded[0], 16)
        sp.dma_start(b["v"][0][:, :, :], vv[g]).then_inc(loaded[0], 16)
        for s in range(2):
            sp.dma_start(b["qT"][s][:, :], qv[g, j, s]).then_inc(loaded[s], 16)

    ov = O[:, HW:2 * HW].rearrange("(x p) (g j s d) -> g j p x s d", p=P, j=2, s=2, d=HD)

    def out(sp, idx, o, stored):
        g, j = idx
        sp.dma_start(ov[g, j], o[:, :, :, :]).then_inc(stored, 16)
        sp.wait_ge(stored, 16)

    attention_stage(nc, "gqa", ident, [2, 2], HD, TOK, units, loads, [48, 16], True, out)


def rope_table():
    t = np.arange(LAT)
    pos = np.stack([t // 64, t % 64], -1).astype(np.float32)
    inv = (np.float32(10000.0) ** (-np.arange(16, dtype=np.float32) / np.float32(16))).astype(np.float32)
    ang = (pos[:, :, None] * inv).astype(np.float32)
    c, s = np.cos(ang), np.sin(ang)
    out = np.zeros((TOK, 2, 2, 2, 16), np.float32)
    out[:, 0] = 1.0
    out[:LAT, 0] = c[:, :, None, :]
    out[:LAT, 1, :, 0], out[:LAT, 1, :, 1] = -s, s
    return out.reshape(TOK, 2, HD)


def window_mask():
    out = np.full((5, P, 640), -1e30, np.float32)
    for k, i in enumerate((0, 1, 3, 6, 7)):
        s = min(max(i - 2, 0), 3)
        for p in range(P):
            qr, qc = 2 * i + p // 64, p % 64
            r0, c0 = min(max(qr - 4, 0), 8), min(max(qc - 8, 0), 48)
            for r in range(10):
                if r0 <= 2 * s + r < r0 + 8:
                    out[k, p, 64 * r + c0:64 * r + c0 + 16] = 0.0
    return out


def gated_stage(nc, name, ident, tiles, xT, o_of, gates_of):
    with Stage(nc, name) as st:
        o = [st.sb(f"o{p}", [P, D]) for p in range(2)]
        g = [st.sb(f"g{p}", [P, D]) for p in range(2)]
        pt = [st.ps(f"pt{i}") for i in range(4)]
        loaded = [st.sem(f"loaded{p}") for p in range(2)]
        silu, gated, trans, evac = (st.sem(n) for n in ("silu", "gated", "trans", "evac"))
        with nc.Fori(*tiles) as i:
            with nc.Block() as block:
                @block.sync
                def _(sp):
                    for p in range(2):
                        sp.dma_start(g[p][:, 0:HW], gates_of(0)(i, p)).then_inc(loaded[p], 16)
                        sp.dma_start(g[p][:, HW:D], gates_of(1)(i, p)).then_inc(loaded[p], 16)
                        sp.dma_start(o[p][:, :], o_of(i, p)).then_inc(loaded[p], 16)

                @block.scalar
                def _(act):
                    for p in range(2):
                        act.wait_ge(loaded[p], 48)
                        nc.scalar.activation(g[p][:, :], g[p][:, :], ACT.Silu).then_inc(silu, 1)
                    for p in range(2):
                        act.wait_ge(trans, 2 * p + 1)
                        nc.scalar.copy(xT[:, 0:4, bass.ds(i * 2 * P + p * P, P)],
                                       pt[2 * p][:, :].rearrange("p (b t) -> p b t", t=P)).then_inc(evac, 1)

                @block.vector
                def _(dve):
                    for p in range(2):
                        dve.wait_ge(silu, p + 1)
                        dve.wait_ge(loaded[p], 48)
                        dve.tensor_tensor(o[p][:, :], o[p][:, :], g[p][:, :], ALU.mult).then_inc(gated, 1)
                    for p in range(2):
                        dve.wait_ge(trans, 2 * p + 2)
                        dve.tensor_copy(xT[:, 4:8, bass.ds(i * 2 * P + p * P, P)],
                                        pt[2 * p + 1][:, :].rearrange("p (b t) -> p b t", t=P)).then_inc(evac, 1)

                @block.tensor
                def _(pe):
                    for p in range(2):
                        pe.wait_ge(gated, p + 1)
                        for b in range(2):
                            for k in range(4):
                                mm = pe.transpose(pt[2 * p + b][:, k * P:(k + 1) * P], o[p][:, (4 * b + k) * P:(4 * b + k + 1) * P], ident[:, :])
                            mm.then_inc(trans, 1)
            st.clear()


LAT0, CTX0, PAD_ROWS = 1, LAT + 2, (0, LAT + 1, LAT + CTX + 2)
U2_ROWS = LAT + CTX + 3
RW = 1664
NF = 9
C = 64
NCH = TOK // C
CCH = CTX // C


def zero_rows_stage(nc, U2):
    with Stage(nc, "zero") as st:
        z = st.sb("z", [1, REC_IN])
        zeroed, stored = st.sem("zeroed"), st.sem("stored")
        with nc.Block() as block:
            @block.vector
            def _(dve):
                dve.memset(z[:, :], 0.0).then_inc(zeroed, 1)

            @block.sync
            def _(sp):
                sp.wait_ge(zeroed, 1)
                for r in PAD_ROWS:
                    sp.dma_start(U2[r:r + 1, :], z[:, :]).then_inc(stored, 16)
                sp.wait_ge(stored, 48)


def rwkv_feature_stage(nc, ap, ident, U2, FE, segments):
    with Stage(nc, "feat") as st:
        u = [st.sb(f"u{a}", [P, RW]) for a in range(3)]
        s = st.sb("s", [P, RW])
        mu = st.sb("mu", [P, RW])
        lora = st.sb("lora", [P, P])
        loraT = st.sb("loraT", [P, P])
        wup = st.sb("wup", [P, 4, HW])
        w0 = st.sb("w0", [P, 4, HW])
        kk_row = st.sb("kk_row", [P, HW])
        ka_row = st.sb("ka_row", [P, HW])
        z = st.sb("z", [P, 4, HW])
        f = st.sb("f", [P, NF, HW])
        sq = st.sb("sq", [P, HW])
        ss = st.sb("ss", [P, HEADS])
        pt = st.ps("pt")
        pz = [st.ps(f"pz{m}") for m in range(4)]
        names = ("const_in", "zeroed", "loaded", "shifted", "tanh", "trans", "turned", "lora_mm", "biased", "gates",
                 "sq_in", "sq_out", "ms_ready", "rt_ready", "done", "stored", "dve_seq")
        (const_in, zeroed, loaded, shifted, tanh, trans, turned, lora_mm, biased, gates,
         sq_in, sq_out, ms_ready, rt_ready, done, stored, dve_seq) = (st.sem(n) for n in names)
        with nc.Block() as block:
            @block.vector
            def _(dve):
                dve.memset(wup[:, :, :], 0.0).then_inc(zeroed, 1)

            @block.sync
            def _(sp):
                sp.dma_start(mu[:, :], ap["rwkv_mu"][0].partition_broadcast(P)).then_inc(const_in, 16)
                sp.dma_start(kk_row[:, :], ap["rwkv_k_k"][0].partition_broadcast(P)).then_inc(const_in, 16)
                sp.dma_start(ka_row[:, :], ap["rwkv_k_a"][0].partition_broadcast(P)).then_inc(const_in, 16)
                sp.wait_ge(zeroed, 1)
                for d in range(2):
                    for q, (wn, bn) in enumerate((("rwkv_w_up", "rwkv_w0"), ("rwkv_a_up", "rwkv_a0"))):
                        m = 2 * q + d
                        sp.dma_start(wup[32 * m:32 * m + 32, m, :], ap[wn][0, d]).then_inc(const_in, 16)
                        sp.dma_start(w0[:, m, :], ap[bn][0, d].partition_broadcast(P)).then_inc(const_in, 16)
                sp.wait_ge(const_in, 16 * 11)
        st.clear()
        for tiles, row0, out0 in segments:
            with nc.Fori(0, tiles) as i:
                with nc.Block() as block:
                    @block.sync
                    def _(sp):
                        for a in range(3):
                            src = U2[row0 + a - 1:row0 + a - 1 + tiles * P, 0:RW].rearrange("(n p) d -> n p d", p=P)
                            sp.dma_start(u[a][:, :], src[i]).then_inc(loaded, 16)
                        sp.wait_ge(done, 1)
                        dst = FE[out0:out0 + tiles * P, :, :].rearrange("(n p) f d -> n p f d", p=P)
                        sp.dma_start(dst[i], f[:, :, :]).then_inc(stored, 16)
                        sp.wait_ge(stored, 16)

                    @block.scalar
                    def _(act):
                        act.wait_ge(shifted, 1)
                        nc.scalar.activation(lora[:, 0:64], s[:, 1536:1600], ACT.Tanh)
                        nc.scalar.copy(lora[:, 64:128], s[:, 1600:1664]).then_inc(tanh, 1)
                        act.wait_ge(trans, 1)
                        nc.scalar.copy(loraT[:, :], pt[:, 0:P]).then_inc(turned, 1)
                        nc.scalar.copy(f[:, 0, :], s[:, 0:512])
                        nc.scalar.copy(f[:, 1, :], s[:, 1024:1536])
                        act.wait_ge(sq_in, 1)
                        nc.scalar.activation(sq[:, :], f[:, 2, :], ACT.Square).then_inc(sq_out, 1)
                        act.wait_ge(ms_ready, 1)
                        nc.scalar.activation(ss[:, :], ss[:, :], ACT.Sqrt).then_inc(rt_ready, 1)
                        act.wait_ge(biased, 1)
                        nc.scalar.activation(z[:, :, :], z[:, :, :], ACT.Sigmoid).then_inc(gates, 1)

                    @block.tensor
                    def _(pe):
                        pe.wait_ge(tanh, 1)
                        pe.transpose(pt[:, 0:P], lora[:, :], ident[:, :]).then_inc(trans, 1)
                        pe.wait_ge(turned, 1)
                        for m in range(4):
                            mm = pe.matmul(pz[m][:, :], loraT[:, :], wup[:, m, :], start=True, stop=True)
                        mm.then_inc(lora_mm, 1)

                    @block.vector
                    def _(dve):
                        link = Linked(dve, dve_seq)
                        dve.wait_ge(loaded, 48)
                        link(dve.tensor_tensor(s[:, :], u[0][:, :], u[2][:, :], ALU.add))
                        link(dve.scalar_tensor_tensor(out=s[:, :], in0=s[:, :], scalar=0.5, in1=u[1][:, :], op0=ALU.mult, op1=ALU.subtract))
                        link(dve.tensor_tensor(s[:, :], s[:, :], mu[:, :], ALU.mult))
                        dve.tensor_tensor(s[:, :], s[:, :], u[1][:, :], ALU.add).then_inc(shifted, 1)
                        dve.wait_ge(shifted, 1)
                        k = s[:, 512:1024]
                        dve.tensor_tensor(f[:, 2, :], k, kk_row[:, :], ALU.mult).then_inc(sq_in, 1)
                        dve.wait_ge(lora_mm, 1)
                        for m in range(4):
                            ins = dve.tensor_tensor(z[:, m, :], pz[m][:, :], w0[:, m, :], ALU.add)
                        ins.then_inc(biased, 1)
                        dve.wait_ge(sq_out, 1)
                        link(dve.tensor_reduce(ss[:, :], sq[:, :].rearrange("p (h d) -> p h d", d=HD), AX.X, ALU.add))
                        dve.tensor_scalar(ss[:, :], ss[:, :], 1e-12, None, ALU.add).then_inc(ms_ready, 1)
                        dve.wait_ge(rt_ready, 1)
                        link(dve.reciprocal(ss[:, :], ss[:, :]))
                        kk = f[:, 2, :].rearrange("p (h d) -> p h d", d=HD)
                        link(dve.tensor_tensor(kk, kk, ss[:, :].unsqueeze(2).to_broadcast([P, HEADS, HD]), ALU.mult))
                        dve.wait_ge(gates, 1)
                        for d in range(2):
                            dve.tensor_scalar(f[:, 3 + 3 * d, :], z[:, d, :], -float(np.exp(-0.5)), None, ALU.mult)
                            link(dve.tensor_tensor(f[:, 5 + 3 * d, :], f[:, 2, :], z[:, 2 + d, :], ALU.mult))
                            link(dve.scalar_tensor_tensor(out=z[:, 2 + d, :], in0=z[:, 2 + d, :], scalar=-1.0, in1=ka_row[:, :], op0=ALU.add, op1=ALU.mult))
                            link(dve.scalar_tensor_tensor(out=f[:, 4 + 3 * d, :], in0=z[:, 2 + d, :], scalar=1.0, in1=k, op0=ALU.add, op1=ALU.mult))
                        dve.sem_inc(done, 1)
                st.clear()


def rwkv_scan_stage(nc, ap, ident, FE, Y):
    W = HEADS * C
    LEV = 6
    with Stage(nc, "scan") as st:
        tri = st.sb("tri", [C, 4, C])
        lev = st.sb("lev", [C, 2, LEV, C])
        lev0 = st.sb("lev0", [C, 2, C])
        keep = st.sb("keep", [C, 2, 2, C])
        ones = st.sb("ones", [C, 1])
        S = [st.sb(f"S{d}", [C, W]) for d in range(2)]
        F = [st.sb(f"F{d}", [C, 6, W]) for d in range(2)]
        ex = [st.sb(f"ex{d}", [C, 3, W]) for d in range(2)]
        eT = [st.sb(f"eT{d}", [C, HEADS]) for d in range(2)]
        q4 = [st.sb(f"q4{d}", [C, 4, W]) for d in range(2)]
        AR = [st.sb(f"AR{d}", [C, HEADS, 2, C]) for d in range(2)]
        KB = [st.sb(f"KB{d}", [C, 2, W]) for d in range(2)]
        GB = [st.sb(f"GB{d}", [C, HEADS, 2, C]) for d in range(2)]
        GK = [st.sb(f"GK{d}", [C, HEADS, 2, C]) for d in range(2)]
        X = [st.sb(f"X{d}", [C, LEV, W]) for d in range(2)]
        T = [st.sb(f"T{d}", [C, W]) for d in range(2)]
        TT = [st.sb(f"TT{d}", [C, W]) for d in range(2)]
        Pm = [st.sb(f"Pm{d}", [C, W]) for d in range(2)]
        Wm = [st.sb(f"Wm{d}", [C, W]) for d in range(2)]
        Un = [st.sb(f"Un{d}", [C, W]) for d in range(2)]
        Yo = [st.sb(f"Yo{d}", [C, W]) for d in range(2)]
        bank = [[st.ps(f"bank{d}{b}", (C, 512)) for b in range(4)] for d in range(2)]
        const_in, cleared = st.sem("const_in"), st.sem("cleared")
        e = [{n: st.sem(f"{n}{d}") for n in (
            "loaded", "sums", "exps", "scaled", "turned", "turned_a", "turned_v", "grams", "masked", "levels", "mb", "t0",
            "p_mm", "p_out", "dt_mm", "dt_out", "w_mm", "w_out", "u_mm", "u_out", "ys_mm", "y_out", "stored", "seq")} for d in range(2)]
        with nc.Block() as block:
            @block.sync
            def _(sp):
                sp.dma_start(tri[:, :, :], ap["tri"]).then_inc(const_in, 16)
                sp.dma_start(lev[:, :, :, :], ap["lev"]).then_inc(const_in, 16)
                sp.dma_start(lev0[:, :, :], ap["lev0"]).then_inc(const_in, 16)
                sp.dma_start(keep[:, :, :, :], ap["keep"]).then_inc(const_in, 16)
                sp.wait_ge(const_in, 64)

            @block.vector
            def _(dve):
                dve.memset(ones[:, :], 1.0).then_inc(cleared, 1)
                for d in range(2):
                    dve.memset(S[d][:, :], 0.0).then_inc(cleared, 1)
                dve.wait_ge(cleared, 3)
        st.clear()
        FEv = FE.rearrange("(n c) f d -> n c f d", c=C)

        def hc(h):
            return slice(h * C, (h + 1) * C)

        def chunk(i, nb, emit):
            at = (i, nb)
            with nc.Block() as block:
                @block.sync
                def _(sp):
                    for d in range(2):
                        sp.dma_start(F[d][:, 0:3, :], FEv[at[d]][:, 0:3, :]).then_inc(e[d]["loaded"], 16)
                        sp.dma_start(F[d][:, 3:6, :], FEv[at[d]][:, 3 + 3 * d:6 + 3 * d, :]).then_inc(e[d]["loaded"], 16)
                    if emit:
                        for d in range(2):
                            sp.wait_ge(e[d]["y_out"], 1)
                            yv = Y[d].rearrange("(n c) w -> n c w", c=C)
                            sp.dma_start(yv[at[d] - CCH], Yo[d][:, :]).then_inc(e[d]["stored"], 16)
                        for d in range(2):
                            sp.wait_ge(e[d]["stored"], 16)

                @block.tensor
                def _(pe):
                    for d in range(2):
                        s, b = e[d], bank[d]
                        pe.wait_ge(s["loaded"], 32)
                        pe.matmul(b[0][:, :], tri[:, 2 * d, :], F[d][:, 3, :], start=True, stop=True)
                        pe.matmul(b[1][:, :], tri[:, 2 * d + 1, :], F[d][:, 3, :], start=True, stop=True)
                        for h in range(HEADS):
                            mm = pe.matmul(b[2][:, h:h + 1], F[d][:, 3, hc(h)], ones[:, :], start=True, stop=True)
                        mm.then_inc(s["sums"], 1)
                    for d in range(2):
                        s, b = e[d], bank[d]
                        for x, to in ((0, 3), (1, 0), (2, 1), (3, 2)):
                            pe.wait_ge(s["scaled"], x + 1)
                            if x == 1:
                                pe.wait_ge(s["exps"], 4)
                            for h in range(HEADS):
                                mm = pe.transpose(b[to][:, hc(h)], q4[d][:, x, hc(h)], ident[0:C, 0:C])
                            mm.then_inc(s["turned"], 1)
                    for d in range(2):
                        s, b = e[d], bank[d]
                        pe.wait_ge(s["turned_a"], 2)
                        pe.wait_ge(s["turned_v"], 2)
                        for x, base in ((1, 0), (0, 2)):
                            for h in range(HEADS):
                                mm = pe.matmul(b[base + h // 4][:, (h % 4) * 2 * C:(h % 4 + 1) * 2 * C], KB[d][:, x, hc(h)],
                                               AR[d][:, h, :, :].rearrange("p a t -> p (a t)"), start=True, stop=True)
                            mm.then_inc(s["grams"], 1)
                    for d in range(2):
                        s, b = e[d], bank[d]
                        pe.wait_ge(s["masked"], 1)
                        for h in range(HEADS):
                            mm = pe.matmul(b[0][:, hc(h)], AR[d][:, h, 0, :], KB[d][:, 1, hc(h)], start=True, stop=True)
                        mm.then_inc(s["mb"], 1)
                    for l in range(1, LEV):
                        for d in range(2):
                            s, b = e[d], bank[d]
                            pe.wait_ge(s["levels"], l + 2)
                            pe.wait_ge(s["t0"], 1)
                            pe.wait_ge(s["masked"], 4)
                            if l > 1:
                                pe.wait_ge(s["dt_out"], l - 1)
                            for h in range(HEADS):
                                mm = pe.matmul(b[1][:, hc(h)], X[d][:, l, hc(h)], T[d][:, hc(h)], start=True, stop=True)
                            mm.then_inc(s["p_mm"], 1)
                        for d in range(2):
                            s, b = e[d], bank[d]
                            pe.wait_ge(s["p_out"], l)
                            for h in range(HEADS):
                                if l < LEV - 1:
                                    pe.matmul(b[2][:, hc(h)], TT[d][:, hc(h)], Pm[d][:, hc(h)], start=True, stop=True)
                                mm = pe.matmul(b[3][:, hc(h)], Pm[d][:, hc(h)], TT[d][:, hc(h)], start=True, stop=True)
                            mm.then_inc(s["dt_mm"], 1)
                    for d in range(2):
                        s, b = e[d], bank[d]
                        for h in range(HEADS):
                            pe.matmul(b[0][:, hc(h)], AR[d][:, h, 0, :], S[d][:, hc(h)], start=True, stop=False)
                            mm = pe.matmul(b[0][:, hc(h)], GK[d][:, h, 0, :], F[d][:, 1, hc(h)], start=False, stop=True)
                        mm.then_inc(s["w_mm"], 1)
                    for d in range(2):
                        s, b = e[d], bank[d]
                        pe.wait_ge(s["w_out"], 1)
                        pe.wait_ge(s["dt_out"], LEV - 1)
                        for h in range(HEADS):
                            mm = pe.matmul(b[1][:, hc(h)], TT[d][:, hc(h)], Wm[d][:, hc(h)], start=True, stop=True)
                        mm.then_inc(s["u_mm"], 1)
                    for d in range(2):
                        s, b = e[d], bank[d]
                        pe.wait_ge(s["u_out"], 1)
                        if emit:
                            for h in range(HEADS):
                                pe.matmul(b[2][:, hc(h)], AR[d][:, h, 1, :], S[d][:, hc(h)], start=True, stop=False)
                                pe.matmul(b[2][:, hc(h)], GK[d][:, h, 1, :], F[d][:, 1, hc(h)], start=False, stop=False)
                                mm = pe.matmul(b[2][:, hc(h)], GB[d][:, h, 1, :], Un[d][:, hc(h)], start=False, stop=True)
                        for h in range(HEADS):
                            pe.matmul(b[3][:, hc(h)], ident[0:C, 0:C], S[d][:, hc(h)], start=True, stop=False)
                            pe.matmul(b[3][:, hc(h)], q4[d][:, 2, hc(h)], F[d][:, 1, hc(h)], start=False, stop=False)
                            mm = pe.matmul(b[3][:, hc(h)], q4[d][:, 3, hc(h)], Un[d][:, hc(h)], start=False, stop=True)
                        mm.then_inc(s["ys_mm"], 1)

                @block.scalar
                def _(act):
                    for d in range(2):
                        s, b = e[d], bank[d]
                        act.wait_ge(s["sums"], 1)
                        nc.scalar.activation(ex[d][:, 0, :], b[1][:, :], ACT.Exp).then_inc(s["exps"], 1)
                        nc.scalar.activation(ex[d][:, 1, :], b[0][:, :], ACT.Exp).then_inc(s["exps"], 1)
                        nc.scalar.activation(ex[d][:, 2, :], b[0][:, :], ACT.Exp, scale=-1.0).then_inc(s["exps"], 1)
                        nc.scalar.activation(eT[d][:, :], b[2][:, 0:HEADS], ACT.Exp).then_inc(s["exps"], 1)
                    for d in range(2):
                        s, b = e[d], bank[d]
                        for x, of in ((0, 3), (1, 0)):
                            act.wait_ge(s["turned"], x + 1)
                            nc.scalar.copy(AR[d][:, :, x, :], b[of][:, :].rearrange("p (h t) -> p h t", t=C)).then_inc(s["turned_a"], 1)
                    for l in range(1, LEV):
                        for d in range(2):
                            s, b = e[d], bank[d]
                            act.wait_ge(s["p_mm"], l)
                            if l > 1:
                                act.wait_ge(s["dt_mm"], l - 1)
                            nc.scalar.copy(Pm[d][:, :], b[1][:, :]).then_inc(s["p_out"], 1)
                    for d in range(2):
                        s, b = e[d], bank[d]
                        act.wait_ge(s["w_mm"], 1)
                        nc.scalar.copy(Wm[d][:, :], b[0][:, :]).then_inc(s["w_out"], 1)
                    if emit:
                        for d in range(2):
                            s, b = e[d], bank[d]
                            act.wait_ge(s["ys_mm"], 1)
                            nc.scalar.copy(Yo[d][:, :], b[2][:, :]).then_inc(s["y_out"], 1)

                @block.gpsimd
                def _(pool):
                    for d in range(2):
                        s = e[d]
                        pool.wait_ge(s["masked"], 2)
                        for l in range(LEV):
                            pool.tensor_tensor(X[d][:, l, :].rearrange("p (h t) -> p h t", t=C), GB[d][:, :, 0, :],
                                               lev[:, d, l:l + 1, :].to_broadcast([C, HEADS, C]), ALU.mult).then_inc(s["levels"], 1)
                            if l == 0:
                                pool.wait_ge(s["levels"], 1)
                                pool.tensor_tensor(TT[d][:, :].rearrange("p (h t) -> p h t", t=C),
                                                   ident[0:C, 0:C].unsqueeze(1).to_broadcast([C, HEADS, C]),
                                                   X[d][:, 0, :].rearrange("p (h t) -> p h t", t=C), ALU.subtract).then_inc(s["levels"], 1)

                @block.vector
                def _(dve):
                    link = Linked(dve, e[0]["seq"])
                    for d in range(2):
                        s = e[d]
                        dve.wait_ge(s["loaded"], 32)
                        for x, (fld, ee) in enumerate(((2, 0), (0, 1), (4, 2), (5, 2))):
                            dve.wait_ge(s["exps"], ee + 1)
                            dve.tensor_tensor(q4[d][:, x, :], F[d][:, fld, :], ex[d][:, ee, :], ALU.mult).then_inc(s["scaled"], 1)
                    for d in range(2):
                        s, b = e[d], bank[d]
                        for x, of in ((0, 1), (1, 2)):
                            dve.wait_ge(s["turned"], x + 3)
                            dve.tensor_copy(KB[d][:, x, :], b[of][:, :]).then_inc(s["turned_v"], 1)
                    for d in range(2):
                        s, b = e[d], bank[d]
                        for g, dst in ((0, GB), (1, GK)):
                            dve.wait_ge(s["grams"], g + 1)
                            for hh in range(2):
                                dve.tensor_tensor(dst[d][:, 4 * hh:4 * hh + 4, :, :].rearrange("p h a t -> p h (a t)"),
                                                  b[2 * g + hh][:, :].rearrange("p (h x) -> p h x", x=2 * C),
                                                  keep[:, d, :, :].rearrange("p a t -> p (a t)").unsqueeze(1).to_broadcast([C, 4, 2 * C]),
                                                  ALU.mult).then_inc(s["masked"], 1)
                    for d in range(2):
                        s, b = e[d], bank[d]
                        dve.wait_ge(s["mb"], 1)
                        link(dve.tensor_tensor(T[d][:, :].rearrange("p (h t) -> p h t", t=C), b[0][:, :].rearrange("p (h t) -> p h t", t=C),
                                               lev0[:, d:d + 1, :].to_broadcast([C, HEADS, C]), ALU.mult))
                        dve.tensor_tensor(T[d][:, :].rearrange("p (h t) -> p h t", t=C), T[d][:, :].rearrange("p (h t) -> p h t", t=C),
                                          ident[0:C, 0:C].unsqueeze(1).to_broadcast([C, HEADS, C]), ALU.add).then_inc(s["t0"], 1)
                    for l in range(1, LEV):
                        for d in range(2):
                            s, b = e[d], bank[d]
                            dve.wait_ge(s["dt_mm"], l)
                            if l == 1:
                                dve.wait_ge(s["t0"], 1)
                                dve.wait_ge(s["levels"], 2)
                            if l < LEV - 1:
                                dve.tensor_tensor(T[d][:, :], T[d][:, :], b[2][:, :], ALU.subtract)
                            dve.tensor_tensor(TT[d][:, :], TT[d][:, :], b[3][:, :], ALU.subtract).then_inc(s["dt_out"], 1)
                            dve.wait_ge(s["dt_out"], l)
                    for d in range(2):
                        s, b = e[d], bank[d]
                        dve.wait_ge(s["u_mm"], 1)
                        dve.tensor_scalar(Un[d][:, :], b[1][:, :], -1.0, None, ALU.mult).then_inc(s["u_out"], 1)
                    for d in range(2):
                        s, b = e[d], bank[d]
                        dve.wait_ge(s["ys_mm"], 1)
                        link(dve.tensor_tensor(S[d][:, :].rearrange("p (h t) -> p h t", t=C), b[3][:, :].rearrange("p (h t) -> p h t", t=C),
                                               eT[d][:, :].unsqueeze(2).to_broadcast([C, HEADS, C]), ALU.mult))

        with nc.Fori(0, CCH) as i:
            chunk(i, i * -1 + (CCH - 1), False)
            st.clear()
        with nc.Fori(CCH, NCH) as i:
            chunk(i, i * -1 + (NCH - 1 + CCH), True)
            st.clear()


def scan_constants():
    s, t = np.meshgrid(np.arange(C), np.arange(C), indexing="ij")
    f = np.float32
    tri = np.stack([s <= t, s < t, s >= t, s > t], 1).astype(f)
    keep = np.stack([np.stack([s < t, s <= t], 1), np.stack([s > t, s >= t], 1)], 1).astype(f)
    lev = np.zeros((C, 2, 6, C), f)
    for n in range(6):
        b = 1 << n
        same = (s // (2 * b)) == (t // (2 * b))
        lev[:, 0, n] = same & (s // b < t // b)
        lev[:, 1, n] = same & (s // b > t // b)
    lev0 = -np.stack([lev[:, 0, 0].T, lev[:, 1, 0].T], 1)
    return tri, keep, lev, np.ascontiguousarray(lev0)


HY0 = RW + HW
NFREQ = 1024


def rows(dram, pairs=False):
    return dram.rearrange("(n q p) d -> n q p d", q=2, p=P) if pairs else dram.rearrange("(n p) d -> n p d", p=P)


def hyena_conv3_stage(nc, ap, U2, HX):
    W3 = 3 * HW
    with Stage(nc, "conv3") as st:
        u = [[st.sb(f"u{p}{a}", [P, W3]) for a in range(3)] for p in range(2)]
        t = [st.sb(f"t{p}", [P, W3]) for p in range(2)]
        taps = st.sb("taps", [P, 3, W3])
        const_in, stored = st.sem("const_in"), st.sem("stored")
        loaded = [st.sem(f"loaded{p}") for p in range(2)]
        done = [st.sem(f"done{p}") for p in range(2)]
        seq = [st.sem(f"seq{p}") for p in range(2)]
        with nc.Block() as block:
            @block.sync
            def _(sp):
                for a in range(3):
                    sp.dma_start(taps[:, a, :], ap["hy_short"][0, a].partition_broadcast(P)).then_inc(const_in, 16)
                sp.wait_ge(const_in, 48)
        st.clear()
        with nc.Fori(0, LT // 2) as i:
            with nc.Block() as block:
                @block.sync
                def _(sp):
                    for p in range(2):
                        for a in range(3):
                            src = rows(U2[LAT0 + a - 1:LAT0 + a - 1 + LAT, HY0:HY0 + W3], True)
                            sp.dma_start(u[p][a][:, :], src[i, p]).then_inc(loaded[p], 16)
                    for p in range(2):
                        sp.wait_ge(done[p], 1)
                        sp.dma_start(HX.rearrange("a (n q p) d -> n q p a d", q=2, p=P)[i, p],
                                     t[p][:, :].rearrange("p (a d) -> p a d", a=3)).then_inc(stored, 16)
                    sp.wait_ge(stored, 32)

                def conv(eng, p):
                    link = Linked(eng, seq[p])
                    eng.wait_ge(loaded[p], 48)
                    link(eng.tensor_tensor(t[p][:, :], u[p][0][:, :], taps[:, 0, :], ALU.mult))
                    for a in (1, 2):
                        link(eng.tensor_tensor(u[p][a][:, :], u[p][a][:, :], taps[:, a, :], ALU.mult))
                        if a == 1:
                            link(eng.tensor_tensor(t[p][:, :], t[p][:, :], u[p][a][:, :], ALU.add))
                    eng.tensor_tensor(t[p][:, :], t[p][:, :], u[p][2][:, :], ALU.add).then_inc(done[p], 1)

                @block.vector
                def _(dve):
                    conv(dve, 0)

                @block.gpsimd
                def _(pool):
                    conv(pool, 1)
            st.clear()


def hyena_stage(nc, ap, HX, O):
    with Stage(nc, "hy") as st:
        z = st.sb("z", [P, LT, HW])
        with Stage(nc, "hyp") as sr:
            plus = sr.sb("plus", [P, LT, 2 * HW], side="right")
            minus = sr.sb("minus", [P, LT, 2 * HW], side="right")
            rk = sr.sb("rk", [P, 2 * HW], side="right")
            Kn = sr.sb("Kn", [1, 2 * HW], side="right")
            hyena_filters(nc, ap, HX, z, plus, minus, rk, Kn)
            KS = st.sb("KS", [P, 2, 8, HW])
            YS = st.sb("YS", [P, 2, 8, HW])
            hyena_spectra(nc, ap, z, KS, YS, (plus, minus, rk, Kn))
        hyena_inverse(nc, ap, 0, HX, YS, z, None)
        hyena_spectra(nc, ap, z, KS, YS, None)
        hyena_inverse(nc, ap, 1, HX, YS, z, O)


def hyena_filters(nc, ap, HX, z, plus, minus, rk, Kn):
    TWO_PI_HI, TWO_PI_LO = 6.28125, float(2 * np.pi - 6.28125)
    MAGIC = 12582912.0
    with Stage(nc, "hyf") as sf:
        feats = sf.sb("feats", [33, LAT])
        w1 = sf.sb("w1", [33, 64])
        w2 = sf.sb("w2", [64, 64])
        w3 = sf.sb("w3", [64, 4 * HW])
        b12 = sf.sb("b12", [64, 2])
        b3 = sf.sb("b3", [P, 4 * HW])
        hid = sf.sb("hid", [64, LAT])
        turn = sf.sb("turn", [64, LAT])
        win = [sf.sb(f"win{p}", [P, HW]) for p in range(2)]
        taps = sf.sb("taps", [P, 4, HW])
        sq = [sf.sb(f"sq{p}", [P, 4, HW]) for p in range(2)]
        ones = sf.sb("ones", [P, P])
        alt = sf.sb("alt", [P, 1])
        ph = [sf.ps(f"ph{i}") for i in range(2)]
        pk = [sf.ps(f"pk{i}") for i in range(4)]
        pn = [sf.ps(f"pn{i}") for i in range(2)]
        names = ("small_in", "set", "hid_mm", "reduced", "sine", "taps_mm", "taps_out", "squared", "sums", "root", "seq", "z_in", "nyq")
        small_in, set_, hid_mm, reduced, sine, taps_mm, taps_out, squared, sums, root, seq, z_in, nyq = (sf.sem(n) for n in names)
        win_in = [sf.sem(f"win_in{p}") for p in range(2)]
        with nc.Block() as block:
            @block.sync
            def _(sp):
                for to, of in ((feats[:, :], ap["hy_feats"]), (w1[:, :], ap["hy_w1"][0]), (w2[:, :], ap["hy_w2"][0]), (w3[:, :], ap["hy_w3"][0]),
                               (b12[:, 0:1], ap["hy_b1"][0].rearrange("(p o) -> p o", o=1)), (b12[:, 1:2], ap["hy_b2"][0].rearrange("(p o) -> p o", o=1)),
                               (alt[:, :], ap["alternate"]), (b3[:, :], ap["hy_b3"][0].partition_broadcast(P))):
                    sp.dma_start(to, of, allow_slow_non_contiguous=True).then_inc(small_in, 16)
                sp.dma_start(z[:, :, :], HX[0].rearrange("(n p) d -> p n d", p=P)).then_inc(z_in, 16)
                for n in range(LT):
                    if n >= 2:
                        sp.wait_ge(taps_out, n - 1)
                    sp.dma_start(win[n % 2][:, :], rows(ap["hy_window"])[n]).then_inc(win_in[n % 2], 16)
                sp.wait_ge(z_in, 16)

            @block.tensor
            def _(pe):
                pe.wait_ge(small_in, 128)
                pe.wait_ge(set_, 1)
                for lay, (w, src) in enumerate(((w1, feats), (w2, hid))):
                    for h in range(2):
                        if lay:
                            pe.wait_ge(sine, 2)
                        mm = pe.matmul(ph[h][0:64, :], w[:, :], src[:, h * 512:(h + 1) * 512], start=True, stop=True)
                        mm.then_inc(hid_mm, 1)
                pe.wait_ge(sine, 4)

                def sum_squares(n):
                    pe.wait_ge(squared, n + 1)
                    for a in range(4):
                        pe.matmul(pn[a % 2][:, :], ones[:, :], sq[n % 2][:, a, :], start=(n == 0 and a < 2), stop=(n == LT - 1 and a >= 2)).then_inc(sums, 1)

                for n in range(LT):
                    if n:
                        pe.wait_ge(taps_out, n)
                    for a in range(4):
                        mm = pe.matmul(pk[a][:, :], hid[:, n * P:(n + 1) * P], w3[:, a * 512:(a + 1) * 512], start=True, stop=True)
                    mm.then_inc(taps_mm, 1)
                    if n:
                        sum_squares(n - 1)
                sum_squares(LT - 1)
                pe.wait_ge(taps_out, LT)
                pe.wait_ge(root, 2)
                for o in range(2):
                    for n in range(LT):
                        mm = pe.matmul(ph[o][0:1, :], alt[:, :], plus[:, n, o * 512:(o + 1) * 512], start=(n == 0), stop=(n == LT - 1))
                    mm.then_inc(nyq, 1)

            @block.scalar
            def _(act):
                act.wait_ge(small_in, 128)
                for lay in range(2):
                    for h in range(2):
                        act.wait_ge(reduced, 2 * lay + h + 1)
                        nc.scalar.activation(hid[:, h * 512:(h + 1) * 512], hid[:, h * 512:(h + 1) * 512], ACT.Sin).then_inc(sine, 1)
                for n in range(LT):
                    act.wait_ge(taps_out, n + 1)
                    if n >= 2:
                        act.wait_ge(sums, 4 * (n - 1))
                    for a in range(2):
                        half = slice(a * 512, (a + 1) * 512)
                        nc.scalar.activation(sq[n % 2][:, a, :], plus[:, n, half], ACT.Square)
                        ins = nc.scalar.activation(sq[n % 2][:, 2 + a, :], minus[:, n, half], ACT.Square)
                    ins.then_inc(squared, 1)
                act.wait_ge(sums, 4 * LT)
                for a in range(2):
                    nc.scalar.activation(rk[:, a * 512:(a + 1) * 512], pn[a][:, :], ACT.Sqrt, scale=0.5).then_inc(root, 1)

            @block.vector
            def _(dve):
                link = Linked(dve, seq)
                dve.memset(ones[:, :], 1.0).then_inc(set_, 1)
                dve.wait_ge(small_in, 128)
                for lay in range(2):
                    for h in range(2):
                        dve.wait_ge(hid_mm, 2 * lay + h + 1)
                        c = slice(h * 512, (h + 1) * 512)
                        x, n = hid[:, c], turn[:, c]
                        if lay:
                            dve.wait_ge(hid_mm, 4)
                        link(dve.tensor_scalar(x, ph[h][0:64, :], b12[:, lay:lay + 1], None, ALU.add))
                        link(dve.tensor_scalar(n, x, float(1 / (2 * np.pi)), MAGIC, ALU.mult, ALU.add))
                        link(dve.tensor_scalar(n, n, MAGIC, None, ALU.subtract))
                        link(dve.scalar_tensor_tensor(out=x, in0=n, scalar=-TWO_PI_HI, in1=x, op0=ALU.mult, op1=ALU.add))
                        link(dve.scalar_tensor_tensor(out=x, in0=n, scalar=-TWO_PI_LO, in1=x, op0=ALU.mult, op1=ALU.add))
                        dve.tensor_scalar(x, x, 3.1415925, -3.1415925, ALU.min, ALU.max).then_inc(reduced, 1)
                for n in range(LT):
                    dve.wait_ge(taps_mm, n + 1)
                    dve.wait_ge(win_in[n % 2], 16 * (n // 2 + 1))
                    for a in range(4):
                        link(dve.tensor_tensor(taps[:, a, :], pk[a][:, :], b3[:, a * 512:(a + 1) * 512], ALU.add))
                    link(dve.tensor_tensor(taps[:, :, :], taps[:, :, :], win[n % 2][:, :].unsqueeze(1).to_broadcast([P, 4, HW]), ALU.mult))
                    if n == 0:
                        link(dve.tensor_tensor(taps[0:1, 0:2, :], taps[0:1, 0:2, :], taps[0:1, 2:4, :], ALU.add))
                        link(dve.memset(taps[0:1, 2:4, :], 0.0))
                    f = taps[:, 0:2, :].rearrange("p a d -> p (a d)")
                    b = taps[:, 2:4, :].rearrange("p a d -> p (a d)")
                    dve.tensor_tensor(plus[:, n, :], f, b, ALU.add).then_inc(seq, 1)
                    link.n += 1
                    dve.tensor_tensor(minus[:, n, :], f, b, ALU.subtract).then_inc(taps_out, 1)
                    dve.wait_ge(taps_out, n + 1)
                    dve.wait_ge(seq, link.n)
                dve.wait_ge(root, 2)
                link(dve.reciprocal(rk[:, :], rk[:, :]))
                for o in range(2):
                    dve.wait_ge(nyq, o + 1)
                    link(dve.tensor_tensor(Kn[0:1, o * 512:(o + 1) * 512], ph[o][0:1, :], rk[0:1, o * 512:(o + 1) * 512], ALU.mult))


def hyena_spectra(nc, ap, z, KS, YS, filters):
    if filters:
        plus, minus, rk, Kn = filters
    with Stage(nc, "hys" + ("1" if filters else "2")) as ss:
        Fm = [ss.sb(f"F{b}", [P, 8, 2, P]) for b in range(2)]
        zs = [ss.sb(f"zs{b}", [P, 2, HW]) for b in range(2)]
        ks = ss.sb("ks", [P, 2, HW])
        tmp = ss.sb("tmp", [P, 2, HW])
        bank = [ss.ps(f"bank{i}") for i in range(6)]
        f_in = [ss.sem(f"f_in{b}") for b in range(2)]
        k_mm, k_out, z_mm, z_out, seq = (ss.sem(n) for n in ("k_mm", "k_out", "z_mm", "z_out", "seq"))

        def products(dve, link, j, b, k_of, first):
            link(dve.tensor_tensor(tmp[:, 0, :], zs[b][:, 0, :], k_of(0), ALU.mult))
            link(dve.tensor_tensor(tmp[:, 1, :], zs[b][:, 1, :], k_of(1), ALU.mult))
            to = YS[:, :, bass.ds(j, 1), :]
            link(dve.tensor_tensor(to[:, 0], tmp[:, 0:1, :], tmp[:, 1:2, :], ALU.subtract))
            if first:
                link(dve.tensor_copy(YS[0:1, 0, 0, :], tmp[0:1, 0, :]))
                link(dve.tensor_copy(Kn1[:, :], tmp[0:1, 1, :]))
            link(dve.tensor_tensor(tmp[:, 0, :], zs[b][:, 0, :], k_of(1), ALU.mult))
            link(dve.tensor_tensor(tmp[:, 1, :], zs[b][:, 1, :], k_of(0), ALU.mult))
            link(dve.tensor_tensor(to[:, 1], tmp[:, 0:1, :], tmp[:, 1:2, :], ALU.add))
            if first:
                link(dve.tensor_copy(YS[0:1, 1, 0, :], Kn1[:, :]))

        Kn1 = ss.sb("Kn1", [1, HW])

        def first_spectra(jj, peeled):
            with nc.Block() as block:
                @block.sync
                def _(sp):
                    for b in range(2):
                        sp.dma_start(Fm[b][:, :, :, :], ap["dft"].rearrange("(n q) p t r f -> n q p t r f", q=2)[jj, b]).then_inc(f_in[b], 16)

                @block.tensor
                def _(pe):
                    for b in range(2):
                        pe.wait_ge(f_in[b], 16)
                        for r in range(2):
                            if b:
                                pe.wait_ge(k_out, 4 * (b - 1) + 2 * r + 2)
                                pe.wait_ge(z_out, 2 * (b - 1) + r + 1)
                            taps = plus if r == 0 else minus
                            for o in range(2):
                                for n in range(LT):
                                    mm = pe.matmul(bank[3 * r + o][:, :], Fm[b][:, n, r, :], taps[:, n, o * 512:(o + 1) * 512], start=(n == 0), stop=(n == LT - 1))
                                mm.then_inc(k_mm, 1)
                            for n in range(LT):
                                mm = pe.matmul(bank[3 * r + 2][:, :], Fm[b][:, n, r, :], z[:, n, :], start=(n == 0), stop=(n == LT - 1))
                            mm.then_inc(z_mm, 1)

                @block.scalar
                def _(act):
                    for b in range(2):
                        for r in range(2):
                            act.wait_ge(z_mm, 2 * b + r + 1)
                            nc.scalar.copy(zs[b][:, r, :], bank[3 * r + 2][:, :]).then_inc(z_out, 1)

                @block.vector
                def _(dve):
                    link = Linked(dve, seq)
                    for b in range(2):
                        j = jj * 2 + b
                        for r in range(2):
                            for o in range(2):
                                dve.wait_ge(k_mm, 4 * b + 2 * r + o + 1)
                                to = ks[:, r:r + 1, :] if o == 0 else KS[:, r, bass.ds(j, 1), :]
                                dve.tensor_tensor(to, bank[3 * r + o][:, :].unsqueeze(1), rk[:, o * 512:(o + 1) * 512].unsqueeze(1), ALU.mult).then_inc(k_out, 1)
                                dve.wait_ge(k_out, 4 * b + 2 * r + o + 1)
                        if peeled and b == 0:
                            link(dve.tensor_copy(ks[0:1, 1, :], Kn[0:1, 0:512]))
                            link(dve.tensor_copy(KS[0:1, 1, 0, :], Kn[0:1, 512:1024]))
                        dve.wait_ge(z_out, 2 * b + 2)
                        products(dve, link, j, b, lambda r: ks[:, r, :], peeled and b == 0)
            ss.clear()

        def second_spectra(jj, peeled):
            with nc.Block() as block:
                @block.sync
                def _(sp):
                    for b in range(2):
                        sp.dma_start(Fm[b][:, :, :, :], ap["dft"].rearrange("(n q) p t r f -> n q p t r f", q=2)[jj, b]).then_inc(f_in[b], 16)

                @block.tensor
                def _(pe):
                    for b in range(2):
                        pe.wait_ge(f_in[b], 16)
                        for r in range(2):
                            for n in range(LT):
                                mm = pe.matmul(bank[2 * b + r][:, :], Fm[b][:, n, r, :], z[:, n, :], start=(n == 0), stop=(n == LT - 1))
                            mm.then_inc(z_mm, 1)

                @block.scalar
                def _(act):
                    for b in range(2):
                        for r in range(2):
                            act.wait_ge(z_mm, 2 * b + r + 1)
                            nc.scalar.copy(zs[b][:, r, :], bank[2 * b + r][:, :]).then_inc(z_out, 1)

                @block.vector
                def _(dve):
                    link = Linked(dve, seq)
                    for b in range(2):
                        j = jj * 2 + b
                        dve.wait_ge(z_out, 2 * b + 2)
                        for r in range(2):
                            link(dve.tensor_copy(ks[:, r:r + 1, :], KS[:, r, bass.ds(j, 1), :]))
                        products(dve, link, j, b, lambda r: ks[:, r, :], peeled and b == 0)
            ss.clear()

        one = first_spectra if filters else second_spectra
        one(0, True)
        with nc.Fori(1, 4) as jj:
            one(jj, False)


def hyena_inverse(nc, ap, order, HX, YS, z, O):
    with Stage(nc, f"inv{order}") as st:
        G = [st.sb(f"G{b}", [P, 16, P]) for b in range(2)]
        x = [st.sb(f"x{b}", [P, HW]) for b in range(2)]
        skip = st.sb("skip", [P, HW])
        t = [st.sb(f"t{b}", [P, HW]) for b in range(2)]
        acc = [st.ps(f"acc{b}") for b in range(2)]
        skip_in = st.sem("skip_in")
        g_in = [st.sem(f"g_in{b}") for b in range(2)]
        mm_done, out, stored, seq = (st.sem(n) for n in ("mm_done", "out", "stored", "seq"))
        with nc.Block() as block:
            @block.sync
            def _(sp):
                sp.dma_start(skip[:, :], ap["hy_skip"][0, order].partition_broadcast(P)).then_inc(skip_in, 16)
                sp.wait_ge(skip_in, 16)
        with nc.Fori(0, LT // 2) as m:
            with nc.Block() as block:
                @block.sync
                def _(sp):
                    for b in range(2):
                        sp.dma_start(G[b][:, :, :], ap["idft"].rearrange("(n q) p c t -> n q p c t", q=2)[m, b]).then_inc(g_in[b], 16)
                        sp.dma_start(x[b][:, :], rows(HX[1 + order], True)[m, b]).then_inc(g_in[b], 16)
                    if O is not None:
                        for b in range(2):
                            sp.wait_ge(out, b + 1)
                            sp.dma_start(rows(O[0:LAT, HW:D], True)[m, b], t[b][:, :]).then_inc(stored, 16)
                        sp.wait_ge(stored, 32)

                @block.tensor
                def _(pe):
                    for b in range(2):
                        pe.wait_ge(g_in[b], 32)
                        for c in range(16):
                            mm = pe.matmul(acc[b][:, :], G[b][:, c, :], YS[:, c // 8, c % 8, :], start=(c == 0), stop=(c == 15))
                        mm.then_inc(mm_done, 1)

                @block.vector
                def _(dve):
                    link = Linked(dve, seq)
                    for b in range(2):
                        dve.wait_ge(g_in[b], 32)
                        zt = z[:, bass.ds(m * 2 + b, 1), :]
                        tb = t[b][:, :].unsqueeze(1)
                        link(dve.tensor_tensor(tb, zt, skip[:, :].unsqueeze(1), ALU.mult))
                        dve.wait_ge(mm_done, b + 1)
                        link(dve.tensor_tensor(t[b][:, :], t[b][:, :], acc[b][:, :], ALU.add))
                        dve.tensor_tensor(zt if O is None else tb, tb, x[b][:, :].unsqueeze(1), ALU.mult).then_inc(out, 1)
                        dve.wait_ge(out, b + 1)
            st.clear()


def hyena_constants():
    f = np.float32
    L = LAT
    t_idx = np.arange(L, dtype=f)
    t = (t_idx / f(L - 1)).astype(f)
    bands = np.linspace(1e-4, 15, 16, dtype=f)
    ang = (f(2.0 * np.pi) * bands[None, :] * t_idx[:, None] / f(L)).astype(f)
    feats = np.concatenate([t[:, None], np.cos(ang), -np.sin(ang)], -1).astype(f)
    deltas = np.linspace(np.log(1e-2) / 0.3, np.log(1e-2) / 1.5, HW, dtype=f)
    window = np.exp(-t[:, None] * np.abs(deltas)).astype(f)
    n, k = np.arange(L), np.arange(NFREQ)
    w = 2 * np.pi * ((n[:, None] * k[None, :]) % 2048) / 2048
    re, im = np.cos(w), -np.sin(w)
    alt = (-1.0) ** n
    im[:, 0] = alt
    dft = np.stack([re, im], 1).reshape(8, P, 2, 8, P).transpose(3, 1, 0, 2, 4)
    gre, gim = 2 * re.T / 2048, 2 * im.T / 2048
    gre[0], gim[0] = 1 / 2048, alt / 2048
    idft = np.concatenate([gre, gim], 0).reshape(16, P, 8, P).transpose(2, 1, 0, 3)
    return (np.ascontiguousarray(feats.T), window, np.ascontiguousarray(dft.astype(f)), np.ascontiguousarray(idft.astype(f)),
            alt[:P, None].astype(f))


def rwkv_readout_stage(nc, ap, FE, Y, O):
    GN_EPS = 64e-5
    with Stage(nc, "read") as st:
        y = [st.sb(f"y{p}", [P, 2, HW]) for p in range(2)]
        f = [st.sb(f"f{p}", [P, 4, HW]) for p in range(2)]
        cst = st.sb("cst", [P, 3, HW])
        sq = [st.sb(f"sq{p}", [P, HW]) for p in range(2)]
        m = [st.sb(f"m{p}", [P, 3, HEADS]) for p in range(2)]
        const_in, ms_ready, rt_ready, centred, squared, done, stored = (st.sem(n) for n in (
            "const_in", "ms_ready", "rt_ready", "centred", "squared", "done", "stored"))
        loaded = [st.sem(f"loaded{p}") for p in range(2)]
        bonus_in = [st.sem(f"bonus_in{p}") for p in range(2)]
        seq, pseq = st.sem("seq"), st.sem("pseq")
        with nc.Block() as block:
            @block.sync
            def _(sp):
                sp.dma_start(cst[:, 0, :], ap["rwkv_gn_w"][0].partition_broadcast(P)).then_inc(const_in, 16)
                sp.dma_start(cst[:, 1, :], ap["rwkv_gn_b"][0].partition_broadcast(P)).then_inc(const_in, 16)
                sp.dma_start(cst[:, 2, :], ap["rwkv_r_k"][0].rearrange("h d -> (h d)").partition_broadcast(P)).then_inc(const_in, 16)
                sp.wait_ge(const_in, 48)
        with nc.Fori(0, LT // 2) as i:
            with nc.Block() as block:
                @block.sync
                def _(sp):
                    fe = FE[CTX:TOK].rearrange("(n q p) f d -> n q p f d", q=2, p=P)
                    for p in range(2):
                        for d in range(2):
                            sp.dma_start(y[p][:, d, :], rows(Y[d], True)[i, p]).then_inc(loaded[p], 16)
                        sp.dma_start(f[p][:, 0:2, :], fe[i, p][:, 0:2, :]).then_inc(loaded[p], 16)
                        sp.dma_start(f[p][:, 2, :], fe[i, p][:, 4, :]).then_inc(loaded[p], 16)
                        sp.dma_start(f[p][:, 3, :], fe[i, p][:, 7, :]).then_inc(loaded[p], 16)
                    for p in range(2):
                        sp.wait_ge(done, p + 1)
                        sp.dma_start(rows(O[0:LAT, 0:HW], True)[i, p], y[p][:, 0, :]).then_inc(stored, 16)
                    sp.wait_ge(stored, 32)

                @block.scalar
                def _(act):
                    for p in range(2):
                        act.wait_ge(centred, p + 1)
                        nc.scalar.activation(sq[p][:, :], y[p][:, 0, :], ACT.Square).then_inc(squared, 1)
                        act.wait_ge(ms_ready, p + 1)
                        nc.scalar.activation(m[p][:, 1, :], m[p][:, 1, :], ACT.Sqrt).then_inc(rt_ready, 1)

                def heads(x):
                    return x.rearrange("p (h d) -> p h d", d=HD)

                @block.gpsimd
                def _(pool):
                    for p in range(2):
                        link = Linked(pool, pseq)
                        link.n = 4 * p
                        pool.wait_ge(loaded[p], 80)
                        link(pool.tensor_tensor(f[p][:, 2, :], f[p][:, 2, :], f[p][:, 3, :], ALU.add))
                        link(pool.tensor_tensor(f[p][:, 2, :], f[p][:, 2, :], f[p][:, 0, :], ALU.mult))
                        link(pool.tensor_tensor(f[p][:, 2, :], f[p][:, 2, :], cst[:, 2, :], ALU.mult))
                        link(pool.tensor_scalar(f[p][:, 2, :], f[p][:, 2, :], 0.5, None, ALU.mult))

                @block.vector
                def _(dve):
                    link = Linked(dve, seq)
                    for p in range(2):
                        dve.wait_ge(loaded[p], 80)
                        yy = y[p][:, 0, :]
                        link(dve.tensor_tensor(yy, yy, y[p][:, 1, :], ALU.add))
                        link(dve.tensor_reduce(m[p][:, 0, :], heads(yy), AX.X, ALU.add))
                        link(dve.tensor_scalar(m[p][:, 0, :], m[p][:, 0, :], 1.0 / HD, None, ALU.mult))
                        dve.tensor_tensor(heads(yy), heads(yy), m[p][:, 0, :].unsqueeze(2).to_broadcast([P, HEADS, HD]), ALU.subtract).then_inc(centred, 1)
                        dve.wait_ge(pseq, 4 * p + 4)
                        link(dve.tensor_reduce(m[p][:, 2, :], heads(f[p][:, 2, :]), AX.X, ALU.add))
                        link(dve.tensor_tensor(heads(f[p][:, 1, :]), heads(f[p][:, 1, :]), m[p][:, 2, :].unsqueeze(2).to_broadcast([P, HEADS, HD]), ALU.mult))
                        dve.wait_ge(squared, p + 1)
                        link(dve.tensor_reduce(m[p][:, 1, :], heads(sq[p][:, :]), AX.X, ALU.add))
                        dve.tensor_scalar(m[p][:, 1, :], m[p][:, 1, :], 1.0 / HD, GN_EPS, ALU.mult, ALU.add).then_inc(ms_ready, 1)
                        dve.wait_ge(rt_ready, p + 1)
                        link(dve.reciprocal(m[p][:, 1, :], m[p][:, 1, :]))
                        link(dve.tensor_tensor(heads(yy), heads(yy), m[p][:, 1, :].unsqueeze(2).to_broadcast([P, HEADS, HD]), ALU.mult))
                        link(dve.tensor_tensor(yy, yy, cst[:, 0, :], ALU.mult))
                        link(dve.tensor_tensor(yy, yy, cst[:, 1, :], ALU.add))
                        dve.tensor_tensor(yy, yy, f[p][:, 1, :], ALU.add).then_inc(done, 1)
            st.clear()


def forget_stage(nc, ap, U3, keep):
    with Stage(nc, "forget") as st:
        f = st.sb("f", [P, LT, HEADS])
        g = st.sb("g", [P, LT, HEADS])
        b = st.sb("b", [P, HEADS])
        tri = st.sb("tri", [P, P])
        ones = st.sb("ones", [P, P])
        pc = st.ps("pc")
        loaded, x_ready, exped, lns, lf, mm_done, seq = (st.sem(n) for n in ("loaded", "x_ready", "exped", "lns", "lf", "mm_done", "seq"))
        with nc.Block() as block:
            @block.sync
            def _(sp):
                sp.dma_start(f[:, :, :], U3[:, 2560:2568].rearrange("(n p) h -> p n h", p=P)).then_inc(loaded, 16)
                sp.dma_start(b[:, :], ap["b_forget_2"][0].partition_broadcast(P)).then_inc(loaded, 16)
                sp.dma_start(tri[:, :], ap["tri128"]).then_inc(loaded, 16)

            @block.scalar
            def _(act):
                act.wait_ge(x_ready, 1)
                nc.scalar.activation(g[:, :, :], g[:, :, :], ACT.Exp).then_inc(exped, 1)
                act.wait_ge(exped, 1)
                nc.scalar.activation(g[:, :, :], g[:, :, :], ACT.Ln, bias=1.0).then_inc(lns, 1)

            @block.vector
            def _(dve):
                link = Linked(dve, seq)
                link(dve.memset(ones[:, :], 1.0))
                dve.wait_ge(loaded, 48)
                link(dve.tensor_tensor(f[:, :, :], f[:, :, :], b[:, :].unsqueeze(1).to_broadcast([P, LT, HEADS]), ALU.add))
                link(dve.tensor_scalar(g[:, :, :], f[:, :, :], -1.0, None, ALU.mult))
                dve.tensor_tensor(g[:, :, :], g[:, :, :], f[:, :, :], ALU.min).then_inc(x_ready, 1)
                dve.wait_ge(lns, 1)
                link(dve.tensor_scalar(f[:, :, :], f[:, :, :], 0.0, None, ALU.min))
                dve.tensor_tensor(f[:, :, :], f[:, :, :], g[:, :, :], ALU.subtract).then_inc(lf, 1)
                dve.wait_ge(mm_done, 1)
                link(dve.tensor_copy(keep[:, :, :], pc[:, 0:LT * HEADS].rearrange("p (n h) -> p n h", h=HEADS)))

            @block.tensor
            def _(pe):
                pe.wait_ge(lf, 1)
                pe.wait_ge(loaded, 48)
                pe.wait_ge(seq, 1)
                for m in range(LT):
                    for n in range(m + 1):
                        mm = pe.matmul(pc[:, m * HEADS:(m + 1) * HEADS], tri[:, :] if n == m else ones[:, :], f[:, n, :], start=(n == 0), stop=(n == m))
                mm.then_inc(mm_done, 1)


KF = HD + 2


def fox_prep_stage(nc, ident, U3, csum, QF):
    with Stage(nc, "foxp") as st:
        u = [st.sb(f"u{p}", [P, 2 * HW]) for p in range(2)]
        aug = [st.sb(f"aug{p}", [P, 16, KF]) for p in range(2)]
        tb = st.sb("tb", [KF, 16, 2 * P])
        pt = [st.ps(f"pt{i}") for i in range(8)]
        loaded = [st.sem(f"loaded{p}") for p in range(2)]
        filled = [st.sem(f"filled{p}") for p in range(2)]
        trans, evac, stored = (st.sem(n) for n in ("trans", "evac", "stored"))
        evac_a = st.sem("evac_a")
        with nc.Fori(0, LT // 2) as i:
            with nc.Block() as block:
                @block.sync
                def _(sp):
                    for p in range(2):
                        sp.dma_start(u[p][:, :], rows(U3, True)[i, p][:, 1024:2048]).then_inc(loaded[p], 16)
                    sp.wait_ge(evac, 4)
                    sp.wait_ge(evac_a, 4)
                    sp.dma_start(QF.rearrange("n c (m t) -> m c n t", t=2 * P)[i], tb[:, :, :]).then_inc(stored, 16)
                    sp.wait_ge(stored, 16)

                @block.vector
                def _(dve):
                    for p in range(2):
                        dve.wait_ge(loaded[p], 16)
                        qk = u[p][:, :].rearrange("p (h d) -> p h d", d=HD)
                        c = csum[:, bass.ds(i * 2 + p, 1), :].rearrange("p o h -> p h o")
                        dve.tensor_scalar(aug[p][:, 0:8, 0:HD], qk[:, 0:8, :], HD ** -0.5, None, ALU.mult).then_inc(filled[p], 1)
                        dve.tensor_copy(aug[p][:, 8:16, 0:HD], qk[:, 8:16, :]).then_inc(filled[p], 1)
                        dve.tensor_copy(aug[p][:, 0:8, HD + 1:HD + 2], c).then_inc(filled[p], 1)
                        dve.tensor_scalar(aug[p][:, 8:16, HD:HD + 1], c, -1.0, None, ALU.mult).then_inc(filled[p], 1)
                        dve.memset(aug[p][:, 0:8, HD:HD + 1], 1.0).then_inc(filled[p], 1)
                        dve.memset(aug[p][:, 8:16, HD + 1:HD + 2], 1.0).then_inc(filled[p], 1)
                    for p in range(2):
                        for g in (1, 3):
                            dve.wait_ge(trans, 4 * p + g + 1)
                            dve.tensor_copy(tb[:, 4 * g:4 * g + 4, p * P:(p + 1) * P], pt[4 * p + g][0:KF, :].rearrange("p (b t) -> p b t", t=P)).then_inc(evac, 1)

                @block.scalar
                def _(act):
                    for p in range(2):
                        for g in (0, 2):
                            act.wait_ge(trans, 4 * p + g + 1)
                            nc.scalar.copy(tb[:, 4 * g:4 * g + 4, p * P:(p + 1) * P], pt[4 * p + g][0:KF, :].rearrange("p (b t) -> p b t", t=P)).then_inc(evac_a, 1)

                @block.tensor
                def _(pe):
                    for p in range(2):
                        pe.wait_ge(filled[p], 6)
                        for g in range(4):
                            for n in range(4):
                                mm = pe.transpose(pt[4 * p + g][0:KF, n * P:(n + 1) * P], aug[p][:, 4 * g + n, :], ident[:, :])
                            mm.then_inc(trans, 1)
            st.clear()


def fox_stage(nc, ap, ident, U3, QF, O):
    units = [dict(q=i * P, keys=[(0, P * (i + 1))], tiles=list(range(i + 1)), bias=None) for i in range(LT)]
    qv = QF[0:8].rearrange("(j s) c t -> j s c t", s=2)
    kv = QF[8:16].rearrange("(j s) c t -> j s c t", s=2)
    vv = U3[:, 2048:2560].rearrange("(m p) (j s d) -> j s p m d", p=P, s=2, d=HD)

    def loads(sp, idx, b, loaded):
        (j,) = idx
        for s in range(2):
            sp.dma_start(b["qT"][s][:, :], qv[j, s]).then_inc(loaded[s], 16)
            sp.dma_start(b["kT"][s][:, :], kv[j, s]).then_inc(loaded[s], 16)
            sp.dma_start(b["v"][s][:, :, :], vv[j, s]).then_inc(loaded[s], 16)

    ov = O[:, HW:D].rearrange("(x p) (j s d) -> j p x s d", p=P, s=2, d=HD)

    def out(sp, idx, o, stored):
        (j,) = idx
        sp.dma_start(ov[j], o[:, :, :, :]).then_inc(stored, 16)
        sp.wait_ge(stored, 16)

    attention_stage(nc, "fox", ident, [4], KF, LAT, units, loads, [48, 48], False, out, causal=ap["causal_mask"])


def spatial_stage(nc, ap, ident, U3, O):
    LN_EPS = 1e-5
    with Stage(nc, "sgu") as st:
        u = [st.sb(f"u{p}", [P, D]) for p in range(2)]
        t = [st.sb(f"t{p}", [P, HW]) for p in range(2)]
        sq = [st.sb(f"sq{p}", [P, HW]) for p in range(2)]
        m = [st.sb(f"m{p}", [P, 2]) for p in range(2)]
        gb = st.sb("gb", [P, 2, HW])
        ws = st.sb("ws", [P, HEADS, P])
        wsT = st.sb("wsT", [P, HEADS, P])
        tri = st.sb("tri", [P, P])
        bs = st.sb("bs", [HEADS, P])
        bsT = st.sb("bsT", [P, HEADS])
        pt = [st.ps(f"pt{i}") for i in range(3)]
        pm = [st.ps(f"pm{i}") for i in range(2)]
        const_in, trans, gelu, centred, squared, ms_ready, rt_ready, v_ready, mixed, done, stored, seq = (st.sem(n) for n in (
            "const_in", "trans", "gelu", "centred", "squared", "ms_ready", "rt_ready", "v_ready", "mixed", "done", "stored", "seq"))
        loaded = [st.sem(f"loaded{p}") for p in range(2)]
        with nc.Block() as block:
            @block.sync
            def _(sp):
                sp.dma_start(gb[:, 0, :], ap["ln_v_gain_2"][0].partition_broadcast(P)).then_inc(const_in, 16)
                sp.dma_start(gb[:, 1, :], ap["ln_v_bias_2"][0].partition_broadcast(P)).then_inc(const_in, 16)
                sp.dma_start(ws[:, :, :], ap["w_spatial_2"][0].rearrange("g t s -> t g s")).then_inc(const_in, 16)
                sp.dma_start(bs[:, :], ap["b_spatial_2"][0]).then_inc(const_in, 16)
                sp.dma_start(tri[:, :], ap["tri128"]).then_inc(const_in, 16)

            @block.tensor
            def _(pe):
                pe.wait_ge(const_in, 80)
                for g in range(HEADS):
                    pe.transpose(pt[g // 4][:, (g % 4) * P:(g % 4 + 1) * P], ws[:, g, :], ident[:, :])
                pe.transpose(pt[2][:, 0:HEADS], bs[:, :], ident[0:HEADS, 0:HEADS]).then_inc(trans, 1)

            @block.vector
            def _(dve):
                link = Linked(dve, seq)
                dve.wait_ge(trans, 1)
                for g in range(HEADS):
                    link(dve.tensor_tensor(wsT[:, g, :], pt[g // 4][:, (g % 4) * P:(g % 4 + 1) * P], tri[:, :], ALU.mult))
                link(dve.tensor_copy(bsT[:, :], pt[2][:, 0:HEADS]))
        st.clear()
        with nc.Fori(0, LT // 2) as i:
            with nc.Block() as block:
                @block.sync
                def _(sp):
                    for p in range(2):
                        sp.dma_start(u[p][:, :], rows(U3, True)[i, p][:, 0:1024]).then_inc(loaded[p], 16)
                    for p in range(2):
                        sp.wait_ge(done, p + 1)
                        sp.dma_start(rows(O[:, 0:HW], True)[i, p], t[p][:, :]).then_inc(stored, 16)
                    sp.wait_ge(stored, 32)

                @block.scalar
                def _(act):
                    for p in range(2):
                        act.wait_ge(loaded[p], 16)
                        nc.scalar.activation(u[p][:, :], u[p][:, :], ACT.Gelu).then_inc(gelu, 1)
                    for p in range(2):
                        act.wait_ge(centred, p + 1)
                        nc.scalar.activation(sq[p][:, :], u[p][:, HW:D], ACT.Square, accum_out=m[p][:, 1:2]).then_inc(squared, 1)
                    for p in range(2):
                        act.wait_ge(ms_ready, p + 1)
                        nc.scalar.activation(m[p][:, 1:2], m[p][:, 1:2], ACT.Sqrt).then_inc(rt_ready, 1)

                @block.tensor
                def _(pe):
                    for p in range(2):
                        pe.wait_ge(v_ready, p + 1)
                        for g in range(HEADS):
                            mm = pe.matmul(pm[p][:, g * HD:(g + 1) * HD], wsT[:, g, :], u[p][:, HW + g * HD:HW + (g + 1) * HD], start=True, stop=True)
                        mm.then_inc(mixed, 1)

                @block.vector
                def _(dve):
                    link = Linked(dve, seq)
                    for p in range(2):
                        v = u[p][:, HW:D]
                        dve.wait_ge(gelu, p + 1)
                        link(dve.tensor_reduce(m[p][:, 0:1], v, AX.X, ALU.add))
                        link(dve.tensor_scalar(m[p][:, 0:1], m[p][:, 0:1], 1.0 / HW, None, ALU.mult))
                        dve.tensor_scalar(v, v, m[p][:, 0:1], None, ALU.subtract).then_inc(centred, 1)
                    for p in range(2):
                        dve.wait_ge(squared, p + 1)
                        dve.tensor_scalar(m[p][:, 1:2], m[p][:, 1:2], 1.0 / HW, LN_EPS, ALU.mult, ALU.add).then_inc(ms_ready, 1)
                    for p in range(2):
                        v = u[p][:, HW:D]
                        dve.wait_ge(rt_ready, p + 1)
                        link(dve.reciprocal(m[p][:, 1:2], m[p][:, 1:2]))
                        link(dve.scalar_tensor_tensor(out=v, in0=v, scalar=m[p][:, 1:2], in1=gb[:, 0, :], op0=ALU.mult, op1=ALU.mult))
                        dve.tensor_tensor(v, v, gb[:, 1, :], ALU.add).then_inc(v_ready, 1)
                    for p in range(2):
                        dve.wait_ge(mixed, p + 1)
                        th = t[p][:, :].rearrange("p (g d) -> p g d", d=HD)
                        link(dve.tensor_tensor(th, pm[p][:, :].rearrange("p (g d) -> p g d", d=HD), bsT[:, :].unsqueeze(2).to_broadcast([P, HEADS, HD]), ALU.add))
                        dve.tensor_tensor(t[p][:, :], t[p][:, :], u[p][:, 0:HW], ALU.mult).then_inc(done, 1)
            st.clear()


def merge_stage(nc, ident, O, xT, gain):
    with Stage(nc, "merge") as st:
        x = [st.sb(f"x{p}", [P, D]) for p in range(2)]
        sq = st.sb("sq", [P, D])
        ss = st.sb("ss", [P, 4])
        rs = st.sb("rs", [P, 4])
        pt = [st.ps(f"pt{i}") for i in range(4)]
        loaded = [st.sem(f"loaded{p}") for p in range(2)]
        ss_ready, ms_ready, rt_ready, scaled, trans, evac, seq = (st.sem(n) for n in ("ss_ready", "ms_ready", "rt_ready", "scaled", "trans", "evac", "seq"))
        with nc.Fori(0, LT // 2) as i:
            with nc.Block() as block:
                @block.sync
                def _(sp):
                    for p in range(2):
                        sp.dma_start(x[p][:, :], rows(O[0:LAT], True)[i, p]).then_inc(loaded[p], 16)

                @block.scalar
                def _(act):
                    for p in range(2):
                        act.wait_ge(loaded[p], 16)
                        for h in range(2):
                            nc.scalar.activation(sq[:, h * HW:(h + 1) * HW], x[p][:, h * HW:(h + 1) * HW], ACT.Square,
                                                 accum_out=ss[:, 2 * p + h:2 * p + h + 1]).then_inc(ss_ready, 1)
                        if p == 0:
                            act.wait_ge(ss_ready, 2)
                    act.wait_ge(ms_ready, 1)
                    nc.scalar.activation(rs[:, :], ss[:, :], ACT.Sqrt).then_inc(rt_ready, 1)
                    for n in range(4):
                        act.wait_ge(trans, n + 1)
                        for k in range(4 * (n % 2), 4 * (n % 2) + 4):
                            nc.scalar.activation(xT[:, k, bass.ds(i * 2 * P + (n // 2) * P, P)], pt[n][:, (k % 4) * P:(k % 4 + 1) * P],
                                                 ACT.Copy if False else ACT.Identity, scale=gain[:, k:k + 1]).then_inc(evac, 1)

                @block.vector
                def _(dve):
                    link = Linked(dve, seq)
                    dve.wait_ge(ss_ready, 4)
                    dve.tensor_scalar(ss[:, :], ss[:, :], 1.0 / HW, NORM_EPS, ALU.mult, ALU.add).then_inc(ms_ready, 1)
                    dve.wait_ge(rt_ready, 1)
                    link(dve.reciprocal(rs[:, :], rs[:, :]))
                    for n in range(4):
                        xh = x[n // 2][:, (n % 2) * HW:(n % 2 + 1) * HW]
                        dve.tensor_scalar(xh, xh, rs[:, n:n + 1], None, ALU.mult).then_inc(scaled, 1)

                @block.tensor
                def _(pe):
                    for n in range(4):
                        pe.wait_ge(scaled, n + 1)
                        for k in range(4):
                            mm = pe.transpose(pt[n][:, k * P:(k + 1) * P], x[n // 2][:, (4 * (n % 2) + k) * P:(4 * (n % 2) + k + 1) * P], ident[:, :])
                        mm.then_inc(trans, 1)
            st.clear()


def ffn_in_stage(nc, ap, xT, hT):
    NF_T = FF // P
    wv = ap["w_ffn_in_2"][0].rearrange("(k p) (u j b n) -> j b u p k n", p=P, u=2, b=2, n=P)
    with Stage(nc, "ffi") as st:
        w = [st.sb(f"w{b}", [P, 2, KT, P]) for b in range(2)]
        g = [st.sb(f"g{b}", [P, LAT]) for b in range(2)]
        acc = [[st.ps(f"acc{b}{i}") for i in range(4)] for b in range(2)]
        w_in = [st.sem(f"w_in{b}") for b in range(2)]
        summed = [st.sem(f"summed{b}") for b in range(2)]
        silu = [st.sem(f"silu{b}") for b in range(2)]
        done = [st.sem(f"done{b}") for b in range(2)]
        turns = NF_T // 2
        with nc.Block() as block:
            @block.sync
            def _(sp):
                for b in range(2):
                    for u in range(2):
                        sp.dma_start(w[b][:, u, :, :], wv[0, b, u]).then_inc(w_in[b], 16)
                with sp.Fori(0, turns - 1) as j:
                    for b in range(2):
                        sp.wait_ge(summed[b], j * 2 + 2)
                        for u in range(2):
                            sp.dma_start(w[b][:, u, :, :], wv[j + 1, b, u]).then_inc(w_in[b], 16)

            @block.tensor
            def _(pe):
                for b in range(2):
                    pe.sem_inc(done[b], 1)
                with pe.Fori(0, turns) as j:
                    for b in range(2):
                        pe.wait_ge(w_in[b], j * 32 + 32)
                        pe.wait_ge(done[b], j + 1)
                        for u in range(2):
                            for h in range(2):
                                for k in range(KT):
                                    mm = pe.matmul(acc[b][2 * u + h][:, :], w[b][:, u, k, :], xT[:, k, h * 512:(h + 1) * 512], start=(k == 0), stop=(k == KT - 1))
                            mm.then_inc(summed[b], 1)

            @block.scalar
            def _(act):
                with act.Fori(0, turns) as j:
                    for b in range(2):
                        act.wait_ge(summed[b], j * 2 + 1)
                        act.wait_ge(done[b], j + 1)
                        for h in range(2):
                            nc.scalar.activation(g[b][:, h * 512:(h + 1) * 512], acc[b][h][:, :], ACT.Silu).then_inc(silu[b], 1)

            @block.vector
            def _(dve):
                with dve.Fori(0, turns) as j:
                    for b in range(2):
                        dve.wait_ge(summed[b], j * 2 + 2)
                        dve.wait_ge(silu[b], j * 2 + 2)
                        for h in range(2):
                            ins = dve.tensor_tensor(hT[:, bass.ds(j * 2 + b, 1), h * 512:(h + 1) * 512], g[b][:, h * 512:(h + 1) * 512].unsqueeze(1),
                                                    acc[b][2 + h][:, :].unsqueeze(1), ALU.mult)
                        ins.then_inc(done[b], 1)


def gemm(nc, name, xT, kt, mt, w, out, n0, n, wn, row_of=lambda m: m * P):
    assert n % (2 * wn) == 0
    wv = w[:, n0:n0 + n].rearrange("(k p) (j b n) -> j b p k n", p=P, b=2, n=wn)
    ov = out[:, n0:n0 + n].rearrange("r (j b n) -> j b r n", b=2, n=wn)
    gemm_stage(nc, name, xT, kt, mt, lambda j, b: wv[j, b], n // (2 * wn), wn,
               lambda j, b, m: ov[j, b][row_of(m):row_of(m) + P, :])


def build(nc, ap, out, scratch, part="ab"):
    U1 = scratch("U1", (TOK, ATTN_IN))
    QT = scratch("QT", (13 * P, TOK))
    REP = scratch("REP", (HEADS, PADR, HD, P))
    O1 = scratch("O1", (TOK, D))
    Y1 = scratch("Y1", (TOK, D))
    X1 = scratch("X1", (LAT, D))
    U2 = scratch("U2", (U2_ROWS, REC_IN))
    FE = scratch("FE", (TOK, NF, HW))
    YS = [scratch(f"YS{d}", (LAT, HW)) for d in range(2)]
    HX = scratch("HX", (3, LAT, HW))
    O2 = scratch("O2", (LAT, D))
    Y2 = scratch("Y2", (LAT, D))
    H0 = scratch("H0", (LAT, D))
    U3 = scratch("U3", (LAT, BLK_IN))
    QF = scratch("QF", (2 * HEADS, KF, LAT))
    O3 = scratch("O3", (LAT, D))
    Y3 = scratch("Y3", (LAT, D))
    H2 = scratch("H2", (LAT, D))
    Y4 = scratch("Y4", (LAT, D))
    x, ctx = ap["x"][0], ap["ctx"][0]

    def pair(dram, first=0):
        v = rows(dram, True)
        return lambda i, p: v[i + (-first), p] if first else v[i, p]

    with Stage(nc, "main") as st:
        ident = st.sb("ident", [P, P])
        gains = st.sb("gains", [P, 3, KT])
        const_in = st.sem("const_in")
        mods = {}
        with nc.Block() as block:
            @block.sync
            def _(sp):
                sp.dma_start(ident[:, :], ap["ident"]).then_inc(const_in, 16)
                for g, (src, lo, hi) in enumerate((("pre_mix_gain_2", 0, 8), ("pre_ffn_gain_2", 0, 8), ("out_norm_a_gain_2", 0, 4), ("out_norm_b_gain_2", 4, 8))):
                    to = {0: 0, 1: 2, 2: 1, 3: 1}[g]
                    sp.dma_start(gains[:, to, lo:hi], cols(ap[src][0]), allow_slow_non_contiguous=True).then_inc(const_in, 16)
                sp.wait_ge(const_in, 80)
        for pre in ("attn", "rec"):
            mods[pre] = (st.sb(f"modA_{pre}", [P, 2, KT]), st.sb(f"modB_{pre}", [P, 2, KT]), st.sb(f"gate_{pre}", [P, 2, D]))
            adaln_stage(nc, ap, pre, mods[pre])
        A, B, G = mods["attn"]
        with Stage(nc, "l1") as s1:
            xT = s1.sb("xT", [P, KT, TOK])
            norm_stage(nc, "n1", ident, (0, LT // 2), xT, pair(x), modA=A[:, 0, :], modB=B[:, 0, :])
            norm_stage(nc, "n1c", ident, (LT // 2, 5), xT, pair(ctx, LT // 2), modA=A[:, 1, :], modB=B[:, 1, :])
            gemm(nc, "g1", xT, KT, LT + CT, ap["attn_w_in"][0], U1, 0, ATTN_IN, 416)
        window_table_stage(nc, ap, REP)
        attn_prep_stage(nc, ap, ident, U1, QT, (0, 5), 0, 0)
        na_stage(nc, ap, ident, U1, QT, REP, O1)
        gqa_stage(nc, ap, ident, U1, QT, O1)
        with Stage(nc, "l1b") as s1:
            xT = s1.sb("xT", [P, KT, TOK])
            gated_stage(nc, "gt1", ident, (0, 5), xT, pair(O1), lambda h: pair(U1[:, 1536:2048] if h == 0 else U1[:, 2816:3328]))
            gemm(nc, "g2", xT, KT, LT + CT, ap["attn_w_out"][0], Y1, 0, D, 512)
        A2, B2, G2 = mods["rec"]
        with Stage(nc, "l2") as s2:
            xT = s2.sb("xT", [P, KT, TOK])
            norm_stage(nc, "n2", ident, (0, LT // 2), xT, pair(x), y_of=pair(Y1[0:LAT]), gate=G[:, 0, :], z_out=pair(X1), modA=A2[:, 0, :], modB=B2[:, 0, :])
            norm_stage(nc, "n2c", ident, (LT // 2, 5), xT, pair(ctx, LT // 2), y_of=pair(Y1), gate=G[:, 1, :], modA=A2[:, 1, :], modB=B2[:, 1, :])
            place = lambda m: LAT0 + m * P if m < LT else CTX0 + (m - LT) * P
            gemm(nc, "g3", xT, KT, LT + CT, ap["rec_w_in"][0], U2, 0, RW, 416, place)
            gemm(nc, "g4", xT, KT, LT, ap["rec_w_in"][0], U2, RW, REC_IN - RW, 320, place)
        zero_rows_stage(nc, U2)
        rwkv_feature_stage(nc, ap, ident, U2, FE, [(CT, CTX0, 0), (LT, LAT0, CTX)])
        rwkv_scan_stage(nc, ap, ident, FE, YS)
        rwkv_readout_stage(nc, ap, FE, YS, O2)
        hyena_conv3_stage(nc, ap, U2, HX)
        hyena_stage(nc, ap, HX, O2)
        lat2 = U2[LAT0:LAT0 + LAT]
        with Stage(nc, "l2b") as s2:
            xT = s2.sb("xT", [P, KT, LAT])
            gated_stage(nc, "gt2", ident, (0, 4), xT, pair(O2), lambda h: pair(lat2[:, RW:RW + HW] if h == 0 else lat2[:, REC_IN - HW:REC_IN]))
            gemm(nc, "g5", xT, KT, LT, ap["rec_w_out"][0], Y2, 0, D, 512)
        with Stage(nc, "l3") as s3:
            xT = s3.sb("xT", [P, KT, LAT])
            norm_stage(nc, "n3", ident, (0, 4), xT, pair(X1), y_of=pair(Y2), gate=G2[:, 0, :], z_row=ap["final_norm"], z_out=pair(H0), modA=gains[:, 0, :])
            gemm(nc, "g6", xT, KT, LT, ap["w_in_2"][0], U3, 0, BLK_IN, 428)
        with Stage(nc, "l3a") as s3:
            csum = s3.sb("csum", [P, LT, HEADS])
            forget_stage(nc, ap, U3, csum)
            fox_prep_stage(nc, ident, U3, csum, QF)
        fox_stage(nc, ap, ident, U3, QF, O3)
        spatial_stage(nc, ap, ident, U3, O3)
        with Stage(nc, "l3b") as s3:
            xT = s3.sb("xT", [P, KT, LAT])
            merge_stage(nc, ident, O3, xT, gains[:, 1, :])
            gemm(nc, "g7", xT, KT, LT, ap["w_out_2"][0], Y3, 0, D, 512)
        with Stage(nc, "l4") as s4:
            hT = s4.sb("hT", [P, FF // P, LAT])
            with Stage(nc, "l4a") as s5:
                xT = s5.sb("xT", [P, KT, LAT])
                norm_stage(nc, "n4", ident, (0, 4), xT, pair(H0), y_of=pair(Y3), y_row=ap["post_mix_gain_2"][0], z_out=pair(H2), modA=gains[:, 2, :])
                ffn_in_stage(nc, ap, xT, hT)
            gemm(nc, "g8", hT, FF // P, LT, ap["w_ffn_out_2"][0], Y4, 0, D, 256)
        norm_stage(nc, "n5", ident, (0, 4), None, pair(H2), y_of=pair(Y4), y_row=ap["post_ffn_gain_2"][0], z_out=pair(out[0]))


def constants():
    tri, keep, lev, lev0 = scan_constants()
    feats, window, dft, idft, alt = hyena_constants()
    s, t = np.meshgrid(np.arange(P), np.arange(P), indexing="ij")
    return dict(ident=np.eye(P, dtype=np.float32), rope=rope_table(), window_mask=window_mask(), tri=tri, keep=keep, lev=lev, lev0=lev0,
                hy_feats=feats, hy_window=window, dft=dft, idft=idft, alternate=alt,
                tri128=(s <= t).astype(np.float32),
                causal_mask=np.where(s >= t, 0.0, -1e30).astype(np.float32))


_INS = ["x", "c", "ctx", "c_ctx", "attn_norm", "attn_ada_w", "attn_ada_b", "attn_w_in", "na_rpb", "gqa_q_gain",
        "gqa_k_gain", "attn_w_out", "rec_norm", "rec_ada_w", "rec_ada_b", "rec_w_in", "rwkv_mu", "rwkv_w0",
        "rwkv_w_up", "rwkv_a0", "rwkv_a_up", "rwkv_k_k", "rwkv_k_a", "rwkv_r_k", "rwkv_gn_w", "rwkv_gn_b", "hy_short",
        "hy_w1", "hy_b1", "hy_w2", "hy_b2", "hy_w3", "hy_b3", "hy_skip", "rec_w_out", "final_norm", "pre_mix_gain_2",
        "w_in_2", "ln_v_gain_2", "ln_v_bias_2", "w_spatial_2", "b_spatial_2", "b_forget_2", "out_norm_a_gain_2",
        "out_norm_b_gain_2", "w_out_2", "post_mix_gain_2", "pre_ffn_gain_2", "w_ffn_in_2", "w_ffn_out_2",
        "post_ffn_gain_2"]


def kernel(**inputs):
    import concourse.bacc as _bacc
    from concourse.bass_utils import run_bass_kernel_spmd as _run

    nc = _bacc.Bacc("TRN2", target_bir_lowering=False, num_devices=1)
    arrays, ap = {}, {}
    data = {name: np.ascontiguousarray(inputs[name]) for name in _INS}
    data.update(constants())
    for name, a in data.items():
        arrays[f"in_{name}"] = a
        ap[name] = nc.dram_tensor(f"in_{name}", a.shape, mybir.dt.from_np(a.dtype), kind="ExternalInput").ap()
    out = nc.dram_tensor("out_0", (1, LAT, D), F32, kind="ExternalOutput").ap()
    build(nc, ap, out, lambda name, shape: nc.dram_tensor(f"s_{name}", shape, F32, kind="Internal").ap())
    r = _run(nc, [arrays], core_ids=[0])
    return r.results[0]["out_0"]
```

```python
from contextlib import ExitStack

import numpy as np
import concourse.bass as bass
from concourse import mybir

F32 = mybir.dt.float32
F32R = mybir.dt.float32r
ACT = mybir.ActivationFunctionType
ALU = mybir.AluOpType
AX = mybir.AxisListType

P = 128
D = 1024
KT = D // P
LAT = 1024
CTX = 256
TOK = LAT + CTX
LT = LAT // P
CT = CTX // P
HD = 64
HEADS = 8
HW = HEADS * HD
ATTN_IN = 3328
REC_IN = 4224
BLK_IN = 2568
FF = 2816
NORM_EPS = 1e-6


class Linked:

    def __init__(self, eng, sem):
        self.eng, self.sem, self.n = eng, sem, 0

    def __call__(self, ins):
        self.n += 1
        ins.then_inc(self.sem, 1)
        self.eng.wait_ge(self.sem, self.n)


def high(eng, to, src):
    return eng.tensor_copy(to, src)


def low(eng, to, src, hi):
    return eng.tensor_tensor(to, src, hi.bitcast(F32), ALU.subtract)


class Stage:

    def __init__(self, nc, name):
        self.nc, self.name, self.stack, self.sems, self.n = nc, name, ExitStack(), [], 0

    def __enter__(self):
        return self

    def sb(self, name, shape, dt=F32, side="left"):
        return self.stack.enter_context(self.nc.sbuf_tensor(f"{self.name}_{name}", shape, dt, side=side))

    def ps(self, name, shape=(P, 512), dt=F32):
        return self.stack.enter_context(self.nc.psum_tensor(f"{self.name}_{name}", list(shape), dt))

    def sem(self, name):
        s = self.stack.enter_context(self.nc.semaphore(f"{self.name}_{name}"))
        self.sems.append(s)
        return s

    def clear(self):
        for s in self.sems:
            self.nc.sync.sem_clear(s)
        self.nc.all_engine_barrier()

    def __exit__(self, *a):
        if a[0] is None:
            self.clear()
        self.stack.close()


def cols(v):
    return v.rearrange("(k p) -> p k", p=P)


def adaln_stage(nc, ap, pre, keep):
    name = "ada" + pre
    with Stage(nc, name) as st:
        w = st.sb("w", [P, KT, 3 * D])
        cc = st.sb("cc", [P, KT, 2])
        sc = st.sb("sc", [P, KT, 2])
        wide = st.sb("wide", [P, KT, 2, P])
        bcol = st.sb("bcol", [P, 16])
        gcol = st.sb("gcol", [P, KT])
        brow = st.sb("brow", [P, D])
        pc = st.ps("pc")
        pg = [st.ps(f"pg{i}") for i in range(4)]
        w_in, small_in, silu, spread, cols_mm, gate_mm, dve_seq = (st.sem(n) for n in (
            "w_in", "small_in", "silu", "spread", "cols_mm", "gate_mm", "dve_seq"))
        wd = ap[pre + "_ada_w"][0].rearrange("(k p) n -> p k n", p=P)
        modA, modB, gate = keep
        with nc.Block() as block:
            @block.sync
            def _(sp):
                sp.dma_start(cc[:, :, 0], cols(ap["c"][0]), allow_slow_non_contiguous=True).then_inc(small_in, 16)
                sp.dma_start(cc[:, :, 1], cols(ap["c_ctx"]), allow_slow_non_contiguous=True).then_inc(small_in, 16)
                for k in range(KT):
                    sp.dma_start(w[:, k, :], wd[:, k, :]).then_inc(w_in, 16)
                sp.dma_start(bcol[:, :], cols(ap[pre + "_ada_b"][0][0:2 * D]), allow_slow_non_contiguous=True).then_inc(small_in, 16)
                sp.dma_start(gcol[:, :], cols(ap[pre + "_norm"][0]), allow_slow_non_contiguous=True).then_inc(small_in, 16)
                sp.dma_start(brow[:, :], ap[pre + "_ada_b"][0][2 * D:3 * D].partition_broadcast(P)).then_inc(small_in, 16)

            @block.scalar
            def _(act):
                act.wait_ge(small_in, 80)
                nc.scalar.activation(sc[:, :, :], cc[:, :, :], ACT.Silu).then_inc(silu, 1)

            @block.tensor
            def _(pe):
                pe.wait_ge(silu, 1)
                pe.wait_ge(w_in, 16 * KT)
                for n in range(16):
                    for k in range(KT):
                        mm = pe.matmul(pc[:, 2 * n:2 * n + 2], w[:, k, n * P:(n + 1) * P], sc[:, k, :],
                                       start=(k == 0), stop=(k == KT - 1))
                mm.then_inc(cols_mm, 1)
                pe.wait_ge(spread, 1)
                for v in range(2):
                    for h in range(2):
                        for k in range(KT):
                            mm = pe.matmul(pg[2 * v + h][:, :], wide[:, k, v, :],
                                           w[:, k, 2 * D + 512 * h:2 * D + 512 * (h + 1)],
                                           start=(k == 0), stop=(k == KT - 1))
                mm.then_inc(gate_mm, 1)

            @block.vector
            def _(dve):
                link = Linked(dve, dve_seq)
                dve.wait_ge(silu, 1)
                dve.tensor_copy(wide[:, :, :, :], sc[:, :, :].unsqueeze(3).to_broadcast([P, KT, 2, P])).then_inc(spread, 1)
                dve.wait_ge(small_in, 80)
                dve.wait_ge(cols_mm, 1)
                pcv = pc[:, 0:32].rearrange("p (n v) -> p v n", v=2)
                for v in range(2):
                    link(dve.tensor_tensor(modB[:, v, :], pcv[:, v, 0:8], bcol[:, 0:8], ALU.add))
                    link(dve.tensor_tensor(modA[:, v, :], pcv[:, v, 8:16], bcol[:, 8:16], ALU.add))
                    link(dve.tensor_scalar(modA[:, v, :], modA[:, v, :], 1.0, None, ALU.add))
                    link(dve.tensor_tensor(modA[:, v, :], modA[:, v, :], gcol[:, :], ALU.mult))
                dve.wait_ge(gate_mm, 1)
                for v in range(2):
                    for h in range(2):
                        s = slice(512 * h, 512 * h + 512)
                        link(dve.tensor_tensor(gate[:, v, s], pg[2 * v + h][:, :], brow[:, s], ALU.add))


def split_blocks(nc, dve, xT, xf, i, evac, split):
    n = 0
    for p in range(2):
        to = bass.ds(i * 2 * P + p * P, P)
        for b in range(2):
            ks = slice(4 * b, 4 * b + 4)
            dve.wait_ge(evac, 8 * p + 4 * b + 4)
            high(dve, xT[0][:, ks, to], xf[:, p, ks, :]).then_inc(split, 1)
            n += 1
            dve.wait_ge(split, n)
            low(dve, xT[1][:, ks, to], xf[:, p, ks, :], xT[0][:, ks, to]).then_inc(split, 1)
            n += 1


def norm_stage(nc, name, ident, tiles, xT, x_of, y_of=None, gate=None, y_row=None, z_row=None, z_out=None,
               modA=None, modB=None):
    lo, hi = tiles
    with Stage(nc, name) as st:
        x = [st.sb(f"x{p}", [P, D]) for p in range(2)]
        y = [st.sb(f"y{p}", [P, D]) for p in range(2)] if y_of else None
        sq = st.sb("sq", [P, D])
        t = [st.sb(f"t{p}", [P, D]) for p in range(2)]
        row = st.sb("row", [P, D])
        xf = st.sb("xf", [P, 2, KT, P]) if xT else None
        ss = st.sb("ss", [P, 8])
        rs = st.sb("rs", [P, 8])
        pt = [st.ps(f"pt{i}") for i in range(4)]
        loaded = [st.sem(f"loaded{p}") for p in range(2)]
        row_in = st.sem("row_in")
        z_ready, ss_ready, ms_ready, rt_ready, xn_ready, trans, evac, stored, dve_seq, zz = (st.sem(n) for n in (
            "z_ready", "ss_ready", "ms_ready", "rt_ready", "xn_ready", "trans", "evac", "stored", "dve_seq", "zz"))
        split = st.sem("split")
        rms_of = []
        for p in range(2):
            if y_row is not None:
                rms_of.append((p, "y"))
            if z_row is not None:
                rms_of.append((p, "z"))
            if xT is not None:
                rms_of.append((p, "n"))
        rowsrc = y_row if y_row is not None else z_row
        if rowsrc is not None:
            with nc.Block() as block:
                @block.sync
                def _(sp):
                    sp.dma_start(row[:, :], rowsrc.partition_broadcast(P)).then_inc(row_in, 16)
                    sp.wait_ge(row_in, 16)
        with nc.Fori(lo, hi) as i:
            with nc.Block() as block:
                nload = 32 if y_of else 16

                @block.sync
                def _(sp):
                    for p in range(2):
                        sp.dma_start(x[p][:, :], x_of(i, p)).then_inc(loaded[p], 16)
                        if y_of:
                            sp.dma_start(y[p][:, :], y_of(i, p)).then_inc(loaded[p], 16)
                    if z_out:
                        for p in range(2):
                            sp.wait_ge(zz, p + 1)
                            sp.dma_start(z_out(i, p), x[p][:, :]).then_inc(stored, 16)
                        sp.wait_ge(stored, 32)

                @block.scalar
                def _(act):
                    for n, (p, what) in enumerate(rms_of):
                        src = y[p] if what == "y" else x[p]
                        act.wait_ge(loaded[p], nload)
                        act.wait_ge(z_ready, n + 1)
                        nc.scalar.activation(sq[:, :], src[:, :], ACT.Square, accum_out=ss[:, n:n + 1]).then_inc(ss_ready, 1)
                        act.wait_ge(ms_ready, n + 1)
                        nc.scalar.activation(rs[:, n:n + 1], ss[:, n:n + 1], ACT.Sqrt).then_inc(rt_ready, 1)
                        if what == "n":
                            for b in range(2):
                                act.wait_ge(trans, 2 * p + b + 1)
                                for k in range(4 * b, 4 * b + 4, 1):
                                    nc.scalar.activation(
                                        xf[:, p, k, :], pt[2 * p + b][:, (k % 4) * P:(k % 4 + 1) * P],
                                        ACT.Identity, scale=modA[:, k:k + 1],
                                        bias=(modB[:, k:k + 1] if modB is not None else 0.0)).then_inc(evac, 1)

                @block.tensor
                def _(pe):
                    if xT is not None:
                        for p in range(2):
                            pe.wait_ge(xn_ready, p + 1)
                            for b in range(2):
                                for k in range(4):
                                    mm = pe.transpose(pt[2 * p + b][:, k * P:(k + 1) * P],
                                                      t[p][:, (4 * b + k) * P:(4 * b + k + 1) * P], ident[:, :])
                                mm.then_inc(trans, 1)

                @block.vector
                def _(dve):
                    link = Linked(dve, dve_seq)
                    n = 0

                    def rstd(n):
                        dve.wait_ge(ss_ready, n + 1)
                        dve.tensor_scalar(ss[:, n:n + 1], ss[:, n:n + 1], 1.0 / D, NORM_EPS, ALU.mult, ALU.add).then_inc(ms_ready, 1)
                        dve.wait_ge(rt_ready, n + 1)
                        link(dve.reciprocal(rs[:, n:n + 1], rs[:, n:n + 1]))

                    for p in range(2):
                        dve.wait_ge(loaded[p], nload)
                        if gate is not None:
                            link(dve.tensor_tensor(t[p][:, :], y[p][:, :], gate[:, :], ALU.mult))
                            link(dve.tensor_tensor(x[p][:, :], x[p][:, :], t[p][:, :], ALU.add))
                        if y_row is not None:
                            dve.sem_inc(z_ready, 1)
                            rstd(n)
                            link(dve.scalar_tensor_tensor(out=t[p][:, :], in0=y[p][:, :], scalar=rs[:, n:n + 1],
                                                          in1=row[:, :], op0=ALU.mult, op1=ALU.mult))
                            link(dve.tensor_tensor(x[p][:, :], x[p][:, :], t[p][:, :], ALU.add))
                            n += 1
                        if z_row is not None:
                            dve.sem_inc(z_ready, 1)
                            rstd(n)
                            link(dve.scalar_tensor_tensor(out=x[p][:, :], in0=x[p][:, :], scalar=rs[:, n:n + 1],
                                                          in1=row[:, :], op0=ALU.mult, op1=ALU.mult))
                            n += 1
                        if z_out:
                            dve.sem_inc(zz, 1)
                        if xT is not None:
                            dve.sem_inc(z_ready, 1)
                            rstd(n)
                            dve.tensor_scalar(t[p][:, :], x[p][:, :], rs[:, n:n + 1], None, ALU.mult).then_inc(xn_ready, 1)
                            n += 1
                    if xT is not None:
                        split_blocks(nc, dve, xT, xf, i, evac, split)
            st.clear()


def gemm_stage(nc, name, xT, kt, mt, w_of, nb, wn, out_of):
    R = 4 if mt % 4 == 0 else 5
    per = mt // R
    G = 4
    kg = kt // G
    with Stage(nc, name) as st:
        w = st.sb("w", [P, kt, wn])
        wh = [st.sb(f"wh{b}", [P, kt, wn], F32R) for b in range(2)]
        wl = [st.sb(f"wl{b}", [P, kt, wn], F32R) for b in range(2)]
        o = [st.sb(f"o{r}", [P, wn]) for r in range(R)]
        acc = [st.ps(f"acc{r}") for r in range(R)]
        w_in, high_out, low_out = st.sem("w_in"), st.sem("high_out"), st.sem("low_out")
        summed = [st.sem(f"summed{r}") for r in range(R)]
        emptied = [st.sem(f"emptied{r}") for r in range(R)]
        stored = [st.sem(f"stored{r}") for r in range(R)]
        with nc.Block() as block:
            @block.sync
            def _(sp):
                sp.dma_start(w[:, :, :], w_of(0, 0)).then_inc(w_in, 16)
                for r in range(R):
                    sp.sem_inc(stored[r], 16)

                def block_of(j, b, following):
                    for m in range(mt):
                        r = m % R
                        sp.wait_ge(emptied[r], (j * 2 + b) * per + m // R + 2)
                        sp.dma_start(out_of(j, b, m), o[r][:, :]).then_inc(stored[r], 16)
                        if m == 0 and following is not None:
                            sp.dma_start(w[:, :, :], w_of(*following)).then_inc(w_in, 16)

                if nb > 1:
                    with sp.Fori(0, nb - 1) as j:
                        block_of(j, 0, (j, 1))
                        block_of(j, 1, (j + 1, 0))
                block_of(nb - 1, 0, (nb - 1, 1))
                block_of(nb - 1, 1, None)
                for r in range(R):
                    sp.wait_ge(stored[r], 16 * (2 * nb * per + 1))

            @block.tensor
            def _(pe):
                for r in range(R):
                    pe.sem_inc(emptied[r], 1)
                with pe.Fori(0, nb) as j:
                    for b in range(2):
                        for m in range(mt):
                            r = m % R
                            pe.wait_ge(emptied[r], (j * 2 + b) * per + m // R + 1)
                            for k in range(kt):
                                if m == 0 and k % kg == 0:
                                    pe.wait_ge(low_out, (j * 2 + b) * G + k // kg + 1)
                                for n, (x, v) in enumerate(((0, wh), (0, wl), (1, wh))):
                                    mm = pe.matmul(acc[r][:, 0:wn], xT[x][:, k, m * P:(m + 1) * P], v[b][:, k, :],
                                                   start=(k == 0 and n == 0), stop=(k == kt - 1 and n == 2))
                            mm.then_inc(summed[r], 1)

            def evacuate(eng, j, b, m):
                r = m % R
                eng.wait_ge(summed[r], (j * 2 + b) * per + m // R + 1)
                eng.wait_ge(stored[r], (j * 2 + b) * per * 16 + m // R * 16 + 16)

            def program(eng, odd, evac, split):
                split(0, 0)

                def block_of(j, b, following):
                    mine = [m for m in range(mt) if m % 2 == odd]
                    for n, m in enumerate(mine):
                        evacuate(eng, j, b, m)
                        evac(j, b, m)
                        if n == 1 and following is not None:
                            split(*following)

                if nb > 1:
                    with eng.Fori(0, nb - 1) as j:
                        block_of(j, 0, (j, 1))
                        block_of(j, 1, (j + 1, 0))
                block_of(nb - 1, 0, (nb - 1, 1))
                block_of(nb - 1, 1, None)

            @block.scalar
            def _(act):
                def split(j, b):
                    act.wait_ge(w_in, (j * 2 + b) * 16 + 16)
                    for g in range(G):
                        ks = slice(g * kg, (g + 1) * kg)
                        nc.scalar.copy(wh[b][:, ks, :], w[:, ks, :]).then_inc(high_out, 1)

                def evac(j, b, m):
                    nc.scalar.copy(o[m % R][:, :], acc[m % R][:, 0:wn]).then_inc(emptied[m % R], 1)

                program(act, 1, evac, split)

            @block.vector
            def _(dve):
                def split(j, b):
                    for g in range(G):
                        ks = slice(g * kg, (g + 1) * kg)
                        dve.wait_ge(high_out, (j * 2 + b) * G + g + 1)
                        low(dve, wl[b][:, ks, :], w[:, ks, :], wh[b][:, ks, :]).then_inc(low_out, 1)

                def evac(j, b, m):
                    dve.tensor_copy(o[m % R][:, :], acc[m % R][:, 0:wn]).then_inc(emptied[m % R], 1)

                program(dve, 0, evac, split)


def attn_prep_stage(nc, ap, ident, U, QT, pairs, rope_rows, row0):
    NH = 10
    lo, hi = pairs
    with Stage(nc, f"prep{lo}") as st:
        u = [st.sb(f"u{p}", [P, 2688]) for p in range(2)]
        sq = st.sb("sq", [P, NH, HD])
        xn = [st.sb(f"xn{p}", [P, NH, HD]) for p in range(2)]
        tmp = st.sb("tmp", [P, NH, HD])
        cs = [st.sb(f"cs{p}", [P, 2, HD]) for p in range(2)]
        gain = st.sb("gain", [P, NH, HD])
        gq = st.sb("gq", [P, 2, HD])
        ss = st.sb("ss", [P, 2, NH])
        tb = st.sb("tb", [P, 13, 2 * P])
        pt = [st.ps(f"pt{i}") for i in range(8)]
        loaded = [st.sem(f"loaded{p}") for p in range(2)]
        gains_in, ss_ready, ms_ready, rt_ready, roped, trans, evac_a, evac_v, stored, dve_seq = (st.sem(n) for n in (
            "gains_in", "ss_ready", "ms_ready", "rt_ready", "roped", "trans", "evac_a", "evac_v", "stored", "dve_seq"))
        with nc.Block() as block:
            @block.sync
            def _(sp):
                sp.dma_start(gq[:, 0, :], ap["gqa_q_gain"][0].partition_broadcast(P)).then_inc(gains_in, 16)
                sp.dma_start(gq[:, 1, :], ap["gqa_k_gain"][0].partition_broadcast(P)).then_inc(gains_in, 16)

            @block.vector
            def _(dve):
                link = Linked(dve, dve_seq)
                dve.wait_ge(gains_in, 32)
                link(dve.tensor_scalar(gain[:, 0:8, :], gq[:, 0:1, :].to_broadcast([P, 8, HD]), HD ** -0.5, None, ALU.mult))
                link(dve.tensor_copy(gain[:, 8:10, :], gq[:, 1:2, :].to_broadcast([P, 2, HD])))
        st.clear()
        SRC = [c * P for c in range(8)]
        with nc.Fori(lo, hi) as i:
            with nc.Block() as block:
                @block.sync
                def _(sp):
                    for p in range(2):
                        sp.dma_start(u[p][:, 0:1024], U.rearrange("(n q p) d -> n q p d", q=2, p=P)[i, p][:, 0:1024]).then_inc(loaded[p], 16)
                        sp.dma_start(u[p][:, 2048:2688], U.rearrange("(n q p) d -> n q p d", q=2, p=P)[i, p][:, 2048:2688]).then_inc(loaded[p], 16)
                        sp.dma_start(cs[p][:, :, :], ap["rope"].rearrange("(n q p) a d -> n q p a d", q=2, p=P)[i, p]).then_inc(loaded[p], 16)
                    sp.wait_ge(evac_a, 4)
                    sp.wait_ge(evac_v, 4)
                    sp.dma_start(QT.rearrange("(b p) (n t) -> n p b t", p=P, t=2 * P)[i], tb[:, :, :]).then_inc(stored, 16)
                    sp.wait_ge(stored, 16)

                @block.scalar
                def _(act):
                    for p in range(2):
                        act.wait_ge(loaded[p], 48)
                        if p:
                            act.wait_ge(ms_ready, p)
                        nc.scalar.activation(sq[:, :, :], u[p][:, 2048:2688].rearrange("p (h d) -> p h d", d=HD), ACT.Square).then_inc(ss_ready, 1)
                        act.wait_ge(ms_ready, p + 1)
                        nc.scalar.activation(ss[:, p, :], ss[:, p, :], ACT.Sqrt).then_inc(rt_ready, 1)
                    for p in range(2):
                        for b in range(2):
                            act.wait_ge(trans, 2 * p + b + 1)
                            nc.scalar.mul(tb[:, 4 * b:4 * b + 4, p * P:(p + 1) * P],
                                          pt[4 * p + b][:, :].rearrange("p (b t) -> p b t", t=P),
                                          HD ** -0.5 if b == 0 else 1.0).then_inc(evac_a, 1)

                @block.tensor
                def _(pe):
                    for p in range(2):
                        pe.wait_ge(loaded[p], 48)
                        for b in range(2):
                            for k in range(4):
                                mm = pe.transpose(pt[4 * p + b][:, k * P:(k + 1) * P], u[p][:, (4 * b + k) * P:(4 * b + k + 1) * P], ident[:, :])
                            mm.then_inc(trans, 1)
                    for p in range(2):
                        pe.wait_ge(roped, p + 1)
                        xf = xn[p][:, :, :].rearrange("p h d -> p (h d)")
                        for k in range(5):
                            mm = pe.transpose(pt[4 * p + 2 + k // 4][:, (k % 4) * P:(k % 4 + 1) * P], xf[:, k * P:(k + 1) * P], ident[:, :])
                            if k in (3, 4):
                                mm.then_inc(trans, 1)

                @block.vector
                def _(dve):
                    link = Linked(dve, dve_seq)
                    for p in range(2):
                        dve.wait_ge(ss_ready, p + 1)
                        link(dve.tensor_reduce(ss[:, p, :], sq[:, :, :], AX.X, ALU.add))
                        dve.tensor_scalar(ss[:, p, :], ss[:, p, :], 1.0 / HD, NORM_EPS, ALU.mult, ALU.add).then_inc(ms_ready, 1)
                        dve.wait_ge(rt_ready, p + 1)
                        link(dve.reciprocal(ss[:, p, :], ss[:, p, :]))
                        link(dve.tensor_tensor(xn[p][:, :, :], u[p][:, 2048:2688].rearrange("p (h d) -> p h d", d=HD),
                                               ss[:, p, :].unsqueeze(2).to_broadcast([P, NH, HD]), ALU.mult))
                        link(dve.tensor_tensor(xn[p][:, :, :], xn[p][:, :, :], gain[:, :, :], ALU.mult))
                        for a in range(2):
                            for s in range(2):
                                to, of = 32 * a + 16 * s, 32 * a + 16 * (1 - s)
                                dve.tensor_tensor(tmp[:, :, to:to + 16], xn[p][:, :, of:of + 16],
                                                  cs[p][:, 1:2, to:to + 16].to_broadcast([P, NH, 16]), ALU.mult).then_inc(dve_seq, 1)
                                link.n += 1
                        dve.wait_ge(dve_seq, link.n)
                        link(dve.tensor_tensor(xn[p][:, :, :], xn[p][:, :, :], cs[p][:, 0:1, :].to_broadcast([P, NH, HD]), ALU.mult))
                        dve.tensor_tensor(xn[p][:, :, :], xn[p][:, :, :], tmp[:, :, :], ALU.add).then_inc(roped, 1)
                        dve.wait_ge(roped, p + 1)
                    for p in range(2):
                        dve.wait_ge(trans, 4 + 2 * p + 1)
                        dve.tensor_copy(tb[:, 8:12, p * P:(p + 1) * P], pt[4 * p + 2][:, :].rearrange("p (b t) -> p b t", t=P)).then_inc(evac_v, 1)
                        dve.wait_ge(trans, 4 + 2 * p + 2)
                        dve.tensor_copy(tb[:, 12, p * P:(p + 1) * P], pt[4 * p + 3][:, 0:P]).then_inc(evac_v, 1)
            st.clear()


def attention_stage(nc, name, ident, loops, K, nk, units, loads, NLOAD, kv_shared, o_out, window=None, causal=None):
    SMAX = max(sum(n for _, n in u["keys"]) for u in units)
    NB = (SMAX + 511) // 512
    NQ = max(u["q"] for u in units) + P
    NT = (SMAX + P - 1) // P
    with Stage(nc, name) as st:
        qT_all = [st.sb(f"qT{s}", [P, NQ]) for s in range(2)]
        kT_all = [st.sb(f"kT{s}", [P, nk]) for s in range(1 if kv_shared else 2)]
        qT, kT = [q[0:K, :] for q in qT_all], [k[0:K, :] for k in kT_all]
        v = [st.sb(f"v{s}", [P, nk // P, HD]) for s in range(1 if kv_shared else 2)]
        prob = [st.sb(f"prob{s}", [P, SMAX]) for s in range(2)]
        probT = [st.sb(f"probT{s}", [P, NT, P]) for s in range(2)]
        mx = st.sb("mx", [P, 2])
        den = st.sb("den", [P, 2])
        rden = st.sb("rden", [P, 2])
        o = st.sb("o", [P, len(units), 2, HD])
        scores = st.ps("scores", [P, 512 * NB])
        pt = [st.ps(f"pt{i}") for i in range(3)]
        po = [st.ps(f"po{i}") for i in range(2)]
        bufs = dict(qT=qT, kT=kT, v=v)
        if window is not None:
            table = [st.sb(f"table{s}", [P, 18 * HD]) for s in range(2)]
            bias = [st.sb(f"bias{s}", [P, 5, 640]) for s in range(2)]
            mask = st.sb("mask", [P, 5, 640])
            biased = [st.sb(f"biased{s}", [P, SMAX]) for s in range(2)]
            bufs["table"] = table
        if causal is not None:
            mask = st.sb("mask", [P, P])
        const_in = st.sem("const_in")
        loaded = [st.sem(f"loaded{s}") for s in range(2)]
        scored, maxed, probs, trans, turned, summed, normed, stored, dve_seq, bias_ready = (st.sem(n) for n in (
            "scored", "maxed", "probs", "trans", "turned", "summed", "normed", "stored", "dve_seq", "bias_ready"))
        work = [(s, x) for s in range(2) for x in range(len(units))]
        groups = []
        for s, x in work:
            tl = units[x]["tiles"]
            groups.append([list(range(g, min(g + 4, len(tl)))) for g in range(0, len(tl), 4)])
        first = [0]
        for g in groups:
            first.append(first[-1] + len(g))
        zeroed = st.sem("zeroed")
        with nc.Block() as block:
            @block.vector
            def _(dve):
                for t in qT_all + kT_all:
                    dve.memset(t[:, :], 0.0).then_inc(zeroed, 1)
                dve.wait_ge(zeroed, len(qT_all + kT_all))

            if window is not None or causal is not None:
                @block.sync
                def _(sp):
                    if window is not None:
                        sp.dma_start(mask[:, :, :], window.rearrange("c p k -> p c k")).then_inc(const_in, 16)
                    else:
                        sp.dma_start(mask[:, :], causal).then_inc(const_in, 16)
                    sp.wait_ge(const_in, 16)
        loop = ExitStack()
        idx = []
        for n in loops:
            idx.append(loop.enter_context(nc.Fori(0, n)))
        with loop:
            with nc.Block() as block:
                @block.sync
                def _(sp):
                    loads(sp, idx, bufs, loaded)
                    sp.wait_ge(normed, len(work))
                    o_out(sp, idx, o, stored)

                if window is not None:
                    @block.gpsimd
                    def _(pool):
                        for s in range(2):
                            pool.wait_ge(loaded[s], NLOAD[s])
                            for c, off in enumerate((8, 6, 4, 2, 0)):
                                pool.tensor_tensor(bias[s][:, c, :], table[s][:, off * HD:off * HD + 640], mask[:, c, :], ALU.add).then_inc(bias_ready, 1)

                @block.tensor
                def _(pe):
                    def score(w):
                        s, x = work[w]
                        u = units[x]
                        ks = 0 if kv_shared else s
                        pe.wait_ge(loaded[s], NLOAD[s])
                        if kv_shared:
                            pe.wait_ge(loaded[0], NLOAD[0])
                        if w:
                            biased_before = window is not None and units[work[w - 1][1]]["bias"] is not None
                            pe.wait_ge(maxed if biased_before else probs, w)
                        at = 0
                        for c0, n in u["keys"]:
                            while n:
                                m = min(n, 512 - at % 512)
                                mm = pe.matmul(scores[:, at:at + m], qT_all[s][:, u["q"]:u["q"] + P], kT_all[ks][:, c0:c0 + m], start=True, stop=True)
                                at, c0, n = at + m, c0 + m, n - m
                        mm.then_inc(scored, 1)

                    def mix(w):
                        s, x = work[w]
                        u = units[x]
                        ks = 0 if kv_shared else s
                        pe.wait_ge(probs, w + 1)
                        if w >= 2:
                            pe.wait_ge(normed, w - 1)
                        for g, tl in enumerate(groups[w]):
                            n = first[w] + g
                            if n >= 3:
                                pe.wait_ge(turned, n - 2)
                            for a, t in enumerate(tl):
                                mm = pe.transpose(pt[n % 3][:, a * P:(a + 1) * P], prob[w % 2][:, t * P:(t + 1) * P], ident[:, :])
                            mm.then_inc(trans, 1)
                        for g, tl in enumerate(groups[w]):
                            pe.wait_ge(turned, first[w] + g + 1)
                            for t in tl:
                                mm = pe.matmul(po[w % 2][:, 0:HD], probT[w % 2][:, t, :], v[ks][:, u["tiles"][t], :],
                                               start=(t == 0), stop=(t == len(u["tiles"]) - 1))
                        mm.then_inc(summed, 1)

                    for w in range(len(work) + 1):
                        if w < len(work):
                            score(w)
                        if w:
                            mix(w - 1)

                @block.scalar
                def _(act):
                    def softmax(w):
                        s, x = work[w]
                        n = sum(m for _, m in units[x]["keys"])
                        act.wait_ge(maxed, w + 1)
                        if w >= 2:
                            act.wait_ge(trans, first[w - 1])
                            act.wait_ge(normed, w - 1)
                        src = biased[w % 2] if window is not None and units[x]["bias"] is not None else scores
                        nc.scalar.activation(prob[w % 2][:, 0:n], src[:, 0:n], ACT.Exp, bias=mx[:, w % 2:w % 2 + 1],
                                             accum_out=den[:, w % 2:w % 2 + 1]).then_inc(probs, 1)

                    def turn(w):
                        if w >= 2:
                            act.wait_ge(summed, w - 1)
                        for g, tl in enumerate(groups[w]):
                            n = first[w] + g
                            act.wait_ge(trans, n + 1)
                            nc.scalar.copy(probT[w % 2][:, tl[0]:tl[-1] + 1, :],
                                           pt[n % 3][:, 0:len(tl) * P].rearrange("p (b t) -> p b t", t=P)).then_inc(turned, 1)

                    for w in range(len(work) + 1):
                        if w:
                            turn(w - 1)
                        if w < len(work):
                            softmax(w)

                @block.vector
                def _(dve):
                    link = Linked(dve, dve_seq)

                    def maximum(w):
                        s, x = work[w]
                        u = units[x]
                        n = sum(m for _, m in u["keys"])
                        dve.wait_ge(scored, w + 1)
                        src = scores
                        if window is not None and u["bias"] is not None:
                            if w >= 2:
                                dve.wait_ge(probs, w - 1)
                            dve.wait_ge(bias_ready, 5 * (s + 1))
                            src = biased[w % 2]
                            dve.tensor_tensor(src[:, 0:640], scores[:, 0:640], bias[s][:, u["bias"], :], ALU.add).then_inc(dve_seq, 1)
                            link.n += 1
                            link(dve.tensor_copy(src[:, 640:n], scores[:, 640:n]))
                        if causal is not None:
                            link(dve.tensor_tensor(scores[:, n - P:n], scores[:, n - P:n], mask[:, :], ALU.add))
                        if w >= 2:
                            dve.wait_ge(probs, w - 1)
                        link(dve.tensor_reduce(mx[:, w % 2:w % 2 + 1], src[:, 0:n], AX.X, ALU.max))
                        dve.tensor_scalar(mx[:, w % 2:w % 2 + 1], mx[:, w % 2:w % 2 + 1], -1.0, None, ALU.mult).then_inc(maxed, 1)

                    def normalize(w):
                        s, x = work[w]
                        dve.wait_ge(probs, w + 1)
                        link(dve.reciprocal(rden[:, w % 2:w % 2 + 1], den[:, w % 2:w % 2 + 1]))
                        dve.wait_ge(summed, w + 1)
                        dve.tensor_scalar(o[:, x, s, :], po[w % 2][:, 0:HD], rden[:, w % 2:w % 2 + 1], None, ALU.mult).then_inc(normed, 1)

                    for w in range(len(work) + 1):
                        if w < len(work):
                            maximum(w)
                        if w:
                            normalize(w - 1)
            st.clear()


PADR = 19


def window_table_stage(nc, ap, REP):
    with Stage(nc, "pad") as st:
        pad = st.sb("pad", [HEADS, PADR, P])
        zeroed, filled, stored = (st.sem(n) for n in ("zeroed", "filled", "stored"))
        with nc.Block() as block:
            @block.vector
            def _(dve):
                dve.memset(pad[:, :, :], 0.0).then_inc(zeroed, 1)

            @block.sync
            def _(sp):
                sp.wait_ge(zeroed, 1)
                sp.dma_start(pad[:, 2:17, 48:79], ap["na_rpb"][0]).then_inc(filled, 16)
                sp.wait_ge(filled, 16)
                for r in range(PADR):
                    sp.dma_start(REP[:, r], pad[:, r:r + 1, :].to_broadcast([HEADS, HD, P])).then_inc(stored, 16)
                sp.wait_ge(stored, 16 * PADR)


def na_stage(nc, ap, ident, U, QT, REP, O):
    start = [min(max(i - 2, 0), 3) for i in range(LT)]
    kind = [{8: 0, 6: 1, 4: 2, 2: 3, 0: 4}[2 * s - 2 * i + 8] for i, s in enumerate(start)]
    units = [dict(q=i * P, keys=[(s * P, 640), (LAT, CTX)], tiles=[s + a for a in range(5)] + [8, 9], bias=k)
             for i, (s, k) in enumerate(zip(start, kind))]
    units += [dict(q=LAT + i * P, keys=[(LAT, CTX)], tiles=[8, 9], bias=None) for i in range(CT)]
    qv = QT[0:HW, :].rearrange("(j s d) t -> j s d t", s=2, d=HD)
    kv = QT[HW:2 * HW, :].rearrange("(j s d) t -> j s d t", s=2, d=HD)
    vv = U[:, 1024:1536].rearrange("(m p) (j s d) -> j s p m d", p=P, s=2, d=HD)
    tables = [bass.AP(tensor=REP.tensor, offset=(1 - r) * HD * P + HD - 1,
                      ap=[[2 * PADR * HD * P, 4], [PADR * HD * P, 2], [P - 1, HD], [HD * P, 18], [1, HD]]) for r in range(2)]

    def loads(sp, idx, b, loaded):
        (j,) = idx
        for s in range(2):
            sp.dma_start(b["qT"][s][:, :], qv[j, s]).then_inc(loaded[s], 16)
            sp.dma_start(b["kT"][s][:, :], kv[j, s]).then_inc(loaded[s], 16)
            sp.dma_start(b["v"][s][:, :, :], vv[j, s]).then_inc(loaded[s], 16)
            for r in range(2):
                sp.dma_start(b["table"][s][HD * r:HD * (r + 1), :].rearrange("p (j k) -> p j k", k=HD), tables[r][j, s]).then_inc(loaded[s], 16)

    ov = O[:, 0:HW].rearrange("(x p) (j s d) -> j p x s d", p=P, s=2, d=HD)

    def out(sp, idx, o, stored):
        (j,) = idx
        sp.dma_start(ov[j], o[:, :, :, :]).then_inc(stored, 16)
        sp.wait_ge(stored, 16)

    attention_stage(nc, "na", ident, [4], HD, TOK, units, loads, [80, 80], False, out, window=ap["window_mask"])


def gqa_stage(nc, ap, ident, U, QT, O):
    units = [dict(q=i * P, keys=[(0, TOK)], tiles=list(range(10)), bias=None) for i in range(LT)]
    units += [dict(q=LAT + i * P, keys=[(LAT, CTX)], tiles=[8, 9], bias=None) for i in range(CT)]
    qv = QT[2 * HW:3 * HW, :].rearrange("(g j s d) t -> g j s d t", j=2, s=2, d=HD)
    kv = QT[3 * HW:3 * HW + 2 * HD, :].rearrange("(g d) t -> g d t", d=HD)
    vv = U[:, 2688:2816].rearrange("(m p) (g d) -> g p m d", p=P, d=HD)

    def loads(sp, idx, b, loaded):
        g, j = idx
        sp.dma_start(b["kT"][0][:, :], kv[g]).then_inc(loaded[0], 16)
        sp.dma_start(b["v"][0][:, :, :], vv[g]).then_inc(loaded[0], 16)
        for s in range(2):
            sp.dma_start(b["qT"][s][:, :], qv[g, j, s]).then_inc(loaded[s], 16)

    ov = O[:, HW:2 * HW].rearrange("(x p) (g j s d) -> g j p x s d", p=P, j=2, s=2, d=HD)

    def out(sp, idx, o, stored):
        g, j = idx
        sp.dma_start(ov[g, j], o[:, :, :, :]).then_inc(stored, 16)
        sp.wait_ge(stored, 16)

    attention_stage(nc, "gqa", ident, [2, 2], HD, TOK, units, loads, [48, 16], True, out)


def rope_table():
    t = np.arange(LAT)
    pos = np.stack([t // 64, t % 64], -1).astype(np.float32)
    inv = (np.float32(10000.0) ** (-np.arange(16, dtype=np.float32) / np.float32(16))).astype(np.float32)
    ang = (pos[:, :, None] * inv).astype(np.float32)
    c, s = np.cos(ang), np.sin(ang)
    out = np.zeros((TOK, 2, 2, 2, 16), np.float32)
    out[:, 0] = 1.0
    out[:LAT, 0] = c[:, :, None, :]
    out[:LAT, 1, :, 0], out[:LAT, 1, :, 1] = -s, s
    return out.reshape(TOK, 2, HD)


def window_mask():
    out = np.full((5, P, 640), -1e30, np.float32)
    for k, i in enumerate((0, 1, 3, 6, 7)):
        s = min(max(i - 2, 0), 3)
        for p in range(P):
            qr, qc = 2 * i + p // 64, p % 64
            r0, c0 = min(max(qr - 4, 0), 8), min(max(qc - 8, 0), 48)
            for r in range(10):
                if r0 <= 2 * s + r < r0 + 8:
                    out[k, p, 64 * r + c0:64 * r + c0 + 16] = 0.0
    return out


def gated_stage(nc, name, ident, tiles, xT, o_of, gates_of):
    with Stage(nc, name) as st:
        o = [st.sb(f"o{p}", [P, D]) for p in range(2)]
        g = [st.sb(f"g{p}", [P, D]) for p in range(2)]
        pt = [st.ps(f"pt{i}") for i in range(4)]
        loaded = [st.sem(f"loaded{p}") for p in range(2)]
        silu, gated, trans, evac, split = (st.sem(n) for n in ("silu", "gated", "trans", "evac", "split"))
        with nc.Fori(*tiles) as i:
            with nc.Block() as block:
                @block.sync
                def _(sp):
                    for p in range(2):
                        sp.dma_start(g[p][:, 0:HW], gates_of(0)(i, p)).then_inc(loaded[p], 16)
                        sp.dma_start(g[p][:, HW:D], gates_of(1)(i, p)).then_inc(loaded[p], 16)
                        sp.dma_start(o[p][:, :], o_of(i, p)).then_inc(loaded[p], 16)

                @block.scalar
                def _(act):
                    for p in range(2):
                        act.wait_ge(loaded[p], 48)
                        nc.scalar.activation(g[p][:, :], g[p][:, :], ACT.Silu).then_inc(silu, 1)
                    for p in range(2):
                        act.wait_ge(trans, 2 * p + 1)
                        nc.scalar.copy(xT[0][:, 0:4, bass.ds(i * 2 * P + p * P, P)],
                                       pt[2 * p][:, :].rearrange("p (b t) -> p b t", t=P)).then_inc(evac, 1)

                @block.vector
                def _(dve):
                    for p in range(2):
                        dve.wait_ge(silu, p + 1)
                        dve.wait_ge(loaded[p], 48)
                        dve.tensor_tensor(o[p][:, :], o[p][:, :], g[p][:, :], ALU.mult).then_inc(gated, 1)
                    for p in range(2):
                        to = bass.ds(i * 2 * P + p * P, P)
                        dve.wait_ge(trans, 2 * p + 2)
                        high(dve, xT[0][:, 4:8, to], pt[2 * p + 1][:, :].rearrange("p (b t) -> p b t", t=P)).then_inc(split, 1)
                        for b in range(2):
                            if b:
                                dve.wait_ge(split, p + 1)
                            else:
                                dve.wait_ge(evac, p + 1)
                            low(dve, xT[1][:, 4 * b:4 * b + 4, to], pt[2 * p + b][:, :].rearrange("p (b t) -> p b t", t=P),
                                xT[0][:, 4 * b:4 * b + 4, to])

                @block.tensor
                def _(pe):
                    for p in range(2):
                        pe.wait_ge(gated, p + 1)
                        for b in range(2):
                            for k in range(4):
                                mm = pe.transpose(pt[2 * p + b][:, k * P:(k + 1) * P], o[p][:, (4 * b + k) * P:(4 * b + k + 1) * P], ident[:, :])
                            mm.then_inc(trans, 1)
            st.clear()


LAT0, CTX0, PAD_ROWS = 1, LAT + 2, (0, LAT + 1, LAT + CTX + 2)
U2_ROWS = LAT + CTX + 3
RW = 1664
NF = 9
C = 64
NCH = TOK // C
CCH = CTX // C


def zero_rows_stage(nc, U2):
    with Stage(nc, "zero") as st:
        z = st.sb("z", [1, REC_IN])
        zeroed, stored = st.sem("zeroed"), st.sem("stored")
        with nc.Block() as block:
            @block.vector
            def _(dve):
                dve.memset(z[:, :], 0.0).then_inc(zeroed, 1)

            @block.sync
            def _(sp):
                sp.wait_ge(zeroed, 1)
                for r in PAD_ROWS:
                    sp.dma_start(U2[r:r + 1, :], z[:, :]).then_inc(stored, 16)
                sp.wait_ge(stored, 48)


def rwkv_feature_stage(nc, ap, ident, U2, FE, segments):
    with Stage(nc, "feat") as st:
        u = [st.sb(f"u{a}", [P, RW]) for a in range(3)]
        s = st.sb("s", [P, RW])
        mu = st.sb("mu", [P, RW])
        lora = st.sb("lora", [P, P])
        loraT = st.sb("loraT", [P, P])
        wup = st.sb("wup", [P, 4, HW])
        w0 = st.sb("w0", [P, 4, HW])
        kk_row = st.sb("kk_row", [P, HW])
        ka_row = st.sb("ka_row", [P, HW])
        z = st.sb("z", [P, 4, HW])
        f = st.sb("f", [P, NF, HW])
        sq = st.sb("sq", [P, HW])
        ss = st.sb("ss", [P, HEADS])
        pt = st.ps("pt")
        pz = [st.ps(f"pz{m}") for m in range(4)]
        names = ("const_in", "zeroed", "loaded", "shifted", "tanh", "trans", "turned", "lora_mm", "biased", "gates",
                 "sq_in", "sq_out", "ms_ready", "rt_ready", "done", "stored", "dve_seq")
        (const_in, zeroed, loaded, shifted, tanh, trans, turned, lora_mm, biased, gates,
         sq_in, sq_out, ms_ready, rt_ready, done, stored, dve_seq) = (st.sem(n) for n in names)
        with nc.Block() as block:
            @block.vector
            def _(dve):
                dve.memset(wup[:, :, :], 0.0).then_inc(zeroed, 1)

            @block.sync
            def _(sp):
                sp.dma_start(mu[:, :], ap["rwkv_mu"][0].partition_broadcast(P)).then_inc(const_in, 16)
                sp.dma_start(kk_row[:, :], ap["rwkv_k_k"][0].partition_broadcast(P)).then_inc(const_in, 16)
                sp.dma_start(ka_row[:, :], ap["rwkv_k_a"][0].partition_broadcast(P)).then_inc(const_in, 16)
                sp.wait_ge(zeroed, 1)
                for d in range(2):
                    for q, (wn, bn) in enumerate((("rwkv_w_up", "rwkv_w0"), ("rwkv_a_up", "rwkv_a0"))):
                        m = 2 * q + d
                        sp.dma_start(wup[32 * m:32 * m + 32, m, :], ap[wn][0, d]).then_inc(const_in, 16)
                        sp.dma_start(w0[:, m, :], ap[bn][0, d].partition_broadcast(P)).then_inc(const_in, 16)
                sp.wait_ge(const_in, 16 * 11)
        st.clear()
        for tiles, row0, out0 in segments:
            with nc.Fori(0, tiles) as i:
                with nc.Block() as block:
                    @block.sync
                    def _(sp):
                        for a in range(3):
                            src = U2[row0 + a - 1:row0 + a - 1 + tiles * P, 0:RW].rearrange("(n p) d -> n p d", p=P)
                            sp.dma_start(u[a][:, :], src[i]).then_inc(loaded, 16)
                        sp.wait_ge(done, 1)
                        dst = FE[out0:out0 + tiles * P].rearrange("(n p) b (x d) -> n p b x d", p=P, d=HD)
                        heads = f[:, :, :].rearrange("p f (a b d) -> p b (f a) d", b=2, d=HD)
                        for b in range(2):
                            sp.dma_start(dst[i][:, b], heads[:, b]).then_inc(stored, 16)
                        sp.wait_ge(stored, 32)

                    @block.scalar
                    def _(act):
                        act.wait_ge(shifted, 1)
                        nc.scalar.activation(lora[:, 0:64], s[:, 1536:1600], ACT.Tanh)
                        nc.scalar.copy(lora[:, 64:128], s[:, 1600:1664]).then_inc(tanh, 1)
                        act.wait_ge(trans, 1)
                        nc.scalar.copy(loraT[:, :], pt[:, 0:P]).then_inc(turned, 1)
                        nc.scalar.copy(f[:, 0, :], s[:, 0:512])
                        nc.scalar.copy(f[:, 1, :], s[:, 1024:1536])
                        act.wait_ge(sq_in, 1)
                        nc.scalar.activation(sq[:, :], f[:, 2, :], ACT.Square).then_inc(sq_out, 1)
                        act.wait_ge(ms_ready, 1)
                        nc.scalar.activation(ss[:, :], ss[:, :], ACT.Sqrt).then_inc(rt_ready, 1)
                        act.wait_ge(biased, 1)
                        nc.scalar.activation(z[:, :, :], z[:, :, :], ACT.Sigmoid).then_inc(gates, 1)

                    @block.tensor
                    def _(pe):
                        pe.wait_ge(tanh, 1)
                        pe.transpose(pt[:, 0:P], lora[:, :], ident[:, :]).then_inc(trans, 1)
                        pe.wait_ge(turned, 1)
                        for m in range(4):
                            mm = pe.matmul(pz[m][:, :], loraT[:, :], wup[:, m, :], start=True, stop=True)
                        mm.then_inc(lora_mm, 1)

                    @block.vector
                    def _(dve):
                        link = Linked(dve, dve_seq)
                        dve.wait_ge(loaded, 48)
                        link(dve.tensor_tensor(s[:, :], u[0][:, :], u[2][:, :], ALU.add))
                        link(dve.scalar_tensor_tensor(out=s[:, :], in0=s[:, :], scalar=0.5, in1=u[1][:, :], op0=ALU.mult, op1=ALU.subtract))
                        link(dve.tensor_tensor(s[:, :], s[:, :], mu[:, :], ALU.mult))
                        dve.tensor_tensor(s[:, :], s[:, :], u[1][:, :], ALU.add).then_inc(shifted, 1)
                        dve.wait_ge(shifted, 1)
                        k = s[:, 512:1024]
                        dve.tensor_tensor(f[:, 2, :], k, kk_row[:, :], ALU.mult).then_inc(sq_in, 1)
                        dve.wait_ge(lora_mm, 1)
                        for m in range(4):
                            ins = dve.tensor_tensor(z[:, m, :], pz[m][:, :], w0[:, m, :], ALU.add)
                        ins.then_inc(biased, 1)
                        dve.wait_ge(sq_out, 1)
                        link(dve.tensor_reduce(ss[:, :], sq[:, :].rearrange("p (h d) -> p h d", d=HD), AX.X, ALU.add))
                        dve.tensor_scalar(ss[:, :], ss[:, :], 1e-12, None, ALU.add).then_inc(ms_ready, 1)
                        dve.wait_ge(rt_ready, 1)
                        link(dve.reciprocal(ss[:, :], ss[:, :]))
                        kk = f[:, 2, :].rearrange("p (h d) -> p h d", d=HD)
                        link(dve.tensor_tensor(kk, kk, ss[:, :].unsqueeze(2).to_broadcast([P, HEADS, HD]), ALU.mult))
                        dve.wait_ge(gates, 1)
                        for d in range(2):
                            dve.tensor_scalar(f[:, 3 + 3 * d, :], z[:, d, :], -float(np.exp(-0.5)), None, ALU.mult)
                            link(dve.tensor_tensor(f[:, 5 + 3 * d, :], f[:, 2, :], z[:, 2 + d, :], ALU.mult))
                            link(dve.scalar_tensor_tensor(out=z[:, 2 + d, :], in0=z[:, 2 + d, :], scalar=-1.0, in1=ka_row[:, :], op0=ALU.add, op1=ALU.mult))
                            link(dve.scalar_tensor_tensor(out=f[:, 4 + 3 * d, :], in0=z[:, 2 + d, :], scalar=1.0, in1=k, op0=ALU.add, op1=ALU.mult))
                        dve.sem_inc(done, 1)
                st.clear()


def rwkv_scan_stage(nc, ap, ident, FE, Y):
    NP2 = HEADS // 2
    W = NP2 * P
    LEV = 6
    with Stage(nc, "scan") as st:
        tri = st.sb("tri", [P, 4, P])
        lev = st.sb("lev", [P, 2, LEV, P])
        lev0 = st.sb("lev0", [P, 2, P])
        keep = st.sb("keep", [P, 2, 2, P])
        ones = st.sb("ones", [P, P])
        S = [st.sb(f"S{d}", [P, W]) for d in range(2)]
        F = [[st.sb(f"F{d}{c}", [P, 6, NP2, C]) for c in range(2)] for d in range(2)]
        ex = [st.sb(f"ex{d}", [P, 3, NP2, C]) for d in range(2)]
        eT = [st.sb(f"eT{d}", [P, W]) for d in range(2)]
        LW = [st.sb(f"LW{d}", [P, NP2, P]) for d in range(2)]
        V = [st.sb(f"V{d}", [P, NP2, P]) for d in range(2)]
        q4 = [st.sb(f"q4{d}", [P, 4, NP2, P]) for d in range(2)]
        AR = [st.sb(f"AR{d}", [P, NP2, 2, P]) for d in range(2)]
        KB = [st.sb(f"KB{d}", [P, 2, W]) for d in range(2)]
        GB = [st.sb(f"GB{d}", [P, NP2, 2, P]) for d in range(2)]
        GK = [st.sb(f"GK{d}", [P, NP2, 2, P]) for d in range(2)]
        X = [st.sb(f"X{d}", [P, LEV, W]) for d in range(2)]
        T = [st.sb(f"T{d}", [P, W]) for d in range(2)]
        TT = [st.sb(f"TT{d}", [P, W]) for d in range(2)]
        Pm = [st.sb(f"Pm{d}", [P, W]) for d in range(2)]
        Wm = [st.sb(f"Wm{d}", [P, W]) for d in range(2)]
        Un = [st.sb(f"Un{d}", [P, W]) for d in range(2)]
        Yo = [st.sb(f"Yo{d}", [P, NP2, P]) for d in range(2)]
        bank = [[st.ps(f"bank{d}{b}") for b in range(4)] for d in range(2)]
        const_in, cleared = st.sem("const_in"), st.sem("cleared")
        e = [{n: st.sem(f"{n}{d}") for n in (
            "loaded0_", "loaded1_", "blocks", "sums", "exps", "scaled", "turned", "turned_a", "turned_v", "grams", "masked", "levels", "mb", "t0",
            "p_mm", "p_out", "dt_mm", "dt_out", "w_mm", "w_out", "u_mm", "u_out", "ys_mm", "y_out", "s_out", "stored", "seq")} for d in range(2)]
        with nc.Block() as block:
            @block.sync
            def _(sp):
                sp.dma_start(tri[:, :, :], ap["tri"]).then_inc(const_in, 16)
                sp.dma_start(lev[:, :, :, :], ap["lev"]).then_inc(const_in, 16)
                sp.dma_start(lev0[:, :, :], ap["lev0"]).then_inc(const_in, 16)
                sp.dma_start(keep[:, :, :, :], ap["keep"]).then_inc(const_in, 16)
                sp.wait_ge(const_in, 64)

            @block.vector
            def _(dve):
                dve.memset(ones[:, :], 1.0).then_inc(cleared, 1)
                for d in range(2):
                    dve.memset(S[d][:, :], 0.0).then_inc(cleared, 1)
                    dve.memset(LW[d][:, :, :], 0.0).then_inc(cleared, 1)
                    dve.memset(V[d][:, :, :], 0.0).then_inc(cleared, 1)
                    dve.memset(q4[d][:, :, :, :], 0.0).then_inc(cleared, 1)
                dve.wait_ge(cleared, 9)
        st.clear()
        FEv = FE.rearrange("(n c) b f -> n c b f", c=C)

        def hp(h):
            return slice(h * P, (h + 1) * P)

        HALF = [slice(0, C), slice(C, P)]

        def chunks(at, emit):
            with nc.Block() as block:
                @block.sync
                def _(sp):
                    for c in range(2):
                        for d in range(2):
                            for b in range(2):
                                sp.dma_start(F[d][c][HALF[b], 0:3, :, :], FEv[at(d, c)][:, b, 0:3 * 256]).then_inc(e[d][f"loaded{c}_"], 16)
                                sp.dma_start(F[d][c][HALF[b], 3:6, :, :], FEv[at(d, c)][:, b, (3 + 3 * d) * 256:(6 + 3 * d) * 256]).then_inc(e[d][f"loaded{c}_"], 16)
                    if emit:
                        for c in range(2):
                            for d in range(2):
                                sp.wait_ge(e[d]["y_out"], c + 1)
                                yv = Y[d].rearrange("(n c) (a b w) -> n b c a w", c=C, b=2, w=HD)
                                for b in range(2):
                                    sp.dma_start(yv[at(d, c) - CCH, b], Yo[d][HALF[b], :, HALF[b]]).then_inc(e[d]["stored"], 16)
                        for d in range(2):
                            sp.wait_ge(e[d]["stored"], 64)

                @block.tensor
                def _(pe):
                    for c in range(2):
                        for d in range(2):
                            s, b, f = e[d], bank[d], F[d][c]
                            pe.wait_ge(s[f"loaded{c}_"], 64)
                            if c:
                                pe.wait_ge(s["s_out"], 1)
                                if emit:
                                    pe.wait_ge(s["y_out"], 1)
                            lw = f[:, 3, :, :].rearrange("p a j -> p (a j)")
                            pe.matmul(b[0][:, 0:256], tri[:, 2 * d, :], lw, start=True, stop=True)
                            pe.matmul(b[1][:, 0:256], tri[:, 2 * d + 1, :], lw, start=True, stop=True)
                            pe.wait_ge(s["blocks"], 4 * c + 2)
                            for h in range(NP2):
                                mm = pe.matmul(b[2][:, hp(h)], LW[d][:, h, :], ones[:, :], start=True, stop=True)
                            mm.then_inc(s["sums"], 1)
                        for d in range(2):
                            s, b = e[d], bank[d]
                            for x, to in ((0, 3), (1, 0), (2, 1), (3, 2)):
                                pe.wait_ge(s["scaled"], 8 * c + 2 * x + 2)
                                if x == 1:
                                    pe.wait_ge(s["exps"], 4 * c + 4)
                                for h in range(NP2):
                                    mm = pe.transpose(b[to][:, hp(h)], q4[d][:, x, h, :], ident[:, :])
                                mm.then_inc(s["turned"], 1)
                        for d in range(2):
                            s, b = e[d], bank[d]
                            pe.wait_ge(s["turned_a"], 2 * c + 2)
                            pe.wait_ge(s["turned_v"], 2 * c + 2)
                            for x, base in ((1, 0), (0, 2)):
                                for h in range(NP2):
                                    mm = pe.matmul(b[base + h // 2][:, (h % 2) * 2 * P:(h % 2 + 1) * 2 * P], KB[d][:, x, hp(h)],
                                                   AR[d][:, h, :, :].rearrange("p a t -> p (a t)"), start=True, stop=True)
                                mm.then_inc(s["grams"], 1)
                        for d in range(2):
                            s, b = e[d], bank[d]
                            pe.wait_ge(s["masked"], 4 * c + 1)
                            for h in range(NP2):
                                mm = pe.matmul(b[0][:, hp(h)], AR[d][:, h, 0, :], KB[d][:, 1, hp(h)], start=True, stop=True)
                            mm.then_inc(s["mb"], 1)
                        for l in range(1, LEV):
                            for d in range(2):
                                s, b = e[d], bank[d]
                                pe.wait_ge(s["levels"], 7 * c + l + 2)
                                pe.wait_ge(s["t0"], c + 1)
                                pe.wait_ge(s["masked"], 4 * c + 4)
                                if l > 1:
                                    pe.wait_ge(s["dt_out"], 5 * c + l - 1)
                                for h in range(NP2):
                                    mm = pe.matmul(b[1][:, hp(h)], X[d][:, l, hp(h)], T[d][:, hp(h)], start=True, stop=True)
                                mm.then_inc(s["p_mm"], 1)
                            for d in range(2):
                                s, b = e[d], bank[d]
                                pe.wait_ge(s["p_out"], 5 * c + l)
                                for h in range(NP2):
                                    if l < LEV - 1:
                                        pe.matmul(b[2][:, hp(h)], TT[d][:, hp(h)], Pm[d][:, hp(h)], start=True, stop=True)
                                    mm = pe.matmul(b[3][:, hp(h)], Pm[d][:, hp(h)], TT[d][:, hp(h)], start=True, stop=True)
                                mm.then_inc(s["dt_mm"], 1)
                        for d in range(2):
                            s, b = e[d], bank[d]
                            pe.wait_ge(s["blocks"], 4 * c + 4)
                            for h in range(NP2):
                                pe.matmul(b[0][:, hp(h)], AR[d][:, h, 0, :], S[d][:, hp(h)], start=True, stop=False)
                                mm = pe.matmul(b[0][:, hp(h)], GK[d][:, h, 0, :], V[d][:, h, :], start=False, stop=True)
                            mm.then_inc(s["w_mm"], 1)
                        for d in range(2):
                            s, b = e[d], bank[d]
                            pe.wait_ge(s["w_out"], c + 1)
                            pe.wait_ge(s["dt_out"], 5 * c + LEV - 1)
                            for h in range(NP2):
                                mm = pe.matmul(b[1][:, hp(h)], TT[d][:, hp(h)], Wm[d][:, hp(h)], start=True, stop=True)
                            mm.then_inc(s["u_mm"], 1)
                        for d in range(2):
                            s, b = e[d], bank[d]
                            pe.wait_ge(s["u_out"], c + 1)
                            if emit:
                                for h in range(NP2):
                                    pe.matmul(b[2][:, hp(h)], AR[d][:, h, 1, :], S[d][:, hp(h)], start=True, stop=False)
                                    pe.matmul(b[2][:, hp(h)], GK[d][:, h, 1, :], V[d][:, h, :], start=False, stop=False)
                                    mm = pe.matmul(b[2][:, hp(h)], GB[d][:, h, 1, :], Un[d][:, hp(h)], start=False, stop=True)
                            for h in range(NP2):
                                pe.matmul(b[3][:, hp(h)], ident[:, :], S[d][:, hp(h)], start=True, stop=False)
                                pe.matmul(b[3][:, hp(h)], q4[d][:, 2, h, :], V[d][:, h, :], start=False, stop=False)
                                mm = pe.matmul(b[3][:, hp(h)], q4[d][:, 3, h, :], Un[d][:, hp(h)], start=False, stop=True)
                            mm.then_inc(s["ys_mm"], 1)

                @block.scalar
                def _(act):
                    for c in range(2):
                        for d in range(2):
                            s, b = e[d], bank[d]
                            act.wait_ge(s["sums"], c + 1)
                            flat = [ex[d][:, x, :, :].rearrange("p a j -> p (a j)") for x in range(3)]
                            nc.scalar.activation(flat[0], b[1][:, 0:256], ACT.Exp).then_inc(s["exps"], 1)
                            nc.scalar.activation(flat[1], b[0][:, 0:256], ACT.Exp).then_inc(s["exps"], 1)
                            nc.scalar.activation(flat[2], b[0][:, 0:256], ACT.Exp, scale=-1.0).then_inc(s["exps"], 1)
                            nc.scalar.activation(eT[d][:, :], b[2][:, :], ACT.Exp).then_inc(s["exps"], 1)
                        for d in range(2):
                            s, b = e[d], bank[d]
                            for x, of in ((0, 3), (1, 0)):
                                act.wait_ge(s["turned"], 4 * c + x + 1)
                                nc.scalar.copy(AR[d][:, :, x, :], b[of][:, :].rearrange("p (h t) -> p h t", t=P)).then_inc(s["turned_a"], 1)
                        for l in range(1, LEV):
                            for d in range(2):
                                s, b = e[d], bank[d]
                                act.wait_ge(s["p_mm"], 5 * c + l)
                                if l > 1:
                                    act.wait_ge(s["dt_mm"], 5 * c + l - 1)
                                nc.scalar.copy(Pm[d][:, :], b[1][:, :]).then_inc(s["p_out"], 1)
                        for d in range(2):
                            s, b = e[d], bank[d]
                            act.wait_ge(s["w_mm"], c + 1)
                            nc.scalar.copy(Wm[d][:, :], b[0][:, :]).then_inc(s["w_out"], 1)
                        if emit:
                            for d in range(2):
                                s, b = e[d], bank[d]
                                act.wait_ge(s["ys_mm"], c + 1)
                                if c:
                                    act.wait_ge(s["stored"], 32)
                                nc.scalar.copy(Yo[d][:, :, :].rearrange("p a w -> p (a w)"), b[2][:, :]).then_inc(s["y_out"], 1)

                @block.gpsimd
                def _(pool):
                    for c in range(2):
                        for d in range(2):
                            s = e[d]
                            pool.wait_ge(s[f"loaded{c}_"], 64)
                            if c:
                                pool.wait_ge(s["ys_mm"], 1)
                                for own in e:
                                    pool.wait_ge(own["levels"], 7)
                            for fld, to in ((3, LW), (1, V)):
                                for b in range(2):
                                    pool.tensor_copy(to[d][HALF[b], :, HALF[b]], F[d][c][HALF[b], fld, :, :]).then_inc(s["blocks"], 1)
                        for d in range(2):
                            s = e[d]
                            for own in e:
                                pool.wait_ge(own["blocks"], 4 * c + 4)
                            pool.wait_ge(s["masked"], 4 * c + 2)
                            for l in range(LEV):
                                pool.tensor_tensor(X[d][:, l, :].rearrange("p (h t) -> p h t", t=P), GB[d][:, :, 0, :],
                                                   lev[:, d, l:l + 1, :].to_broadcast([P, NP2, P]), ALU.mult).then_inc(s["levels"], 1)
                                if l == 0:
                                    pool.wait_ge(s["levels"], 7 * c + 1)
                                    pool.tensor_tensor(TT[d][:, :].rearrange("p (h t) -> p h t", t=P),
                                                       ident[:, :].unsqueeze(1).to_broadcast([P, NP2, P]),
                                                       X[d][:, 0, :].rearrange("p (h t) -> p h t", t=P), ALU.subtract).then_inc(s["levels"], 1)

                @block.vector
                def _(dve):
                    link = Linked(dve, e[0]["seq"])
                    for c in range(2):
                        for d in range(2):
                            s = e[d]
                            dve.wait_ge(s[f"loaded{c}_"], 64)
                            if c:
                                dve.wait_ge(s["ys_mm"], 1)
                            for x, (fld, ee) in enumerate(((2, 0), (0, 1), (4, 2), (5, 2))):
                                dve.wait_ge(s["exps"], 4 * c + ee + 1)
                                for b in range(2):
                                    dve.tensor_tensor(q4[d][HALF[b], x, :, HALF[b]], F[d][c][HALF[b], fld, :, :], ex[d][HALF[b], ee, :, :], ALU.mult).then_inc(s["scaled"], 1)
                        for d in range(2):
                            s, b = e[d], bank[d]
                            for x, of in ((0, 1), (1, 2)):
                                dve.wait_ge(s["turned"], 4 * c + x + 3)
                                dve.tensor_copy(KB[d][:, x, :], b[of][:, :]).then_inc(s["turned_v"], 1)
                        for d in range(2):
                            s, b = e[d], bank[d]
                            for g, dst in ((0, GB), (1, GK)):
                                dve.wait_ge(s["grams"], 2 * c + g + 1)
                                for hh in range(2):
                                    dve.tensor_tensor(dst[d][:, 2 * hh:2 * hh + 2, :, :].rearrange("p h a t -> p h (a t)"),
                                                      b[2 * g + hh][:, :].rearrange("p (h x) -> p h x", x=2 * P),
                                                      keep[:, d, :, :].rearrange("p a t -> p (a t)").unsqueeze(1).to_broadcast([P, 2, 2 * P]),
                                                      ALU.mult).then_inc(s["masked"], 1)
                        for d in range(2):
                            s, b = e[d], bank[d]
                            dve.wait_ge(s["mb"], c + 1)
                            link(dve.tensor_tensor(T[d][:, :].rearrange("p (h t) -> p h t", t=P), b[0][:, :].rearrange("p (h t) -> p h t", t=P),
                                                   lev0[:, d:d + 1, :].to_broadcast([P, NP2, P]), ALU.mult))
                            dve.tensor_tensor(T[d][:, :].rearrange("p (h t) -> p h t", t=P), T[d][:, :].rearrange("p (h t) -> p h t", t=P),
                                              ident[:, :].unsqueeze(1).to_broadcast([P, NP2, P]), ALU.add).then_inc(s["t0"], 1)
                        for l in range(1, LEV):
                            for d in range(2):
                                s, b = e[d], bank[d]
                                dve.wait_ge(s["dt_mm"], 5 * c + l)
                                if l == 1:
                                    dve.wait_ge(s["t0"], c + 1)
                                    dve.wait_ge(s["levels"], 7 * c + 2)
                                if l < LEV - 1:
                                    dve.tensor_tensor(T[d][:, :], T[d][:, :], b[2][:, :], ALU.subtract)
                                dve.tensor_tensor(TT[d][:, :], TT[d][:, :], b[3][:, :], ALU.subtract).then_inc(s["dt_out"], 1)
                                dve.wait_ge(s["dt_out"], 5 * c + l)
                        for d in range(2):
                            s, b = e[d], bank[d]
                            dve.wait_ge(s["u_mm"], c + 1)
                            dve.tensor_scalar(Un[d][:, :], b[1][:, :], -1.0, None, ALU.mult).then_inc(s["u_out"], 1)
                        for d in range(2):
                            s, b = e[d], bank[d]
                            dve.wait_ge(s["ys_mm"], c + 1)
                            dve.tensor_tensor(S[d][:, :], b[3][:, :], eT[d][:, :], ALU.mult).then_inc(s["s_out"], 1)

        with nc.Fori(0, CCH // 2) as i:
            chunks(lambda d, c: i * 2 + c if d == 0 else i * -2 + (CCH - 1 - c), False)
            st.clear()
        with nc.Fori(CCH // 2, NCH // 2) as i:
            chunks(lambda d, c: i * 2 + c if d == 0 else i * -2 + (NCH - 1 + CCH - c), True)
            st.clear()


def scan_constants():
    s, t = np.meshgrid(np.arange(P), np.arange(P), indexing="ij")
    f = np.float32
    own = s // C == t // C
    tri = np.stack([own & (s <= t), own & (s < t), own & (s >= t), own & (s > t)], 1).astype(f)
    keep = np.stack([np.stack([own & (s < t), own & (s <= t)], 1), np.stack([own & (s > t), own & (s >= t)], 1)], 1).astype(f)
    lev = np.zeros((P, 2, 6, P), f)
    for n in range(6):
        b = 1 << n
        same = (s // (2 * b)) == (t // (2 * b))
        lev[:, 0, n] = same & (s // b < t // b)
        lev[:, 1, n] = same & (s // b > t // b)
    lev0 = -np.stack([lev[:, 0, 0].T, lev[:, 1, 0].T], 1)
    return tri, keep, lev, np.ascontiguousarray(lev0)


HY0 = RW + HW
NFREQ = 1024


def rows(dram, pairs=False):
    return dram.rearrange("(n q p) d -> n q p d", q=2, p=P) if pairs else dram.rearrange("(n p) d -> n p d", p=P)


def hyena_conv3_stage(nc, ap, U2, HX):
    W3 = 3 * HW
    with Stage(nc, "conv3") as st:
        u = [[st.sb(f"u{p}{a}", [P, W3]) for a in range(3)] for p in range(2)]
        t = [st.sb(f"t{p}", [P, W3]) for p in range(2)]
        taps = st.sb("taps", [P, 3, W3])
        const_in, stored = st.sem("const_in"), st.sem("stored")
        loaded = [st.sem(f"loaded{p}") for p in range(2)]
        done = [st.sem(f"done{p}") for p in range(2)]
        seq = [st.sem(f"seq{p}") for p in range(2)]
        with nc.Block() as block:
            @block.sync
            def _(sp):
                for a in range(3):
                    sp.dma_start(taps[:, a, :], ap["hy_short"][0, a].partition_broadcast(P)).then_inc(const_in, 16)
                sp.wait_ge(const_in, 48)
        st.clear()
        with nc.Fori(0, LT // 2) as i:
            with nc.Block() as block:
                @block.sync
                def _(sp):
                    for p in range(2):
                        for a in range(3):
                            src = rows(U2[LAT0 + a - 1:LAT0 + a - 1 + LAT, HY0:HY0 + W3], True)
                            sp.dma_start(u[p][a][:, :], src[i, p]).then_inc(loaded[p], 16)
                    for p in range(2):
                        sp.wait_ge(done[p], 1)
                        sp.dma_start(HX.rearrange("a (n q p) d -> n q p a d", q=2, p=P)[i, p],
                                     t[p][:, :].rearrange("p (a d) -> p a d", a=3)).then_inc(stored, 16)
                    sp.wait_ge(stored, 32)

                def conv(eng, p):
                    link = Linked(eng, seq[p])
                    eng.wait_ge(loaded[p], 48)
                    link(eng.tensor_tensor(t[p][:, :], u[p][0][:, :], taps[:, 0, :], ALU.mult))
                    for a in (1, 2):
                        link(eng.tensor_tensor(u[p][a][:, :], u[p][a][:, :], taps[:, a, :], ALU.mult))
                        if a == 1:
                            link(eng.tensor_tensor(t[p][:, :], t[p][:, :], u[p][a][:, :], ALU.add))
                    eng.tensor_tensor(t[p][:, :], t[p][:, :], u[p][2][:, :], ALU.add).then_inc(done[p], 1)

                @block.vector
                def _(dve):
                    conv(dve, 0)

                @block.gpsimd
                def _(pool):
                    conv(pool, 1)
            st.clear()


def hyena_stage(nc, ap, HX, O):
    with Stage(nc, "hy") as st:
        z = st.sb("z", [P, LT, HW])
        with Stage(nc, "hyp") as sr:
            plus = sr.sb("plus", [P, LT, 2 * HW], side="right")
            minus = sr.sb("minus", [P, LT, 2 * HW], side="right")
            rk = sr.sb("rk", [P, 2 * HW], side="right")
            Kn = sr.sb("Kn", [1, 2 * HW], side="right")
            hyena_filters(nc, ap, HX, z, plus, minus, rk, Kn)
            KS = st.sb("KS", [P, 2, 8, HW])
            YS = st.sb("YS", [P, 2, 8, HW])
            hyena_spectra(nc, ap, z, KS, YS, (plus, minus, rk, Kn))
        hyena_inverse(nc, ap, 0, HX, YS, z, None)
        hyena_spectra(nc, ap, z, KS, YS, None)
        hyena_inverse(nc, ap, 1, HX, YS, z, O)


def hyena_filters(nc, ap, HX, z, plus, minus, rk, Kn):
    TWO_PI_HI, TWO_PI_LO = 6.28125, float(2 * np.pi - 6.28125)
    MAGIC = 12582912.0
    with Stage(nc, "hyf") as sf:
        feats = sf.sb("feats", [33, LAT])
        w1 = sf.sb("w1", [33, 64])
        w2 = sf.sb("w2", [64, 64])
        w3 = sf.sb("w3", [64, 4 * HW])
        b12 = sf.sb("b12", [64, 2])
        b3 = sf.sb("b3", [P, 4 * HW])
        hid = sf.sb("hid", [64, LAT])
        turn = sf.sb("turn", [64, LAT])
        win = [sf.sb(f"win{p}", [P, HW]) for p in range(2)]
        taps = sf.sb("taps", [P, 4, HW])
        sq = [sf.sb(f"sq{p}", [P, 4, HW]) for p in range(2)]
        ones = sf.sb("ones", [P, P])
        alt = sf.sb("alt", [P, 1])
        ph = [sf.ps(f"ph{i}") for i in range(2)]
        pk = [sf.ps(f"pk{i}") for i in range(4)]
        pn = [sf.ps(f"pn{i}") for i in range(2)]
        names = ("small_in", "set", "hid_mm", "reduced", "sine", "taps_mm", "taps_out", "squared", "sums", "root", "seq", "z_in", "nyq")
        small_in, set_, hid_mm, reduced, sine, taps_mm, taps_out, squared, sums, root, seq, z_in, nyq = (sf.sem(n) for n in names)
        win_in = [sf.sem(f"win_in{p}") for p in range(2)]
        with nc.Block() as block:
            @block.sync
            def _(sp):
                for to, of in ((feats[:, :], ap["hy_feats"]), (w1[:, :], ap["hy_w1"][0]), (w2[:, :], ap["hy_w2"][0]), (w3[:, :], ap["hy_w3"][0]),
                               (b12[:, 0:1], ap["hy_b1"][0].rearrange("(p o) -> p o", o=1)), (b12[:, 1:2], ap["hy_b2"][0].rearrange("(p o) -> p o", o=1)),
                               (alt[:, :], ap["alternate"]), (b3[:, :], ap["hy_b3"][0].partition_broadcast(P))):
                    sp.dma_start(to, of, allow_slow_non_contiguous=True).then_inc(small_in, 16)
                sp.dma_start(z[:, :, :], HX[0].rearrange("(n p) d -> p n d", p=P)).then_inc(z_in, 16)
                for n in range(LT):
                    if n >= 2:
                        sp.wait_ge(taps_out, n - 1)
                    sp.dma_start(win[n % 2][:, :], rows(ap["hy_window"])[n]).then_inc(win_in[n % 2], 16)
                sp.wait_ge(z_in, 16)

            @block.tensor
            def _(pe):
                pe.wait_ge(small_in, 128)
                pe.wait_ge(set_, 1)
                for lay, (w, src) in enumerate(((w1, feats), (w2, hid))):
                    for h in range(2):
                        if lay:
                            pe.wait_ge(sine, 2)
                        mm = pe.matmul(ph[h][0:64, :], w[:, :], src[:, h * 512:(h + 1) * 512], start=True, stop=True)
                        mm.then_inc(hid_mm, 1)
                pe.wait_ge(sine, 4)

                def sum_squares(n):
                    pe.wait_ge(squared, n + 1)
                    for a in range(4):
                        pe.matmul(pn[a % 2][:, :], ones[:, :], sq[n % 2][:, a, :], start=(n == 0 and a < 2), stop=(n == LT - 1 and a >= 2)).then_inc(sums, 1)

                for n in range(LT):
                    if n:
                        pe.wait_ge(taps_out, n)
                    for a in range(4):
                        mm = pe.matmul(pk[a][:, :], hid[:, n * P:(n + 1) * P], w3[:, a * 512:(a + 1) * 512], start=True, stop=True)
                    mm.then_inc(taps_mm, 1)
                    if n:
                        sum_squares(n - 1)
                sum_squares(LT - 1)
                pe.wait_ge(taps_out, LT)
                pe.wait_ge(root, 2)
                for o in range(2):
                    for n in range(LT):
                        mm = pe.matmul(ph[o][0:1, :], alt[:, :], plus[:, n, o * 512:(o + 1) * 512], start=(n == 0), stop=(n == LT - 1))
                    mm.then_inc(nyq, 1)

            @block.scalar
            def _(act):
                act.wait_ge(small_in, 128)
                for lay in range(2):
                    for h in range(2):
                        act.wait_ge(reduced, 2 * lay + h + 1)
                        nc.scalar.activation(hid[:, h * 512:(h + 1) * 512], hid[:, h * 512:(h + 1) * 512], ACT.Sin).then_inc(sine, 1)
                for n in range(LT):
                    act.wait_ge(taps_out, n + 1)
                    if n >= 2:
                        act.wait_ge(sums, 4 * (n - 1))
                    for a in range(2):
                        half = slice(a * 512, (a + 1) * 512)
                        nc.scalar.activation(sq[n % 2][:, a, :], plus[:, n, half], ACT.Square)
                        ins = nc.scalar.activation(sq[n % 2][:, 2 + a, :], minus[:, n, half], ACT.Square)
                    ins.then_inc(squared, 1)
                act.wait_ge(sums, 4 * LT)
                for a in range(2):
                    nc.scalar.activation(rk[:, a * 512:(a + 1) * 512], pn[a][:, :], ACT.Sqrt, scale=0.5).then_inc(root, 1)

            @block.vector
            def _(dve):
                link = Linked(dve, seq)
                dve.memset(ones[:, :], 1.0).then_inc(set_, 1)
                dve.wait_ge(small_in, 128)
                for lay in range(2):
                    for h in range(2):
                        dve.wait_ge(hid_mm, 2 * lay + h + 1)
                        c = slice(h * 512, (h + 1) * 512)
                        x, n = hid[:, c], turn[:, c]
                        if lay:
                            dve.wait_ge(hid_mm, 4)
                        link(dve.tensor_scalar(x, ph[h][0:64, :], b12[:, lay:lay + 1], None, ALU.add))
                        link(dve.tensor_scalar(n, x, float(1 / (2 * np.pi)), MAGIC, ALU.mult, ALU.add))
                        link(dve.tensor_scalar(n, n, MAGIC, None, ALU.subtract))
                        link(dve.scalar_tensor_tensor(out=x, in0=n, scalar=-TWO_PI_HI, in1=x, op0=ALU.mult, op1=ALU.add))
                        link(dve.scalar_tensor_tensor(out=x, in0=n, scalar=-TWO_PI_LO, in1=x, op0=ALU.mult, op1=ALU.add))
                        dve.tensor_scalar(x, x, 3.1415925, -3.1415925, ALU.min, ALU.max).then_inc(reduced, 1)
                for n in range(LT):
                    dve.wait_ge(taps_mm, n + 1)
                    dve.wait_ge(win_in[n % 2], 16 * (n // 2 + 1))
                    for a in range(4):
                        link(dve.tensor_tensor(taps[:, a, :], pk[a][:, :], b3[:, a * 512:(a + 1) * 512], ALU.add))
                    link(dve.tensor_tensor(taps[:, :, :], taps[:, :, :], win[n % 2][:, :].unsqueeze(1).to_broadcast([P, 4, HW]), ALU.mult))
                    if n == 0:
                        link(dve.tensor_tensor(taps[0:1, 0:2, :], taps[0:1, 0:2, :], taps[0:1, 2:4, :], ALU.add))
                        link(dve.memset(taps[0:1, 2:4, :], 0.0))
                    f = taps[:, 0:2, :].rearrange("p a d -> p (a d)")
                    b = taps[:, 2:4, :].rearrange("p a d -> p (a d)")
                    dve.tensor_tensor(plus[:, n, :], f, b, ALU.add).then_inc(seq, 1)
                    link.n += 1
                    dve.tensor_tensor(minus[:, n, :], f, b, ALU.subtract).then_inc(taps_out, 1)
                    dve.wait_ge(taps_out, n + 1)
                    dve.wait_ge(seq, link.n)
                dve.wait_ge(root, 2)
                link(dve.reciprocal(rk[:, :], rk[:, :]))
                for o in range(2):
                    dve.wait_ge(nyq, o + 1)
                    link(dve.tensor_tensor(Kn[0:1, o * 512:(o + 1) * 512], ph[o][0:1, :], rk[0:1, o * 512:(o + 1) * 512], ALU.mult))


def hyena_spectra(nc, ap, z, KS, YS, filters):
    if filters:
        plus, minus, rk, Kn = filters
    with Stage(nc, "hys" + ("1" if filters else "2")) as ss:
        Fm = [ss.sb(f"F{b}", [P, 8, 2, P]) for b in range(2)]
        zs = [ss.sb(f"zs{b}", [P, 2, HW]) for b in range(2)]
        ks = ss.sb("ks", [P, 2, HW])
        tmp = ss.sb("tmp", [P, 2, HW])
        bank = [ss.ps(f"bank{i}") for i in range(6)]
        f_in = [ss.sem(f"f_in{b}") for b in range(2)]
        k_mm, k_out, z_mm, z_out, seq = (ss.sem(n) for n in ("k_mm", "k_out", "z_mm", "z_out", "seq"))

        def products(dve, link, j, b, k_of, first):
            link(dve.tensor_tensor(tmp[:, 0, :], zs[b][:, 0, :], k_of(0), ALU.mult))
            link(dve.tensor_tensor(tmp[:, 1, :], zs[b][:, 1, :], k_of(1), ALU.mult))
            to = YS[:, :, bass.ds(j, 1), :]
            link(dve.tensor_tensor(to[:, 0], tmp[:, 0:1, :], tmp[:, 1:2, :], ALU.subtract))
            if first:
                link(dve.tensor_copy(YS[0:1, 0, 0, :], tmp[0:1, 0, :]))
                link(dve.tensor_copy(Kn1[:, :], tmp[0:1, 1, :]))
            link(dve.tensor_tensor(tmp[:, 0, :], zs[b][:, 0, :], k_of(1), ALU.mult))
            link(dve.tensor_tensor(tmp[:, 1, :], zs[b][:, 1, :], k_of(0), ALU.mult))
            link(dve.tensor_tensor(to[:, 1], tmp[:, 0:1, :], tmp[:, 1:2, :], ALU.add))
            if first:
                link(dve.tensor_copy(YS[0:1, 1, 0, :], Kn1[:, :]))

        Kn1 = ss.sb("Kn1", [1, HW])

        def first_spectra(jj, peeled):
            with nc.Block() as block:
                @block.sync
                def _(sp):
                    for b in range(2):
                        sp.dma_start(Fm[b][:, :, :, :], ap["dft"].rearrange("(n q) p t r f -> n q p t r f", q=2)[jj, b]).then_inc(f_in[b], 16)

                @block.tensor
                def _(pe):
                    for b in range(2):
                        pe.wait_ge(f_in[b], 16)
                        for r in range(2):
                            if b:
                                pe.wait_ge(k_out, 4 * (b - 1) + 2 * r + 2)
                                pe.wait_ge(z_out, 2 * (b - 1) + r + 1)
                            taps = plus if r == 0 else minus
                            for o in range(2):
                                for n in range(LT):
                                    mm = pe.matmul(bank[3 * r + o][:, :], Fm[b][:, n, r, :], taps[:, n, o * 512:(o + 1) * 512], start=(n == 0), stop=(n == LT - 1))
                                mm.then_inc(k_mm, 1)
                            for n in range(LT):
                                mm = pe.matmul(bank[3 * r + 2][:, :], Fm[b][:, n, r, :], z[:, n, :], start=(n == 0), stop=(n == LT - 1))
                            mm.then_inc(z_mm, 1)

                @block.scalar
                def _(act):
                    for b in range(2):
                        for r in range(2):
                            act.wait_ge(z_mm, 2 * b + r + 1)
                            nc.scalar.copy(zs[b][:, r, :], bank[3 * r + 2][:, :]).then_inc(z_out, 1)

                @block.vector
                def _(dve):
                    link = Linked(dve, seq)
                    for b in range(2):
                        j = jj * 2 + b
                        for r in range(2):
                            for o in range(2):
                                dve.wait_ge(k_mm, 4 * b + 2 * r + o + 1)
                                to = ks[:, r:r + 1, :] if o == 0 else KS[:, r, bass.ds(j, 1), :]
                                dve.tensor_tensor(to, bank[3 * r + o][:, :].unsqueeze(1), rk[:, o * 512:(o + 1) * 512].unsqueeze(1), ALU.mult).then_inc(k_out, 1)
                                dve.wait_ge(k_out, 4 * b + 2 * r + o + 1)
                        if peeled and b == 0:
                            link(dve.tensor_copy(ks[0:1, 1, :], Kn[0:1, 0:512]))
                            link(dve.tensor_copy(KS[0:1, 1, 0, :], Kn[0:1, 512:1024]))
                        dve.wait_ge(z_out, 2 * b + 2)
                        products(dve, link, j, b, lambda r: ks[:, r, :], peeled and b == 0)
            ss.clear()

        def second_spectra(jj, peeled):
            with nc.Block() as block:
                @block.sync
                def _(sp):
                    for b in range(2):
                        sp.dma_start(Fm[b][:, :, :, :], ap["dft"].rearrange("(n q) p t r f -> n q p t r f", q=2)[jj, b]).then_inc(f_in[b], 16)

                @block.tensor
                def _(pe):
                    for b in range(2):
                        pe.wait_ge(f_in[b], 16)
                        for r in range(2):
                            for n in range(LT):
                                mm = pe.matmul(bank[2 * b + r][:, :], Fm[b][:, n, r, :], z[:, n, :], start=(n == 0), stop=(n == LT - 1))
                            mm.then_inc(z_mm, 1)

                @block.scalar
                def _(act):
                    for b in range(2):
                        for r in range(2):
                            act.wait_ge(z_mm, 2 * b + r + 1)
                            nc.scalar.copy(zs[b][:, r, :], bank[2 * b + r][:, :]).then_inc(z_out, 1)

                @block.vector
                def _(dve):
                    link = Linked(dve, seq)
                    for b in range(2):
                        j = jj * 2 + b
                        dve.wait_ge(z_out, 2 * b + 2)
                        for r in range(2):
                            link(dve.tensor_copy(ks[:, r:r + 1, :], KS[:, r, bass.ds(j, 1), :]))
                        products(dve, link, j, b, lambda r: ks[:, r, :], peeled and b == 0)
            ss.clear()

        one = first_spectra if filters else second_spectra
        one(0, True)
        with nc.Fori(1, 4) as jj:
            one(jj, False)


def hyena_inverse(nc, ap, order, HX, YS, z, O):
    with Stage(nc, f"inv{order}") as st:
        G = [st.sb(f"G{b}", [P, 16, P]) for b in range(2)]
        x = [st.sb(f"x{b}", [P, HW]) for b in range(2)]
        skip = st.sb("skip", [P, HW])
        t = [st.sb(f"t{b}", [P, HW]) for b in range(2)]
        acc = [st.ps(f"acc{b}") for b in range(2)]
        skip_in = st.sem("skip_in")
        g_in = [st.sem(f"g_in{b}") for b in range(2)]
        mm_done, out, stored, seq = (st.sem(n) for n in ("mm_done", "out", "stored", "seq"))
        with nc.Block() as block:
            @block.sync
            def _(sp):
                sp.dma_start(skip[:, :], ap["hy_skip"][0, order].partition_broadcast(P)).then_inc(skip_in, 16)
                sp.wait_ge(skip_in, 16)
        with nc.Fori(0, LT // 2) as m:
            with nc.Block() as block:
                @block.sync
                def _(sp):
                    for b in range(2):
                        sp.dma_start(G[b][:, :, :], ap["idft"].rearrange("(n q) p c t -> n q p c t", q=2)[m, b]).then_inc(g_in[b], 16)
                        sp.dma_start(x[b][:, :], rows(HX[1 + order], True)[m, b]).then_inc(g_in[b], 16)
                    if O is not None:
                        for b in range(2):
                            sp.wait_ge(out, b + 1)
                            sp.dma_start(rows(O[0:LAT, HW:D], True)[m, b], t[b][:, :]).then_inc(stored, 16)
                        sp.wait_ge(stored, 32)

                @block.tensor
                def _(pe):
                    for b in range(2):
                        pe.wait_ge(g_in[b], 32)
                        for c in range(16):
                            mm = pe.matmul(acc[b][:, :], G[b][:, c, :], YS[:, c // 8, c % 8, :], start=(c == 0), stop=(c == 15))
                        mm.then_inc(mm_done, 1)

                @block.vector
                def _(dve):
                    link = Linked(dve, seq)
                    for b in range(2):
                        dve.wait_ge(g_in[b], 32)
                        zt = z[:, bass.ds(m * 2 + b, 1), :]
                        tb = t[b][:, :].unsqueeze(1)
                        link(dve.tensor_tensor(tb, zt, skip[:, :].unsqueeze(1), ALU.mult))
                        dve.wait_ge(mm_done, b + 1)
                        link(dve.tensor_tensor(t[b][:, :], t[b][:, :], acc[b][:, :], ALU.add))
                        dve.tensor_tensor(zt if O is None else tb, tb, x[b][:, :].unsqueeze(1), ALU.mult).then_inc(out, 1)
                        dve.wait_ge(out, b + 1)
            st.clear()


def hyena_constants():
    f = np.float32
    L = LAT
    t_idx = np.arange(L, dtype=f)
    t = (t_idx / f(L - 1)).astype(f)
    bands = np.linspace(1e-4, 15, 16, dtype=f)
    ang = (f(2.0 * np.pi) * bands[None, :] * t_idx[:, None] / f(L)).astype(f)
    feats = np.concatenate([t[:, None], np.cos(ang), -np.sin(ang)], -1).astype(f)
    deltas = np.linspace(np.log(1e-2) / 0.3, np.log(1e-2) / 1.5, HW, dtype=f)
    window = np.exp(-t[:, None] * np.abs(deltas)).astype(f)
    n, k = np.arange(L), np.arange(NFREQ)
    w = 2 * np.pi * ((n[:, None] * k[None, :]) % 2048) / 2048
    re, im = np.cos(w), -np.sin(w)
    alt = (-1.0) ** n
    im[:, 0] = alt
    dft = np.stack([re, im], 1).reshape(8, P, 2, 8, P).transpose(3, 1, 0, 2, 4)
    gre, gim = 2 * re.T / 2048, 2 * im.T / 2048
    gre[0], gim[0] = 1 / 2048, alt / 2048
    idft = np.concatenate([gre, gim], 0).reshape(16, P, 8, P).transpose(2, 1, 0, 3)
    return (np.ascontiguousarray(feats.T), window, np.ascontiguousarray(dft.astype(f)), np.ascontiguousarray(idft.astype(f)),
            alt[:P, None].astype(f))


def rwkv_readout_stage(nc, ap, FE, Y, O):
    GN_EPS = 64e-5
    with Stage(nc, "read") as st:
        y = [st.sb(f"y{p}", [P, 2, HW]) for p in range(2)]
        f = [st.sb(f"f{p}", [P, 4, HW]) for p in range(2)]
        cst = st.sb("cst", [P, 3, HW])
        sq = [st.sb(f"sq{p}", [P, HW]) for p in range(2)]
        m = [st.sb(f"m{p}", [P, 3, HEADS]) for p in range(2)]
        const_in, ms_ready, rt_ready, centred, squared, done, stored = (st.sem(n) for n in (
            "const_in", "ms_ready", "rt_ready", "centred", "squared", "done", "stored"))
        loaded = [st.sem(f"loaded{p}") for p in range(2)]
        bonus_in = [st.sem(f"bonus_in{p}") for p in range(2)]
        seq, pseq = st.sem("seq"), st.sem("pseq")
        with nc.Block() as block:
            @block.sync
            def _(sp):
                sp.dma_start(cst[:, 0, :], ap["rwkv_gn_w"][0].partition_broadcast(P)).then_inc(const_in, 16)
                sp.dma_start(cst[:, 1, :], ap["rwkv_gn_b"][0].partition_broadcast(P)).then_inc(const_in, 16)
                sp.dma_start(cst[:, 2, :], ap["rwkv_r_k"][0].rearrange("h d -> (h d)").partition_broadcast(P)).then_inc(const_in, 16)
                sp.wait_ge(const_in, 48)
        with nc.Fori(0, LT // 2) as i:
            with nc.Block() as block:
                @block.sync
                def _(sp):
                    fe = FE[CTX:TOK].rearrange("(n q p) b (f a d) -> n q b f p a d", q=2, p=P, a=4, d=HD)
                    for p in range(2):
                        for d in range(2):
                            sp.dma_start(y[p][:, d, :], rows(Y[d], True)[i, p]).then_inc(loaded[p], 16)
                        for to, of in enumerate((0, 1, 4, 7)):
                            for b in range(2):
                                sp.dma_start(f[p][:, to, :].rearrange("p (a b d) -> p b a d", b=2, d=HD)[:, b], fe[i, p][b, of]).then_inc(loaded[p], 16)
                    for p in range(2):
                        sp.wait_ge(done, p + 1)
                        sp.dma_start(rows(O[0:LAT, 0:HW], True)[i, p], y[p][:, 0, :]).then_inc(stored, 16)
                    sp.wait_ge(stored, 32)

                @block.scalar
                def _(act):
                    for p in range(2):
                        act.wait_ge(centred, p + 1)
                        nc.scalar.activation(sq[p][:, :], y[p][:, 0, :], ACT.Square).then_inc(squared, 1)
                        act.wait_ge(ms_ready, p + 1)
                        nc.scalar.activation(m[p][:, 1, :], m[p][:, 1, :], ACT.Sqrt).then_inc(rt_ready, 1)

                def heads(x):
                    return x.rearrange("p (h d) -> p h d", d=HD)

                @block.gpsimd
                def _(pool):
                    for p in range(2):
                        link = Linked(pool, pseq)
                        link.n = 4 * p
                        pool.wait_ge(loaded[p], 160)
                        link(pool.tensor_tensor(f[p][:, 2, :], f[p][:, 2, :], f[p][:, 3, :], ALU.add))
                        link(pool.tensor_tensor(f[p][:, 2, :], f[p][:, 2, :], f[p][:, 0, :], ALU.mult))
                        link(pool.tensor_tensor(f[p][:, 2, :], f[p][:, 2, :], cst[:, 2, :], ALU.mult))
                        link(pool.tensor_scalar(f[p][:, 2, :], f[p][:, 2, :], 0.5, None, ALU.mult))

                @block.vector
                def _(dve):
                    link = Linked(dve, seq)
                    for p in range(2):
                        dve.wait_ge(loaded[p], 160)
                        yy = y[p][:, 0, :]
                        link(dve.tensor_tensor(yy, yy, y[p][:, 1, :], ALU.add))
                        link(dve.tensor_reduce(m[p][:, 0, :], heads(yy), AX.X, ALU.add))
                        link(dve.tensor_scalar(m[p][:, 0, :], m[p][:, 0, :], 1.0 / HD, None, ALU.mult))
                        dve.tensor_tensor(heads(yy), heads(yy), m[p][:, 0, :].unsqueeze(2).to_broadcast([P, HEADS, HD]), ALU.subtract).then_inc(centred, 1)
                        dve.wait_ge(pseq, 4 * p + 4)
                        link(dve.tensor_reduce(m[p][:, 2, :], heads(f[p][:, 2, :]), AX.X, ALU.add))
                        link(dve.tensor_tensor(heads(f[p][:, 1, :]), heads(f[p][:, 1, :]), m[p][:, 2, :].unsqueeze(2).to_broadcast([P, HEADS, HD]), ALU.mult))
                        dve.wait_ge(squared, p + 1)
                        link(dve.tensor_reduce(m[p][:, 1, :], heads(sq[p][:, :]), AX.X, ALU.add))
                        dve.tensor_scalar(m[p][:, 1, :], m[p][:, 1, :], 1.0 / HD, GN_EPS, ALU.mult, ALU.add).then_inc(ms_ready, 1)
                        dve.wait_ge(rt_ready, p + 1)
                        link(dve.reciprocal(m[p][:, 1, :], m[p][:, 1, :]))
                        link(dve.tensor_tensor(heads(yy), heads(yy), m[p][:, 1, :].unsqueeze(2).to_broadcast([P, HEADS, HD]), ALU.mult))
                        link(dve.tensor_tensor(yy, yy, cst[:, 0, :], ALU.mult))
                        link(dve.tensor_tensor(yy, yy, cst[:, 1, :], ALU.add))
                        dve.tensor_tensor(yy, yy, f[p][:, 1, :], ALU.add).then_inc(done, 1)
            st.clear()


def forget_stage(nc, ap, U3, keep):
    with Stage(nc, "forget") as st:
        f = st.sb("f", [P, LT, HEADS])
        g = st.sb("g", [P, LT, HEADS])
        b = st.sb("b", [P, HEADS])
        tri = st.sb("tri", [P, P])
        ones = st.sb("ones", [P, P])
        pc = st.ps("pc")
        loaded, x_ready, exped, lns, lf, mm_done, seq = (st.sem(n) for n in ("loaded", "x_ready", "exped", "lns", "lf", "mm_done", "seq"))
        with nc.Block() as block:
            @block.sync
            def _(sp):
                sp.dma_start(f[:, :, :], U3[:, 2560:2568].rearrange("(n p) h -> p n h", p=P)).then_inc(loaded, 16)
                sp.dma_start(b[:, :], ap["b_forget_2"][0].partition_broadcast(P)).then_inc(loaded, 16)
                sp.dma_start(tri[:, :], ap["tri128"]).then_inc(loaded, 16)

            @block.scalar
            def _(act):
                act.wait_ge(x_ready, 1)
                nc.scalar.activation(g[:, :, :], g[:, :, :], ACT.Exp).then_inc(exped, 1)
                act.wait_ge(exped, 1)
                nc.scalar.activation(g[:, :, :], g[:, :, :], ACT.Ln, bias=1.0).then_inc(lns, 1)

            @block.vector
            def _(dve):
                link = Linked(dve, seq)
                link(dve.memset(ones[:, :], 1.0))
                dve.wait_ge(loaded, 48)
                link(dve.tensor_tensor(f[:, :, :], f[:, :, :], b[:, :].unsqueeze(1).to_broadcast([P, LT, HEADS]), ALU.add))
                link(dve.tensor_scalar(g[:, :, :], f[:, :, :], -1.0, None, ALU.mult))
                dve.tensor_tensor(g[:, :, :], g[:, :, :], f[:, :, :], ALU.min).then_inc(x_ready, 1)
                dve.wait_ge(lns, 1)
                link(dve.tensor_scalar(f[:, :, :], f[:, :, :], 0.0, None, ALU.min))
                dve.tensor_tensor(f[:, :, :], f[:, :, :], g[:, :, :], ALU.subtract).then_inc(lf, 1)
                dve.wait_ge(mm_done, 1)
                link(dve.tensor_copy(keep[:, :, :], pc[:, 0:LT * HEADS].rearrange("p (n h) -> p n h", h=HEADS)))

            @block.tensor
            def _(pe):
                pe.wait_ge(lf, 1)
                pe.wait_ge(loaded, 48)
                pe.wait_ge(seq, 1)
                for m in range(LT):
                    for n in range(m + 1):
                        mm = pe.matmul(pc[:, m * HEADS:(m + 1) * HEADS], tri[:, :] if n == m else ones[:, :], f[:, n, :], start=(n == 0), stop=(n == m))
                mm.then_inc(mm_done, 1)


KF = HD + 2


def fox_prep_stage(nc, ident, U3, csum, QF):
    with Stage(nc, "foxp") as st:
        u = [st.sb(f"u{p}", [P, 2 * HW]) for p in range(2)]
        aug = [st.sb(f"aug{p}", [P, 16, KF]) for p in range(2)]
        tb = st.sb("tb", [KF, 16, 2 * P])
        pt = [st.ps(f"pt{i}") for i in range(8)]
        loaded = [st.sem(f"loaded{p}") for p in range(2)]
        filled = [st.sem(f"filled{p}") for p in range(2)]
        trans, evac, stored = (st.sem(n) for n in ("trans", "evac", "stored"))
        evac_a = st.sem("evac_a")
        with nc.Fori(0, LT // 2) as i:
            with nc.Block() as block:
                @block.sync
                def _(sp):
                    for p in range(2):
                        sp.dma_start(u[p][:, :], rows(U3, True)[i, p][:, 1024:2048]).then_inc(loaded[p], 16)
                    sp.wait_ge(evac, 4)
                    sp.wait_ge(evac_a, 4)
                    sp.dma_start(QF.rearrange("n c (m t) -> m c n t", t=2 * P)[i], tb[:, :, :]).then_inc(stored, 16)
                    sp.wait_ge(stored, 16)

                @block.vector
                def _(dve):
                    for p in range(2):
                        dve.wait_ge(loaded[p], 16)
                        qk = u[p][:, :].rearrange("p (h d) -> p h d", d=HD)
                        c = csum[:, bass.ds(i * 2 + p, 1), :].rearrange("p o h -> p h o")
                        dve.tensor_scalar(aug[p][:, 0:8, 0:HD], qk[:, 0:8, :], HD ** -0.5, None, ALU.mult).then_inc(filled[p], 1)
                        dve.tensor_copy(aug[p][:, 8:16, 0:HD], qk[:, 8:16, :]).then_inc(filled[p], 1)
                        dve.tensor_copy(aug[p][:, 0:8, HD + 1:HD + 2], c).then_inc(filled[p], 1)
                        dve.tensor_scalar(aug[p][:, 8:16, HD:HD + 1], c, -1.0, None, ALU.mult).then_inc(filled[p], 1)
                        dve.memset(aug[p][:, 0:8, HD:HD + 1], 1.0).then_inc(filled[p], 1)
                        dve.memset(aug[p][:, 8:16, HD + 1:HD + 2], 1.0).then_inc(filled[p], 1)
                    for p in range(2):
                        for g in (1, 3):
                            dve.wait_ge(trans, 4 * p + g + 1)
                            dve.tensor_copy(tb[:, 4 * g:4 * g + 4, p * P:(p + 1) * P], pt[4 * p + g][0:KF, :].rearrange("p (b t) -> p b t", t=P)).then_inc(evac, 1)

                @block.scalar
                def _(act):
                    for p in range(2):
                        for g in (0, 2):
                            act.wait_ge(trans, 4 * p + g + 1)
                            nc.scalar.copy(tb[:, 4 * g:4 * g + 4, p * P:(p + 1) * P], pt[4 * p + g][0:KF, :].rearrange("p (b t) -> p b t", t=P)).then_inc(evac_a, 1)

                @block.tensor
                def _(pe):
                    for p in range(2):
                        pe.wait_ge(filled[p], 6)
                        for g in range(4):
                            for n in range(4):
                                mm = pe.transpose(pt[4 * p + g][0:KF, n * P:(n + 1) * P], aug[p][:, 4 * g + n, :], ident[:, :])
                            mm.then_inc(trans, 1)
            st.clear()


def fox_stage(nc, ap, ident, U3, QF, O):
    units = [dict(q=i * P, keys=[(0, P * (i + 1))], tiles=list(range(i + 1)), bias=None) for i in range(LT)]
    qv = QF[0:8].rearrange("(j s) c t -> j s c t", s=2)
    kv = QF[8:16].rearrange("(j s) c t -> j s c t", s=2)
    vv = U3[:, 2048:2560].rearrange("(m p) (j s d) -> j s p m d", p=P, s=2, d=HD)

    def loads(sp, idx, b, loaded):
        (j,) = idx
        for s in range(2):
            sp.dma_start(b["qT"][s][:, :], qv[j, s]).then_inc(loaded[s], 16)
            sp.dma_start(b["kT"][s][:, :], kv[j, s]).then_inc(loaded[s], 16)
            sp.dma_start(b["v"][s][:, :, :], vv[j, s]).then_inc(loaded[s], 16)

    ov = O[:, HW:D].rearrange("(x p) (j s d) -> j p x s d", p=P, s=2, d=HD)

    def out(sp, idx, o, stored):
        (j,) = idx
        sp.dma_start(ov[j], o[:, :, :, :]).then_inc(stored, 16)
        sp.wait_ge(stored, 16)

    attention_stage(nc, "fox", ident, [4], KF, LAT, units, loads, [48, 48], False, out, causal=ap["causal_mask"])


def spatial_stage(nc, ap, ident, U3, O):
    LN_EPS = 1e-5
    with Stage(nc, "sgu") as st:
        u = [st.sb(f"u{p}", [P, D]) for p in range(2)]
        t = [st.sb(f"t{p}", [P, HW]) for p in range(2)]
        sq = [st.sb(f"sq{p}", [P, HW]) for p in range(2)]
        m = [st.sb(f"m{p}", [P, 2]) for p in range(2)]
        gb = st.sb("gb", [P, 2, HW])
        ws = st.sb("ws", [P, HEADS, P])
        wsT = st.sb("wsT", [P, HEADS, P])
        tri = st.sb("tri", [P, P])
        bs = st.sb("bs", [HEADS, P])
        bsT = st.sb("bsT", [P, HEADS])
        pt = [st.ps(f"pt{i}") for i in range(3)]
        pm = [st.ps(f"pm{i}") for i in range(2)]
        const_in, trans, gelu, centred, squared, ms_ready, rt_ready, v_ready, mixed, done, stored, seq = (st.sem(n) for n in (
            "const_in", "trans", "gelu", "centred", "squared", "ms_ready", "rt_ready", "v_ready", "mixed", "done", "stored", "seq"))
        loaded = [st.sem(f"loaded{p}") for p in range(2)]
        with nc.Block() as block:
            @block.sync
            def _(sp):
                sp.dma_start(gb[:, 0, :], ap["ln_v_gain_2"][0].partition_broadcast(P)).then_inc(const_in, 16)
                sp.dma_start(gb[:, 1, :], ap["ln_v_bias_2"][0].partition_broadcast(P)).then_inc(const_in, 16)
                sp.dma_start(ws[:, :, :], ap["w_spatial_2"][0].rearrange("g t s -> t g s")).then_inc(const_in, 16)
                sp.dma_start(bs[:, :], ap["b_spatial_2"][0]).then_inc(const_in, 16)
                sp.dma_start(tri[:, :], ap["tri128"]).then_inc(const_in, 16)

            @block.tensor
            def _(pe):
                pe.wait_ge(const_in, 80)
                for g in range(HEADS):
                    pe.transpose(pt[g // 4][:, (g % 4) * P:(g % 4 + 1) * P], ws[:, g, :], ident[:, :])
                pe.transpose(pt[2][:, 0:HEADS], bs[:, :], ident[0:HEADS, 0:HEADS]).then_inc(trans, 1)

            @block.vector
            def _(dve):
                link = Linked(dve, seq)
                dve.wait_ge(trans, 1)
                for g in range(HEADS):
                    link(dve.tensor_tensor(wsT[:, g, :], pt[g // 4][:, (g % 4) * P:(g % 4 + 1) * P], tri[:, :], ALU.mult))
                link(dve.tensor_copy(bsT[:, :], pt[2][:, 0:HEADS]))
        st.clear()
        with nc.Fori(0, LT // 2) as i:
            with nc.Block() as block:
                @block.sync
                def _(sp):
                    for p in range(2):
                        sp.dma_start(u[p][:, :], rows(U3, True)[i, p][:, 0:1024]).then_inc(loaded[p], 16)
                    for p in range(2):
                        sp.wait_ge(done, p + 1)
                        sp.dma_start(rows(O[:, 0:HW], True)[i, p], t[p][:, :]).then_inc(stored, 16)
                    sp.wait_ge(stored, 32)

                @block.scalar
                def _(act):
                    for p in range(2):
                        act.wait_ge(loaded[p], 16)
                        nc.scalar.activation(u[p][:, :], u[p][:, :], ACT.Gelu).then_inc(gelu, 1)
                    for p in range(2):
                        act.wait_ge(centred, p + 1)
                        nc.scalar.activation(sq[p][:, :], u[p][:, HW:D], ACT.Square, accum_out=m[p][:, 1:2]).then_inc(squared, 1)
                    for p in range(2):
                        act.wait_ge(ms_ready, p + 1)
                        nc.scalar.activation(m[p][:, 1:2], m[p][:, 1:2], ACT.Sqrt).then_inc(rt_ready, 1)

                @block.tensor
                def _(pe):
                    for p in range(2):
                        pe.wait_ge(v_ready, p + 1)
                        for g in range(HEADS):
                            mm = pe.matmul(pm[p][:, g * HD:(g + 1) * HD], wsT[:, g, :], u[p][:, HW + g * HD:HW + (g + 1) * HD], start=True, stop=True)
                        mm.then_inc(mixed, 1)

                @block.vector
                def _(dve):
                    link = Linked(dve, seq)
                    for p in range(2):
                        v = u[p][:, HW:D]
                        dve.wait_ge(gelu, p + 1)
                        link(dve.tensor_reduce(m[p][:, 0:1], v, AX.X, ALU.add))
                        link(dve.tensor_scalar(m[p][:, 0:1], m[p][:, 0:1], 1.0 / HW, None, ALU.mult))
                        dve.tensor_scalar(v, v, m[p][:, 0:1], None, ALU.subtract).then_inc(centred, 1)
                    for p in range(2):
                        dve.wait_ge(squared, p + 1)
                        dve.tensor_scalar(m[p][:, 1:2], m[p][:, 1:2], 1.0 / HW, LN_EPS, ALU.mult, ALU.add).then_inc(ms_ready, 1)
                    for p in range(2):
                        v = u[p][:, HW:D]
                        dve.wait_ge(rt_ready, p + 1)
                        link(dve.reciprocal(m[p][:, 1:2], m[p][:, 1:2]))
                        link(dve.scalar_tensor_tensor(out=v, in0=v, scalar=m[p][:, 1:2], in1=gb[:, 0, :], op0=ALU.mult, op1=ALU.mult))
                        dve.tensor_tensor(v, v, gb[:, 1, :], ALU.add).then_inc(v_ready, 1)
                    for p in range(2):
                        dve.wait_ge(mixed, p + 1)
                        th = t[p][:, :].rearrange("p (g d) -> p g d", d=HD)
                        link(dve.tensor_tensor(th, pm[p][:, :].rearrange("p (g d) -> p g d", d=HD), bsT[:, :].unsqueeze(2).to_broadcast([P, HEADS, HD]), ALU.add))
                        dve.tensor_tensor(t[p][:, :], t[p][:, :], u[p][:, 0:HW], ALU.mult).then_inc(done, 1)
            st.clear()


def merge_stage(nc, ident, O, xT, gain):
    with Stage(nc, "merge") as st:
        x = [st.sb(f"x{p}", [P, D]) for p in range(2)]
        sq = st.sb("sq", [P, D])
        ss = st.sb("ss", [P, 4])
        rs = st.sb("rs", [P, 4])
        pt = [st.ps(f"pt{i}") for i in range(4)]
        loaded = [st.sem(f"loaded{p}") for p in range(2)]
        ss_ready, ms_ready, rt_ready, scaled, trans, evac, split, seq = (st.sem(n) for n in ("ss_ready", "ms_ready", "rt_ready", "scaled", "trans", "evac", "split", "seq"))
        xf = st.sb("xf", [P, 2, KT, P])
        with nc.Fori(0, LT // 2) as i:
            with nc.Block() as block:
                @block.sync
                def _(sp):
                    for p in range(2):
                        sp.dma_start(x[p][:, :], rows(O[0:LAT], True)[i, p]).then_inc(loaded[p], 16)

                @block.scalar
                def _(act):
                    for p in range(2):
                        act.wait_ge(loaded[p], 16)
                        for h in range(2):
                            nc.scalar.activation(sq[:, h * HW:(h + 1) * HW], x[p][:, h * HW:(h + 1) * HW], ACT.Square,
                                                 accum_out=ss[:, 2 * p + h:2 * p + h + 1]).then_inc(ss_ready, 1)
                        if p == 0:
                            act.wait_ge(ss_ready, 2)
                    act.wait_ge(ms_ready, 1)
                    nc.scalar.activation(rs[:, :], ss[:, :], ACT.Sqrt).then_inc(rt_ready, 1)
                    for n in range(4):
                        act.wait_ge(trans, n + 1)
                        for k in range(4 * (n % 2), 4 * (n % 2) + 4):
                            nc.scalar.activation(xf[:, n // 2, k, :], pt[n][:, (k % 4) * P:(k % 4 + 1) * P],
                                                 ACT.Identity, scale=gain[:, k:k + 1]).then_inc(evac, 1)

                @block.vector
                def _(dve):
                    link = Linked(dve, seq)
                    dve.wait_ge(ss_ready, 4)
                    dve.tensor_scalar(ss[:, :], ss[:, :], 1.0 / HW, NORM_EPS, ALU.mult, ALU.add).then_inc(ms_ready, 1)
                    dve.wait_ge(rt_ready, 1)
                    link(dve.reciprocal(rs[:, :], rs[:, :]))
                    for n in range(4):
                        xh = x[n // 2][:, (n % 2) * HW:(n % 2 + 1) * HW]
                        dve.tensor_scalar(xh, xh, rs[:, n:n + 1], None, ALU.mult).then_inc(scaled, 1)
                    split_blocks(nc, dve, xT, xf, i, evac, split)

                @block.tensor
                def _(pe):
                    for n in range(4):
                        pe.wait_ge(scaled, n + 1)
                        for k in range(4):
                            mm = pe.transpose(pt[n][:, k * P:(k + 1) * P], x[n // 2][:, (4 * (n % 2) + k) * P:(4 * (n % 2) + k + 1) * P], ident[:, :])
                        mm.then_inc(trans, 1)
            st.clear()


def ffn_in_stage(nc, ap, xT, hT):
    turns = FF // P // 2
    wv = ap["w_ffn_in_2"][0].rearrange("(k p) (u j b n) -> j b u p k n", p=P, u=2, b=2, n=P)
    with Stage(nc, "ffi") as st:
        w = [st.sb(f"w{u}", [P, KT, P]) for u in range(2)]
        wh = [st.sb(f"wh{u}", [P, KT, P], F32R) for u in range(2)]
        wl = [st.sb(f"wl{u}", [P, KT, P], F32R) for u in range(2)]
        g = st.sb("g", [P, LAT])
        acc = [[st.ps(f"acc{b}{i}") for i in range(4)] for b in range(2)]
        w_in, high_out, low_out, summed = ([st.sem(f"{n}{u}") for u in range(2)] for n in ("w_in", "high_out", "low_out", "summed"))
        silu, done = st.sem("silu"), st.sem("done")

        def tiles(eng, tile):
            with eng.Fori(0, turns - 1) as j:
                tile(j * 2, 0, (j, 1))
                tile(j * 2 + 1, 1, (j + 1, 0))
            tile(2 * turns - 2, 0, (turns - 1, 1))
            tile(2 * turns - 1, 1, None)

        with nc.Block() as block:
            @block.sync
            def _(sp):
                for u in range(2):
                    sp.dma_start(w[u][:, :, :], wv[0, 0, u]).then_inc(w_in[u], 16)

                def tile(t, b, following):
                    if following is not None:
                        for u in range(2):
                            sp.wait_ge(low_out[u], t + 1)
                            sp.dma_start(w[u][:, :, :], wv[following[0], following[1], u]).then_inc(w_in[u], 16)

                tiles(sp, tile)

            @block.tensor
            def _(pe):
                pe.sem_inc(done, 2)

                def tile(t, b, following):
                    pe.wait_ge(done, t + 1)
                    for u in range(2):
                        pe.wait_ge(low_out[u], t + 1)
                        for h in range(2):
                            for k in range(KT):
                                for n, (v, x) in enumerate(((wh, 0), (wh, 1), (wl, 0))):
                                    mm = pe.matmul(acc[b][2 * u + h][:, :], v[u][:, k, :], xT[x][:, k, h * 512:(h + 1) * 512],
                                                   start=(k == 0 and n == 0), stop=(k == KT - 1 and n == 2))
                        mm.then_inc(summed[u], 1)

                tiles(pe, tile)

            @block.scalar
            def _(act):
                def split(t, u):
                    act.wait_ge(w_in[u], t * 16 + 16)
                    nc.scalar.copy(wh[u][:, :, :], w[u][:, :, :]).then_inc(high_out[u], 1)

                for u in range(2):
                    split(0, u)

                def tile(t, b, following):
                    act.wait_ge(summed[0], t + 1)
                    if following is not None:
                        split(t + 1, 0)
                    act.wait_ge(done, t + 2)
                    for h in range(2):
                        nc.scalar.activation(g[:, h * 512:(h + 1) * 512], acc[b][h][:, :], ACT.Silu).then_inc(silu, 1)
                    if following is not None:
                        act.wait_ge(summed[1], t + 1)
                        split(t + 1, 1)

                tiles(act, tile)

            @block.vector
            def _(dve):
                def split(t, u):
                    dve.wait_ge(high_out[u], t + 1)
                    low(dve, wl[u][:, :, :], w[u][:, :, :], wh[u][:, :, :]).then_inc(low_out[u], 1)

                for u in range(2):
                    split(0, u)

                def tile(t, b, following):
                    if following is not None:
                        split(t + 1, 0)
                    dve.wait_ge(summed[1], t + 1)
                    if following is not None:
                        split(t + 1, 1)
                    dve.wait_ge(silu, t * 2 + 2)
                    for h in range(2):
                        ins = dve.tensor_tensor(hT[:, bass.ds(t, 1), h * 512:(h + 1) * 512], g[:, h * 512:(h + 1) * 512].unsqueeze(1),
                                                acc[b][2 + h][:, :].unsqueeze(1), ALU.mult)
                    ins.then_inc(done, 1)

                tiles(dve, tile)


def ffn_out_stage(nc, w, hT, out):
    kt = FF // P
    wv = w.rearrange("(k p) (h n) -> h k p n", p=P, n=512)
    ov = out.rearrange("(m p) (h n) -> h m p n", p=P, n=512)
    with Stage(nc, "g8") as st:
        wr = [st.sb(f"wr{s}", [P, 512]) for s in range(2)]
        wh = [st.sb(f"wh{s}", [P, 512], F32R) for s in range(2)]
        wl = [st.sb(f"wl{s}", [P, 512], F32R) for s in range(2)]
        hh = [st.sb(f"hh{s}", [P, LAT], F32R) for s in range(2)]
        hl = [st.sb(f"hl{s}", [P, LAT], F32R) for s in range(2)]
        o = [st.sb(f"o{r}", [P, 512]) for r in range(LT)]
        acc = [st.ps(f"acc{r}") for r in range(LT)]
        w_in = [st.sem(f"w_in{s}") for s in range(2)]
        h_high, h_low, w_high, w_low, step_done, summed, emptied_a, emptied_v, stored = (st.sem(n) for n in (
            "h_high", "h_low", "w_high", "w_low", "step_done", "summed", "emptied_a", "emptied_v", "stored"))

        def steps(eng, half, step):
            step(half * kt, 0, 0, "first")
            step(half * kt + 1, 1, 1, "")
            with eng.Fori(1, kt // 2 - 1) as j:
                for s in range(2):
                    step(j * 2 + (half * kt + s), j * 2 + s, s, "")
            step(half * kt + kt - 2, kt - 2, 0, "")
            step(half * kt + kt - 1, kt - 1, 1, "last")

        with nc.Block() as block:
            @block.sync
            def _(sp):
                for s in range(2):
                    sp.dma_start(wr[s][:, :], wv[0, s]).then_inc(w_in[s], 16)
                for half in range(2):
                    with sp.Fori(0, kt // 2 - 1) as j:
                        for s in range(2):
                            sp.wait_ge(w_low, j * 2 + (half * kt + s + 1))
                            sp.dma_start(wr[s][:, :], wv[half, 2:].rearrange("(j s) p n -> s j p n", s=2)[s, j]).then_inc(w_in[s], 16)
                    if half == 0:
                        for s in range(2):
                            sp.wait_ge(w_low, kt - 2 + s + 1)
                            sp.dma_start(wr[s][:, :], wv[1, s]).then_inc(w_in[s], 16)
                    for m in range(LT):
                        sp.wait_ge(emptied_a if m % 2 else emptied_v, half * LT // 2 + m // 2 + 1)
                        sp.dma_start(ov[half, m], o[m][:, :]).then_inc(stored, 16)
                sp.wait_ge(stored, 16 * 2 * LT)

            @block.tensor
            def _(pe):
                for half in range(2):
                    def step(n, k, s, place):
                        pe.wait_ge(h_low, n + 1)
                        pe.wait_ge(w_low, n + 1)
                        for m in range(LT):
                            if place == "first" and half:
                                pe.wait_ge(emptied_a if m % 2 else emptied_v, m // 2 + 1)
                            for i, (x, v) in enumerate(((hh, wh), (hh, wl), (hl, wh))):
                                mm = pe.matmul(acc[m][:, :], x[s][:, m * P:(m + 1) * P], v[s][:, :],
                                               start=(place == "first" and i == 0), stop=(place == "last" and i == 2))
                            if place == "last" and m < LT - 1:
                                mm.then_inc(summed, 1)
                        mm.then_inc(step_done, 1)
                    steps(pe, half, step)

            @block.scalar
            def _(act):
                for half in range(2):
                    def step(n, k, s, place):
                        if type(n) is not int or n >= 2:
                            act.wait_ge(step_done, n + (-1))
                        nc.scalar.copy(hh[s][:, :].unsqueeze(1), hT[:, bass.ds(k, 1), :]).then_inc(h_high, 1)
                        act.wait_ge(w_in[s], (n + (2 - s)) * 8)
                        nc.scalar.copy(wh[s][:, :], wr[s][:, :]).then_inc(w_high, 1)
                    steps(act, half, step)
                    for m in range(1, LT, 2):
                        if m < LT - 1:
                            act.wait_ge(summed, half * (LT - 1) + m + 1)
                        else:
                            act.wait_ge(step_done, (half + 1) * kt)
                        if half:
                            act.wait_ge(stored, 16 * LT)
                        nc.scalar.copy(o[m][:, :], acc[m][:, :]).then_inc(emptied_a, 1)

            @block.vector
            def _(dve):
                for half in range(2):
                    def step(n, k, s, place):
                        if type(n) is not int or n >= 2:
                            dve.wait_ge(step_done, n + (-1))
                        dve.wait_ge(h_high, n + 1)
                        low(dve, hl[s][:, :].unsqueeze(1), hT[:, bass.ds(k, 1), :], hh[s][:, :].unsqueeze(1)).then_inc(h_low, 1)
                        dve.wait_ge(w_high, n + 1)
                        low(dve, wl[s][:, :], wr[s][:, :], wh[s][:, :]).then_inc(w_low, 1)
                    steps(dve, half, step)
                    for m in range(0, LT, 2):
                        dve.wait_ge(summed, half * (LT - 1) + m + 1)
                        if half:
                            dve.wait_ge(stored, 16 * LT)
                        dve.tensor_copy(o[m][:, :], acc[m][:, :]).then_inc(emptied_v, 1)


def gemm(nc, name, xT, kt, mt, w, out, n0, n, wn, row_of=lambda m: m * P):
    assert n % (2 * wn) == 0
    wv = w[:, n0:n0 + n].rearrange("(k p) (j b n) -> j b p k n", p=P, b=2, n=wn)
    ov = out[:, n0:n0 + n].rearrange("r (j b n) -> j b r n", b=2, n=wn)
    gemm_stage(nc, name, xT, kt, mt, lambda j, b: wv[j, b], n // (2 * wn), wn,
               lambda j, b, m: ov[j, b][row_of(m):row_of(m) + P, :])


def build(nc, ap, out, scratch, part="ab"):
    U1 = scratch("U1", (TOK, ATTN_IN))
    QT = scratch("QT", (13 * P, TOK))
    REP = scratch("REP", (HEADS, PADR, HD, P))
    O1 = scratch("O1", (TOK, D))
    Y1 = scratch("Y1", (TOK, D))
    X1 = scratch("X1", (LAT, D))
    U2 = scratch("U2", (U2_ROWS, REC_IN))
    FE = scratch("FE", (TOK, 2, NF * HW // 2))
    YS = [scratch(f"YS{d}", (LAT, HW)) for d in range(2)]
    HX = scratch("HX", (3, LAT, HW))
    O2 = scratch("O2", (LAT, D))
    Y2 = scratch("Y2", (LAT, D))
    H0 = scratch("H0", (LAT, D))
    U3 = scratch("U3", (LAT, BLK_IN))
    QF = scratch("QF", (2 * HEADS, KF, LAT))
    O3 = scratch("O3", (LAT, D))
    Y3 = scratch("Y3", (LAT, D))
    H2 = scratch("H2", (LAT, D))
    Y4 = scratch("Y4", (LAT, D))
    x, ctx = ap["x"][0], ap["ctx"][0]

    def pair(dram, first=0):
        v = rows(dram, True)
        return lambda i, p: v[i + (-first), p] if first else v[i, p]

    with Stage(nc, "main") as st:
        ident = st.sb("ident", [P, P])
        gains = st.sb("gains", [P, 3, KT])
        const_in = st.sem("const_in")
        mods = {}
        with nc.Block() as block:
            @block.sync
            def _(sp):
                sp.dma_start(ident[:, :], ap["ident"]).then_inc(const_in, 16)
                for g, (src, lo, hi) in enumerate((("pre_mix_gain_2", 0, 8), ("pre_ffn_gain_2", 0, 8), ("out_norm_a_gain_2", 0, 4), ("out_norm_b_gain_2", 4, 8))):
                    to = {0: 0, 1: 2, 2: 1, 3: 1}[g]
                    sp.dma_start(gains[:, to, lo:hi], cols(ap[src][0]), allow_slow_non_contiguous=True).then_inc(const_in, 16)
                sp.wait_ge(const_in, 80)
        for pre in ("attn", "rec"):
            mods[pre] = (st.sb(f"modA_{pre}", [P, 2, KT]), st.sb(f"modB_{pre}", [P, 2, KT]), st.sb(f"gate_{pre}", [P, 2, D]))
            adaln_stage(nc, ap, pre, mods[pre])
        A, B, G = mods["attn"]
        with Stage(nc, "l1") as s1:
            xT = [s1.sb(n, [P, KT, TOK], F32R) for n in ("x_high", "x_low")]
            norm_stage(nc, "n1", ident, (0, LT // 2), xT, pair(x), modA=A[:, 0, :], modB=B[:, 0, :])
            norm_stage(nc, "n1c", ident, (LT // 2, 5), xT, pair(ctx, LT // 2), modA=A[:, 1, :], modB=B[:, 1, :])
            gemm(nc, "g1", xT, KT, LT + CT, ap["attn_w_in"][0], U1, 0, ATTN_IN, 416)
        window_table_stage(nc, ap, REP)
        attn_prep_stage(nc, ap, ident, U1, QT, (0, 5), 0, 0)
        na_stage(nc, ap, ident, U1, QT, REP, O1)
        gqa_stage(nc, ap, ident, U1, QT, O1)
        with Stage(nc, "l1b") as s1:
            xT = [s1.sb(n, [P, KT, TOK], F32R) for n in ("x_high", "x_low")]
            gated_stage(nc, "gt1", ident, (0, 5), xT, pair(O1), lambda h: pair(U1[:, 1536:2048] if h == 0 else U1[:, 2816:3328]))
            gemm(nc, "g2", xT, KT, LT + CT, ap["attn_w_out"][0], Y1, 0, D, 512)
        A2, B2, G2 = mods["rec"]
        with Stage(nc, "l2") as s2:
            xT = [s2.sb(n, [P, KT, TOK], F32R) for n in ("x_high", "x_low")]
            norm_stage(nc, "n2", ident, (0, LT // 2), xT, pair(x), y_of=pair(Y1[0:LAT]), gate=G[:, 0, :], z_out=pair(X1), modA=A2[:, 0, :], modB=B2[:, 0, :])
            norm_stage(nc, "n2c", ident, (LT // 2, 5), xT, pair(ctx, LT // 2), y_of=pair(Y1), gate=G[:, 1, :], modA=A2[:, 1, :], modB=B2[:, 1, :])
            place = lambda m: LAT0 + m * P if m < LT else CTX0 + (m - LT) * P
            gemm(nc, "g3", xT, KT, LT + CT, ap["rec_w_in"][0], U2, 0, RW, 416, place)
            gemm(nc, "g4", xT, KT, LT, ap["rec_w_in"][0], U2, RW, REC_IN - RW, 320, place)
        zero_rows_stage(nc, U2)
        rwkv_feature_stage(nc, ap, ident, U2, FE, [(CT, CTX0, 0), (LT, LAT0, CTX)])
        rwkv_scan_stage(nc, ap, ident, FE, YS)
        rwkv_readout_stage(nc, ap, FE, YS, O2)
        hyena_conv3_stage(nc, ap, U2, HX)
        hyena_stage(nc, ap, HX, O2)
        lat2 = U2[LAT0:LAT0 + LAT]
        with Stage(nc, "l2b") as s2:
            xT = [s2.sb(n, [P, KT, LAT], F32R) for n in ("x_high", "x_low")]
            gated_stage(nc, "gt2", ident, (0, 4), xT, pair(O2), lambda h: pair(lat2[:, RW:RW + HW] if h == 0 else lat2[:, REC_IN - HW:REC_IN]))
            gemm(nc, "g5", xT, KT, LT, ap["rec_w_out"][0], Y2, 0, D, 512)
        with Stage(nc, "l3") as s3:
            xT = [s3.sb(n, [P, KT, LAT], F32R) for n in ("x_high", "x_low")]
            norm_stage(nc, "n3", ident, (0, 4), xT, pair(X1), y_of=pair(Y2), gate=G2[:, 0, :], z_row=ap["final_norm"], z_out=pair(H0), modA=gains[:, 0, :])
            gemm(nc, "g6", xT, KT, LT, ap["w_in_2"][0], U3, 0, BLK_IN, 428)
        with Stage(nc, "l3a") as s3:
            csum = s3.sb("csum", [P, LT, HEADS])
            forget_stage(nc, ap, U3, csum)
            fox_prep_stage(nc, ident, U3, csum, QF)
        fox_stage(nc, ap, ident, U3, QF, O3)
        spatial_stage(nc, ap, ident, U3, O3)
        with Stage(nc, "l3b") as s3:
            xT = [s3.sb(n, [P, KT, LAT], F32R) for n in ("x_high", "x_low")]
            merge_stage(nc, ident, O3, xT, gains[:, 1, :])
            gemm(nc, "g7", xT, KT, LT, ap["w_out_2"][0], Y3, 0, D, 512)
        with Stage(nc, "l4") as s4:
            with Stage(nc, "l4a") as s5:
                xT = [s5.sb(n, [P, KT, LAT], F32R) for n in ("x_high", "x_low")]
                norm_stage(nc, "n4", ident, (0, 4), xT, pair(H0), y_of=pair(Y3), y_row=ap["post_mix_gain_2"][0], z_out=pair(H2), modA=gains[:, 2, :])
                hT = s4.sb("hT", [P, FF // P, LAT], side="right")
                ffn_in_stage(nc, ap, xT, hT)
            ffn_out_stage(nc, ap["w_ffn_out_2"][0], hT, Y4)
        norm_stage(nc, "n5", ident, (0, 4), None, pair(H2), y_of=pair(Y4), y_row=ap["post_ffn_gain_2"][0], z_out=pair(out[0]))


def constants():
    tri, keep, lev, lev0 = scan_constants()
    feats, window, dft, idft, alt = hyena_constants()
    s, t = np.meshgrid(np.arange(P), np.arange(P), indexing="ij")
    return dict(ident=np.eye(P, dtype=np.float32), rope=rope_table(), window_mask=window_mask(), tri=tri, keep=keep, lev=lev, lev0=lev0,
                hy_feats=feats, hy_window=window, dft=dft, idft=idft, alternate=alt,
                tri128=(s <= t).astype(np.float32),
                causal_mask=np.where(s >= t, 0.0, -1e30).astype(np.float32))


_INS = ["x", "c", "ctx", "c_ctx", "attn_norm", "attn_ada_w", "attn_ada_b", "attn_w_in", "na_rpb", "gqa_q_gain",
        "gqa_k_gain", "attn_w_out", "rec_norm", "rec_ada_w", "rec_ada_b", "rec_w_in", "rwkv_mu", "rwkv_w0",
        "rwkv_w_up", "rwkv_a0", "rwkv_a_up", "rwkv_k_k", "rwkv_k_a", "rwkv_r_k", "rwkv_gn_w", "rwkv_gn_b", "hy_short",
        "hy_w1", "hy_b1", "hy_w2", "hy_b2", "hy_w3", "hy_b3", "hy_skip", "rec_w_out", "final_norm", "pre_mix_gain_2",
        "w_in_2", "ln_v_gain_2", "ln_v_bias_2", "w_spatial_2", "b_spatial_2", "b_forget_2", "out_norm_a_gain_2",
        "out_norm_b_gain_2", "w_out_2", "post_mix_gain_2", "pre_ffn_gain_2", "w_ffn_in_2", "w_ffn_out_2",
        "post_ffn_gain_2"]


def kernel(**inputs):
    import concourse.bacc as _bacc
    from concourse.bass_utils import run_bass_kernel_spmd as _run

    nc = _bacc.Bacc("TRN2", target_bir_lowering=False, num_devices=1)
    arrays, ap = {}, {}
    data = {name: np.ascontiguousarray(inputs[name]) for name in _INS}
    data.update(constants())
    for name, a in data.items():
        arrays[f"in_{name}"] = a
        ap[name] = nc.dram_tensor(f"in_{name}", a.shape, mybir.dt.from_np(a.dtype), kind="ExternalInput").ap()
    out = nc.dram_tensor("out_0", (1, LAT, D), F32, kind="ExternalOutput").ap()
    build(nc, ap, out, lambda name, shape: nc.dram_tensor(f"s_{name}", shape, F32, kind="Internal").ap())
    r = _run(nc, [arrays], core_ids=[0])
    return r.results[0]["out_0"]
```
